# Optimizing a Trainium2 kernel written in Bass

```python
import math
import jax, jax.numpy as jnp
from jax import lax
import numpy as np

D_MODEL = 1024
BATCH = 1
SEQ = 512
DEPTH = 2

RMS_EPS = 1e-6
HEAD_DIM = 64
A_Q_HEADS = 8
A_KV_HEADS = 2
A_GROUP = A_Q_HEADS // A_KV_HEADS
A_WINDOW = 128
B_HEADS = 8
ATTN_BLOCK = 128
EVEN_IN = (A_Q_HEADS + 2 * A_KV_HEADS + 3 * B_HEADS) * HEAD_DIM + B_HEADS
EVEN_MIX = (A_Q_HEADS + B_HEADS) * HEAD_DIM
C_HEADS = 16
C_HEAD_DIM = 64
C_INNER = C_HEADS * C_HEAD_DIM
C_GROUPS = 2
C_HPG = C_HEADS // C_GROUPS
C_STATE = 128
C_CONV = 4
C_CHUNK = 128
C_CONV_DIM = C_INNER + 2 * C_GROUPS * C_STATE
D_HEADS = 4
D_KEY = D_MODEL // 2
D_VAL = D_MODEL
D_HK = D_KEY // D_HEADS
D_HV = D_VAL // D_HEADS
D_GATE_RANK = 16
D_GATE_NORM = 16.0
D_CHUNK = 64
ODD_IN = C_INNER + C_CONV_DIM + C_HEADS + 2 * D_KEY + D_VAL + D_GATE_RANK + D_VAL
ODD_MIX = C_INNER + D_VAL
MOE_GROUPS = 4
MOE_EPG = 8
MOE_EXPERTS = MOE_GROUPS * MOE_EPG
MOE_TOPK = 2
MOE_FF = 512
MOE_BLOCK = 128
N_EVEN = (DEPTH + 1) // 2
N_ODD = DEPTH // 2

kernel_name = 'hybrid_swa_fox_ssd_gla_hmoe'

def rmsnorm(x, g):
    xf = x.astype(jnp.float32)
    y = xf * lax.rsqrt(jnp.mean(xf * xf, axis=-1, keepdims=True) + RMS_EPS)
    return (y * g.astype(jnp.float32)).astype(x.dtype)

def split_cols(p, widths):
    offs = [int(o) for o in np.cumsum(widths)[:-1]]
    return jnp.split(p, offs, axis=-1)

def alibi_slopes(n_heads):
    return jnp.asarray(2.0 ** (-8.0 * np.arange(1, n_heads + 1) / n_heads), dtype=jnp.float32)

def sliding_window_sink_attention(q, k, v, sinks):
    b, s, kvh, g, hd = q.shape
    blk = A_WINDOW
    nb = s // blk

    def windows(t):
        tp = jnp.pad(t, ((0, 0), (blk, 0), (0, 0), (0, 0))).reshape(b, nb + 1, blk, kvh, hd)
        return jnp.concatenate([tp[:, :-1], tp[:, 1:]], axis=2)

    kw, vw = windows(k), windows(v)
    qb = q.reshape(b, nb, blk, kvh, g, hd)
    scores = jnp.einsum('bnqkgd,bnskd->bnkgqs', qb, kw).astype(jnp.float32) * (hd ** -0.5)
    dist = blk + jnp.arange(blk)[:, None] - jnp.arange(2 * blk)[None, :]
    key_pos = jnp.arange(nb)[:, None, None] * blk + jnp.arange(2 * blk)[None, None, :] - blk
    valid = (dist >= 0) & (dist < A_WINDOW) & (key_pos >= 0)
    slopes = alibi_slopes(kvh * g).reshape(kvh, g, 1, 1)
    scores = scores - slopes * dist.astype(jnp.float32)
    scores = jnp.where(valid[None, :, None, None], scores, -jnp.inf)
    sink = sinks.astype(jnp.float32).reshape(1, 1, kvh, g, 1, 1)
    m = jnp.maximum(jnp.max(scores, axis=-1, keepdims=True), sink)
    p = jnp.exp(scores - m)
    p = p / (jnp.sum(p, axis=-1, keepdims=True) + jnp.exp(sink - m))
    out = jnp.einsum('bnkgqs,bnskd->bnqkgd', p.astype(v.dtype), vw)
    return out.reshape(b, s, kvh * g, hd)

def forgetting_attention(q, k, v, log_f):
    b, s, h, hd = q.shape
    nb = s // ATTN_BLOCK
    c = jnp.transpose(jnp.cumsum(log_f, axis=1), (0, 2, 1))
    kpos = jnp.arange(s)

    def block(n):
        start = n * ATTN_BLOCK
        qb = lax.dynamic_slice_in_dim(q, start, ATTN_BLOCK, axis=1)
        cb = lax.dynamic_slice_in_dim(c, start, ATTN_BLOCK, axis=2)
        sc = jnp.einsum('bqhd,bshd->bhqs', qb, k).astype(jnp.float32) * (hd ** -0.5)
        sc = sc + cb[..., None] - c[:, :, None, :]
        qpos = start + jnp.arange(ATTN_BLOCK)
        sc = jnp.where(kpos[None, :] <= qpos[:, None], sc, -jnp.inf)
        p = jax.nn.softmax(sc, axis=-1).astype(v.dtype)
        return jnp.einsum('bhqs,bshd->bqhd', p, v)

    out = lax.map(block, jnp.arange(nb))
    return jnp.transpose(out, (1, 0, 2, 3, 4)).reshape(b, s, h, hd)

def causal_depthwise_conv(x, w, bias):
    kw, ch = w.shape
    y = lax.conv_general_dilated(x, w[:, None, :].astype(x.dtype), window_strides=(1,), padding=[(kw - 1, 0)],
                                 dimension_numbers=('NWC', 'WIO', 'NWC'), feature_group_count=ch)
    return y + bias.astype(y.dtype)

def ssd_chunked(x, dt, a, bm, cm):
    b, s, g, hg, p = x.shape
    n = bm.shape[-1]
    q = C_CHUNK
    nc = s // q
    xd = (x.astype(jnp.float32) * dt[..., None]).reshape(b, nc, q, g, hg, p)
    acs = jnp.cumsum(jnp.transpose((dt * a).reshape(b, nc, q, g, hg), (0, 3, 4, 1, 2)), axis=-1)
    bc = bm.astype(jnp.float32).reshape(b, nc, q, g, n)
    cc = cm.astype(jnp.float32).reshape(b, nc, q, g, n)
    tri = jnp.tril(jnp.ones((q, q), dtype=bool))
    seg = jnp.exp(jnp.where(tri, acs[..., :, None] - acs[..., None, :], -jnp.inf))
    cb = jnp.einsum('bclgn,bcsgn->bgcls', cc, bc)
    y_diag = jnp.einsum('bgcls,bghcls,bcsghp->bclghp', cb, seg, xd)
    decay_to_end = jnp.exp(acs[..., -1:] - acs)
    states = jnp.einsum('bcsgn,bghcs,bcsghp->bcghpn', bc, decay_to_end, xd)
    chunk_decay = jnp.exp(acs[..., -1])

    def step(hstate, inp):
        st, dec = inp
        return hstate * dec[..., None, None] + st, hstate

    h0 = jnp.zeros((b, g, hg, p, n), jnp.float32)
    _, prev = lax.scan(step, h0, (jnp.moveaxis(states, 1, 0), jnp.moveaxis(chunk_decay, 3, 0)))
    y_off = jnp.einsum('bclgn,cbghpn,bghcl->bclghp', cc, prev, jnp.exp(acs))
    return (y_diag + y_off).reshape(b, s, g, hg, p)

def gla_chunked(q, k, v, log_alpha):
    b, s, h, dk = q.shape
    dv = v.shape[-1]
    cq = D_CHUNK
    nc = s // cq
    qc = (q.astype(jnp.float32) * (dk ** -0.5)).reshape(b, nc, cq, h, dk)
    kc = k.astype(jnp.float32).reshape(b, nc, cq, h, dk)
    vc = v.astype(jnp.float32).reshape(b, nc, cq, h, dv)
    gcs = jnp.cumsum(log_alpha.reshape(b, nc, cq, h, dk), axis=2)
    q_dec = qc * jnp.exp(gcs)
    k_inv = kc * jnp.exp(-gcs)
    k_end = kc * jnp.exp(gcs[:, :, -1:] - gcs)
    tri = jnp.tril(jnp.ones((cq, cq), dtype=bool))
    attn = jnp.where(tri, jnp.einsum('bclhd,bcshd->bchls', q_dec, k_inv), 0.0)
    o_intra = jnp.einsum('bchls,bcshv->bclhv', attn, vc)
    states = jnp.einsum('bcshd,bcshv->bchdv', k_end, vc)
    chunk_decay = jnp.exp(gcs[:, :, -1])

    def step(hstate, inp):
        st, dec = inp
        return hstate * dec[..., None] + st, hstate

    h0 = jnp.zeros((b, h, dk, dv), jnp.float32)
    _, prev = lax.scan(step, h0, (jnp.moveaxis(states, 1, 0), jnp.moveaxis(chunk_decay, 1, 0)))
    o_inter = jnp.einsum('bclhd,cbhdv->bclhv', q_dec, prev)
    return (o_intra + o_inter).reshape(b, s, h, dv)

def even_mixer(h, w_in, sinks, forget_bias, w_out):
    b, s, _ = h.shape
    proj = h @ w_in
    q_a, k_a, v_a, q_b, k_b, v_b, f_b = split_cols(
        proj, (A_Q_HEADS * HEAD_DIM, A_KV_HEADS * HEAD_DIM, A_KV_HEADS * HEAD_DIM,
               B_HEADS * HEAD_DIM, B_HEADS * HEAD_DIM, B_HEADS * HEAD_DIM, B_HEADS))
    out_a = sliding_window_sink_attention(q_a.reshape(b, s, A_KV_HEADS, A_GROUP, HEAD_DIM),
                                          k_a.reshape(b, s, A_KV_HEADS, HEAD_DIM),
                                          v_a.reshape(b, s, A_KV_HEADS, HEAD_DIM), sinks)
    log_f = jax.nn.log_sigmoid(f_b.astype(jnp.float32) + forget_bias.astype(jnp.float32))
    out_b = forgetting_attention(q_b.reshape(b, s, B_HEADS, HEAD_DIM), k_b.reshape(b, s, B_HEADS, HEAD_DIM),
                                 v_b.reshape(b, s, B_HEADS, HEAD_DIM), log_f)
    heads = jnp.concatenate([out_a.reshape(b, s, -1), out_b.reshape(b, s, -1)], axis=-1).astype(h.dtype)
    return heads @ w_out

def odd_mixer(h, w_in, conv_w, conv_b, dt_bias, a_log, d_skip, ssd_norm, gk_w, gk_b, gla_norm, w_out):
    b, s, _ = h.shape
    proj = h @ w_in
    z, xbc, dt, q, k, v, g_lr, r = split_cols(
        proj, (C_INNER, C_CONV_DIM, C_HEADS, D_KEY, D_KEY, D_VAL, D_GATE_RANK, D_VAL))
    xbc = jax.nn.silu(causal_depthwise_conv(xbc, conv_w, conv_b))
    xs, bm, cm = split_cols(xbc, (C_INNER, C_GROUPS * C_STATE, C_GROUPS * C_STATE))
    dt = jax.nn.softplus(dt.astype(jnp.float32) + dt_bias.astype(jnp.float32)).reshape(b, s, C_GROUPS, C_HPG)
    a = -jnp.exp(a_log.astype(jnp.float32)).reshape(C_GROUPS, C_HPG)
    xs = xs.reshape(b, s, C_GROUPS, C_HPG, C_HEAD_DIM)
    y = ssd_chunked(xs, dt, a, bm.reshape(b, s, C_GROUPS, C_STATE), cm.reshape(b, s, C_GROUPS, C_STATE))
    y = y + d_skip.astype(jnp.float32).reshape(C_GROUPS, C_HPG, 1) * xs.astype(jnp.float32)
    y = rmsnorm(y.reshape(b, s, C_INNER) * jax.nn.silu(z.astype(jnp.float32)), ssd_norm)
    log_alpha = jax.nn.log_sigmoid((g_lr @ gk_w + gk_b).astype(jnp.float32)) / D_GATE_NORM
    o = gla_chunked(q.reshape(b, s, D_HEADS, D_HK), k.reshape(b, s, D_HEADS, D_HK),
                    v.reshape(b, s, D_HEADS, D_HV), log_alpha.reshape(b, s, D_HEADS, D_HK))
    o = rmsnorm(o, gla_norm).reshape(b, s, D_VAL) * jax.nn.silu(r.astype(jnp.float32))
    mixed = jnp.concatenate([y, o], axis=-1).astype(h.dtype)
    return mixed @ w_out

def hierarchical_moe(h, w_group, b_group, w_router, b_router, w_gate, w_up, w_down):
    b, s, d = h.shape
    n_tok = b * s
    xt = h.reshape(n_tok, d)
    g_prob = jax.nn.softmax((xt @ w_group).astype(jnp.float32) + b_group.astype(jnp.float32), axis=-1)
    g_w, g_idx = lax.top_k(g_prob, 1)
    e_logits = ((xt @ w_router).astype(jnp.float32) + b_router.astype(jnp.float32)).reshape(n_tok, MOE_GROUPS, MOE_EPG)
    e_logits = jnp.take_along_axis(e_logits, g_idx[:, :, None], axis=1)[:, 0]
    e_w, e_idx = lax.top_k(jax.nn.softmax(e_logits, axis=-1), MOE_TOPK)
    e_w = e_w / jnp.sum(e_w, axis=-1, keepdims=True)
    gate = (g_w * e_w).reshape(-1)
    expert = (g_idx * MOE_EPG + e_idx).reshape(-1).astype(jnp.int32)
    token = jnp.repeat(jnp.arange(n_tok, dtype=jnp.int32), MOE_TOPK)
    n_assign = n_tok * MOE_TOPK
    order = jnp.argsort(expert)
    expert_s, token_s, gate_s = expert[order], token[order], gate[order]
    counts = jnp.zeros((MOE_EXPERTS,), jnp.int32).at[expert].add(1)
    starts = jnp.cumsum(counts) - counts
    padded = (counts + MOE_BLOCK - 1) // MOE_BLOCK * MOE_BLOCK
    pad_ends = jnp.cumsum(padded)
    pad_starts = pad_ends - padded
    row = pad_starts[expert_s] + (jnp.arange(n_assign, dtype=jnp.int32) - starts[expert_s])
    n_blocks = (n_assign + MOE_EXPERTS * (MOE_BLOCK - 1) + MOE_BLOCK - 1) // MOE_BLOCK
    n_rows = n_blocks * MOE_BLOCK
    row_token = jnp.full((n_rows,), n_tok, jnp.int32).at[row].set(token_s)
    row_gate = jnp.zeros((n_rows,), jnp.float32).at[row].set(gate_s)
    block_start = jnp.arange(n_blocks, dtype=jnp.int32) * MOE_BLOCK
    block_expert = jnp.minimum(jnp.sum(block_start[:, None] >= pad_ends[None, :], axis=1),
                               MOE_EXPERTS - 1).astype(jnp.int32)
    x_rows = jnp.concatenate([xt, jnp.zeros((1, d), xt.dtype)], axis=0)[row_token].reshape(n_blocks, MOE_BLOCK, d)

    def expert_block(args):
        xb, e = args
        return (jax.nn.silu(xb @ w_gate[e]) * (xb @ w_up[e])) @ w_down[e]

    y_rows = lax.map(expert_block, (x_rows, block_expert)).reshape(n_rows, d)
    y = jax.ops.segment_sum(y_rows.astype(jnp.float32) * row_gate[:, None], row_token, num_segments=n_tok + 1)[:n_tok]
    return y.reshape(b, s, d).astype(h.dtype)

def setup_inputs(seed: int = 0) -> dict:
    key = jax.random.key(seed)
    ks = jax.random.split(key, 26)
    f32 = jnp.float32

    def nrm(k, shape, scale):
        return jax.random.normal(k, shape, f32) * scale

    dt0 = jnp.exp(jax.random.uniform(ks[11], (N_ODD, C_HEADS), f32) * (math.log(0.1) - math.log(0.001)) + math.log(0.001))
    return {
        'x': nrm(ks[0], (BATCH, SEQ, D_MODEL), 1.0),
        'norm_mix': 1.0 + nrm(ks[1], (DEPTH, D_MODEL), 0.02),
        'norm_moe': 1.0 + nrm(ks[2], (DEPTH, D_MODEL), 0.02),
        'norm_final': 1.0 + nrm(ks[3], (D_MODEL,), 0.02),
        'even_w_in': nrm(ks[4], (N_EVEN, D_MODEL, EVEN_IN), D_MODEL ** -0.5),
        'even_sinks': nrm(ks[5], (N_EVEN, A_Q_HEADS), 0.5),
        'even_forget_bias': 4.0 + nrm(ks[6], (N_EVEN, B_HEADS), 0.5),
        'even_w_out': nrm(ks[7], (N_EVEN, EVEN_MIX, D_MODEL), EVEN_MIX ** -0.5),
        'odd_w_in': nrm(ks[8], (N_ODD, D_MODEL, ODD_IN), D_MODEL ** -0.5),
        'odd_conv_w': nrm(ks[9], (N_ODD, C_CONV, C_CONV_DIM), C_CONV ** -0.5),
        'odd_conv_b': nrm(ks[10], (N_ODD, C_CONV_DIM), 0.02),
        'odd_dt_bias': dt0 + jnp.log(-jnp.expm1(-dt0)),
        'odd_a_log': jnp.log(jax.random.uniform(ks[12], (N_ODD, C_HEADS), f32, 1.0, 16.0)),
        'odd_d_skip': 1.0 + nrm(ks[13], (N_ODD, C_HEADS), 0.1),
        'odd_ssd_norm': 1.0 + nrm(ks[14], (N_ODD, C_INNER), 0.02),
        'odd_gk_w': nrm(ks[15], (N_ODD, D_GATE_RANK, D_KEY), D_GATE_RANK ** -0.5),
        'odd_gk_b': nrm(ks[16], (N_ODD, D_KEY), 0.02),
        'odd_gla_norm': 1.0 + nrm(ks[17], (N_ODD, D_HV), 0.02),
        'odd_w_out': nrm(ks[18], (N_ODD, ODD_MIX, D_MODEL), ODD_MIX ** -0.5),
        'moe_w_group': nrm(ks[19], (DEPTH, D_MODEL, MOE_GROUPS), D_MODEL ** -0.5),
        'moe_b_group': nrm(ks[20], (DEPTH, MOE_GROUPS), 0.01),
        'moe_w_router': nrm(ks[21], (DEPTH, D_MODEL, MOE_EXPERTS), D_MODEL ** -0.5),
        'moe_b_router': nrm(ks[22], (DEPTH, MOE_EXPERTS), 0.01),
        'moe_w_gate': nrm(ks[23], (DEPTH, MOE_EXPERTS, D_MODEL, MOE_FF), D_MODEL ** -0.5),
        'moe_w_up': nrm(ks[24], (DEPTH, MOE_EXPERTS, D_MODEL, MOE_FF), D_MODEL ** -0.5),
        'moe_w_down': nrm(ks[25], (DEPTH, MOE_EXPERTS, MOE_FF, D_MODEL), MOE_FF ** -0.5),
    }

def reference(x, norm_mix, norm_moe, norm_final, even_w_in, even_sinks, even_forget_bias, even_w_out,
              odd_w_in, odd_conv_w, odd_conv_b, odd_dt_bias, odd_a_log, odd_d_skip, odd_ssd_norm,
              odd_gk_w, odd_gk_b, odd_gla_norm, odd_w_out, moe_w_group, moe_b_group, moe_w_router,
              moe_b_router, moe_w_gate, moe_w_up, moe_w_down):
    h = x
    for layer in range(DEPTH):
        i = layer // 2
        hn = rmsnorm(h, norm_mix[layer])
        if layer % 2 == 0:
            mix = even_mixer(hn, even_w_in[i], even_sinks[i], even_forget_bias[i], even_w_out[i])
        else:
            mix = odd_mixer(hn, odd_w_in[i], odd_conv_w[i], odd_conv_b[i], odd_dt_bias[i], odd_a_log[i],
                            odd_d_skip[i], odd_ssd_norm[i], odd_gk_w[i], odd_gk_b[i], odd_gla_norm[i], odd_w_out[i])
        h = h + mix.astype(h.dtype)
        h = h + hierarchical_moe(rmsnorm(h, norm_moe[layer]), moe_w_group[layer], moe_b_group[layer],
                                 moe_w_router[layer], moe_b_router[layer], moe_w_gate[layer],
                                 moe_w_up[layer], moe_w_down[layer])
    return rmsnorm(h, norm_final)


_drawn_inputs = setup_inputs


def setup_inputs(seed=0):
    import zlib

    import numpy as np

    out = dict(_drawn_inputs(seed))
    spreads = {}
    factors = {'norm_final': 9.001,
     'odd_gk_b': 7.331,
     'odd_gla_norm': 13.034,
     'moe_b_group': 3.489,
     'odd_conv_b': 4.474,
     'odd_ssd_norm': 4.95}
    for name, (base, spread) in spreads.items():
        noise = np.random.default_rng([zlib.crc32(name.encode()), seed]).standard_normal(out[name].shape)
        drawn = base * np.exp(spread * noise) if base else spread * noise
        out[name] = __import__('jax').numpy.asarray(drawn.astype(out[name].dtype))
    for name, factor in factors.items():
        out[name] = (out[name] * factor).astype(out[name].dtype)
    return out
```

```python
from contextlib import ExitStack

import numpy as np

import concourse.bass as bass
from concourse import mybir
from concourse.alu_op_type import AluOpType as ALU

ACT = mybir.ActivationFunctionType
AX = mybir.AxisListType
F32 = mybir.dt.float32
BF16 = mybir.dt.bfloat16
U32 = mybir.dt.uint32
I32 = mybir.dt.int32

P = 128
EPS = 1e-6
BIG = 1e30
CAP = 64


class Steps:

    def __init__(self, eng, sem):
        self.eng, self.sem, self.count = eng, sem, 0

    def __call__(self, instruction):
        self.count += 1
        instruction.then_inc(self.sem, 1)
        self.eng.wait_ge(self.sem, self.count)


def build(nc, x, norm_mix, norm_moe, norm_final, even_w_in, even_sinks, even_forget_bias, even_w_out,
          odd_w_in, odd_conv_w, odd_conv_b, odd_dt_bias, odd_a_log, odd_d_skip, odd_ssd_norm,
          odd_gk_w, odd_gk_b, odd_gla_norm, odd_w_out, moe_w_group, moe_b_group, moe_w_router,
          moe_b_router, moe_w_gate, moe_w_up, moe_w_down, out):
    T, D = x.shape[1:]
    NT, KC = T // P, D // P
    E, FF = moe_w_gate.shape[1], moe_w_gate.shape[3]
    NG = moe_w_group.shape[2]
    EPG = E // NG
    NR = NG + E
    NB = 2 * T
    MAXOV = NB // (CAP + 1)
    OVR = MAXOV + 1
    CR = T // CAP
    XROWS = E * CAP + OVR * CAP
    HQ = 8
    NC_IN = 1024 + 2 * 256
    CH = NC_IN // P
    RING = 6
    OVS = 9
    NPARAMS = 23

    EV_IN, EV_OUT = 0, 5
    MOE0 = 7
    OD = MOE0 + 3 * E
    OD_BC, OD_XS, OD_Z, OD_Q, OD_K, OD_V, OD_R, OD_OUT = OD, OD + 1, OD + 3, OD + 5, OD + 6, OD + 7, OD + 9, OD + 11
    MOE1 = OD + 15
    MOE = (MOE0, MOE1)

    ctx = ExitStack()
    with ctx:
        def sb(name, shape, dt=F32):
            return ctx.enter_context(nc.sbuf_tensor(name, shape, dt))

        made = {}

        def sem(name):
            if name not in made:
                made[name] = ctx.enter_context(nc.semaphore(name))
            return made[name]

        xrows = nc.dram_tensor("xrows", [XROWS, D], F32).ap()
        yrows = nc.dram_tensor("yrows", [XROWS, D], F32).ap()
        hsave = nc.dram_tensor("hsave", [T, D], F32).ap()

        ring = sb("ring", [P, RING, 8 * 512])
        arena = sb("arena", [P, 104 * 256])

        def at(kb, *shape, dt=F32):
            n = int(np.prod(shape))
            a = arena[:, int(kb * 256):int(kb * 256) + n]
            names = "abcd"[:len(shape)]
            if len(shape) == 1:
                return a
            pat = "p (" + " ".join(names) + ") -> p " + " ".join(names)
            return a.rearrange(pat, **{k: v for k, v in zip(names[1:], shape[1:])})

        def unit(n):
            return ring[:, n % RING, :].rearrange("p (c n) -> p c n", c=8)

        ident = sb("ident", [P, P])
        upper = sb("upper", [P, P], BF16)
        ones_b = sb("ones_b", [P, P], BF16)
        dist = sb("dist", [P, 256])
        cmask = sb("cmask", [P, P])
        tri = sb("tri", [P, P])
        gmask = sb("gmask", [P, P])
        wf = sb("wf", [P, 8, 8])
        wdg = sb("wdg", [P, 8, 32])
        prow = sb("prow", [80, P])
        pcol = sb("pcol", [P, 80])
        gmix = sb("gmix", [P, 2, 8])
        gmoe = sb("gmoe", [P, 2, 8])
        fbias = sb("fbias", [8, 1])
        sink8 = sb("sink8", [P, HQ])
        rbias = sb("rbias", [NR, 2])
        dskip = sb("dskip", [P, 16])
        dtb = sb("dtb", [16, 1])
        acol = sb("acol", [16, 1])
        gla8 = sb("gla8", [P, 8])
        ssq = sb("ssq", [P, 16])
        rstd = sb("rstd", [P, 16])
        stat = sb("stat", [P, 8, 4])
        datok = sb("datok", [P, NT, 2, 16])
        endb = sb("endb", [P, 3, 16])
        slots = sb("slots", [P, 2 * NT], U32)
        gates = sb("gates", [P, NT, 2])
        ovtab = sb("ovtab", [1, OVR + 1], I32)
        ones_f = sb("ones_f", [P, 1])
        it32 = sb("it32", [P, E])
        gid32 = sb("gid32", [P, E])
        thr = sb("thr", [P, CR])
        CONVW, CONVB, GKB, SSDN, GLAN = 0, 48, 60, 64, 72

        B = [ctx.enter_context(nc.psum_tensor(f"bank{i}", [P, 512], F32)) for i in range(8)]

        hnT = at(0, 8, 512)
        h = at(88, NT, D)
        xs = at(16, NT, D)

        def bc_in(col, n):
            return col.unsqueeze(2).to_broadcast([col.shape[0], col.shape[1], n])

        def bc_out(row, n):
            return row.unsqueeze(1).to_broadcast([row.shape[0], n, row.shape[1]])

        x_loaded = [sem(f"x_loaded{t}") for t in range(NT)]
        unit_loaded = [sem(f"unit_loaded{i}") for i in range(RING)]
        n_params = [0]

        def loaded(eng, n):
            eng.wait_ge(unit_loaded[n % RING], 16 * (n // RING + 1))

        block = ctx.enter_context(nc.Block())

        qpad = at(16, HQ, 512)
        qb, kb = at(32, HQ, 512), at(48, HQ, 512)
        kaT, va, vb = at(64, 512), at(66, NT, P), at(68, NT, 512)
        headsA, headsB = at(76, 4, 512), at(0, 4, 512)
        e_xs = at(48, NT, D)
        SA, PTA = at(88, HQ, 256), at(96, HQ, 2, P)
        PB, PTB = at(88, 4, 512), at(16, 2, 4, 512)
        fx, fe, cT, c8, cn8 = at(76, 512), at(78, 512), at(80, 512), at(82, 512), at(84, 512)
        zrow = at(68, D)
        JOBS = (["qa0", "qa1", "qa2", "qa3", "ka", "va", "f", "qb0", "qb1", "qb2", "qb3",
                 "pt0_0", "pt0_1", "pt0_2", "pt0_3", "pv0", "kb0", "kb1", "kb2", "kb3",
                 "pt1_0", "pt1_1", "pt1_2", "pt1_3", "pv1", "vb0", "vb1", "vb2", "vb3",
                 "pt2_0", "pt2_1", "pt2_2", "pt2_3", "pv2", "pt3_0", "pt3_1", "pt3_2", "pt3_3", "pv3"])
        JI = {name: i for i, name in enumerate(JOBS)}

        def kept_before(j, parity):
            return (j + 1) // 2 if parity == 0 else j // 2

        SCORES_AFTER = {"f": 0, "qb3": 1, "kb3": 2, "vb3": 3}

        xin = [at(32, D), at(36, D)]
        xT = [at(40, 8, CAP), at(42, 8, CAP)]
        sg, hb = at(44, 512), at(46, 512)
        hT = [at(48, 4, CAP), at(49, 4, CAP)]
        ysb = [at(50, 512), at(52, 512)]
        yg = at(54, 8, D)
        wr = at(86, 8, NR)
        lgT = at(56, 512)
        lg = at(58, NT, NR)
        gp, gm8, gi8 = at(59, NT, 8), at(59.125, NT, 8), at(59.25, NT, 8).bitcast(U32)
        em8, ei8 = at(59.375, NT, 8), at(59.5, NT, 8).bitcast(U32)
        gf, rt_dv, rt_gs = at(59.625, NT), at(59.65625, NT), at(59.6875, NT, NG)
        ef, gw, rden = at(59.75, 2, NT), at(59.78125, NT), at(59.8125, NT)
        rk, ok, rsl = at(59.84375, NT), at(59.875, NT), at(59.90625, NT)
        geq, em, onehot = at(60, NT, E), at(60.5, NT, E), [at(61, NT, E), at(61.5, NT, E)]
        rank, picked = at(62, NT, E), at(62.5, NT, E)
        cnt32, nover, oend, oexcl = at(63, E), at(63.125, E), at(63.25, E), at(63.375, E)
        ovf = at(63.5, OVR)
        cntb = at(64, NT * E // 2).bitcast(BF16).rearrange("p (t e) -> p t e", t=NT)
        cmp = at(65, E, CR - 1)
        cmp2 = at(67, OVR, E)

        XS, Y = at(16, NT, D), at(32, NT, D)
        BT, CT = at(48, 2, 512), at(52, 2, 512)
        Btok, CBT = at(56, NT, 2, P), at(60, 2, NT, P)
        MT = [at(64, 16, P), at(72, 16, P)]
        acc = [at(64, 512), at(66, 512)]
        cso = [at(68, 512), at(70, 512)]
        zt = [at(64, 512), at(66, 512)]
        seg = [at(80, 4, P), at(82, 4, P)]
        xdec, prev = at(84, D), at(88, D)
        tmp = at(92, 512)
        dtx, dt2, acsT, m128 = at(96, 512), at(98, 512), at(100, 512), at(102, 512)
        CONV = [8, 9, 10, 11, 0, 1, 2, 3, 4, 5, 6, 7]
        TURNED = [0, 1, 4, 5, 6, 7, 8, 9, 10, 11]
        yT = at(16, 8, 512)
        V = at(32, NT, D)
        O = V
        QD, ATT, KTOK, ST = at(48, 4, 512), at(56, 4, 512), at(64, NT, 512), at(72, 4, 256)
        g1, g2, g3, gen, gke, gki, gkd = (at(76 + 2 * i, 512) for i in range(7))
        glrT, gkw, m64 = at(90, 512), at(92, 512), at(94, 512)
        oT = at(56, 8, 512)
        rt = [at(76, 512), at(78, 512)]
        fin_g = at(0, D)
        fin_o = at(16, NT, D)
        odec = sb("odec", [P, 4, 8])

        def norm_act(act, k, src, junk):
            for t in range(NT):
                if k == 0:
                    act.wait_ge(x_loaded[t], 16)
                nc.scalar.activation(junk(t), src[:, t, :], ACT.Square,
                                     accum_out=ssq[:, t:t + 1]).then_inc(sem("norm_squares"), 1)
            act.wait_ge(sem("norm_recip"), k + 1)
            nc.scalar.activation(rstd[:, 0:NT], rstd[:, 0:NT], ACT.Sqrt).then_inc(sem("norm_rstd"), 1)

        def norm_dve(dve, step, k, src, dst, dstT, gain, first=False):
            dve.wait_ge(sem("norm_squares"), NT * (k + 1))
            step(nc.vector.tensor_scalar(ssq[:, 0:NT], ssq[:, 0:NT], 1.0 / D, EPS, ALU.mult, ALU.add))
            nc.vector.reciprocal(rstd[:, 0:NT], ssq[:, 0:NT]).then_inc(sem("norm_recip"), 1)
            dve.wait_ge(sem("norm_rstd"), k + 1)
            for t in range(NT):
                nc.vector.tensor_scalar(dst[:, t, :], src[:, t, :], rstd[:, t:t + 1], None,
                                        ALU.mult).then_inc(sem("norm_rows"), 1)
            if dstT is None:
                return
            if first:
                dve.wait_ge(sem("params"), 16 * NPARAMS)
            for i in range(2 * NT):
                t, g = i // 2, i % 2
                dve.wait_ge(sem("norm_turned"), 8 * k + i + 1)
                nc.vector.tensor_tensor(dstT[:, 4 * g:4 * g + 4, t * P:t * P + P],
                                        B[i % 2][:, :].rearrange("p (c n) -> p c n", c=4),
                                        bc_in(gain[:, 4 * g:4 * g + 4], P),
                                        ALU.mult).then_inc(sem("norm_kept"), 1)
            dve.wait_ge(sem("norm_kept"), 8 * k + 8)

        def norm_pe(pe, k, rows, strided):
            for i in range(2 * NT):
                t, g = i // 2, i % 2
                pe.wait_ge(sem("norm_rows"), NT * k + t + 1)
                if i >= 2:
                    pe.wait_ge(sem("norm_kept"), 8 * k + i - 1)
                for j in range(4):
                    c = 4 * g + j
                    if strided:
                        src = rows[:, t, :].rearrange("p (q c) -> p c q", c=KC)[:, c, :]
                    else:
                        src = rows[:, t, c * P:c * P + P]
                    last = nc.tensor.transpose(B[i % 2][:, j * P:j * P + P], src, ident[:, :])
                last.then_inc(sem("norm_turned"), 1)
            pe.wait_ge(sem("norm_kept"), 8 * k + 8)

        def project_T(dst, w, col, m):
            for c in range(KC):
                last = nc.tensor.matmul(dst, w[:, c, col:col + m], hnT[:, c, :], start=c == 0, stop=c == KC - 1)
            return last

        def project(dst, t, w, col, n):
            for c in range(KC):
                last = nc.tensor.matmul(dst, hnT[:, c, t * P:t * P + P], w[:, c, col:col + n],
                                        start=c == 0, stop=c == KC - 1)
            return last

        @block.sync
        def _(sp):
            w_ev = even_w_in[0].rearrange("(p c) n -> p c n", c=8)
            w_od = odd_w_in[0].rearrange("(p c) n -> p c n", c=8)
            wo_ev = even_w_out[0].rearrange("(c p) n -> p c n", p=P)
            wo_od = odd_w_out[0].rearrange("(k c p) n -> k p c n", k=2, p=P)
            ev_cols = [(0, 512), (512, 256), (768, 512), (1280, 512), (1792, 512)]
            od_cols = [2048, 1024, 1536, 0, 512, 2576, 3088, 3600, 4112, 4640, 5152]

            last_use = {EV_IN: ("job_done", JI["qa3"] + 1), EV_IN + 1: ("job_done", JI["va"] + 1),
                        EV_IN + 2: ("job_done", JI["qb3"] + 1), EV_IN + 3: ("job_done", JI["kb3"] + 1),
                        EV_IN + 4: ("job_done", JI["vb3"] + 1), EV_OUT: ("out_products", 4),
                        EV_OUT + 1: ("out_products", 8),
                        OD_BC: ("conv_products", 4), OD_XS: ("conv_products", 8), OD_XS + 1: ("conv_products", 12),
                        OD_Z: ("z_products", 4), OD_Z + 1: ("z_products", 8),
                        OD_Q: ("gla_products", 11), OD_K: ("gla_products", 12),
                        OD_V: ("v_products", 4), OD_V + 1: ("v_products", 8),
                        OD_R: ("r_products", 4), OD_R + 1: ("r_products", 8)}
            last_use.update({OD_OUT + i: ("out_products", 8 + 4 * (i + 1)) for i in range(4)})

            def freed(n):
                if n in last_use:
                    name, count = last_use[n]
                    sp.wait_ge(sem(name), count)
                elif n >= 0:
                    L = 0 if n < OD else 1
                    e, j = divmod(n - MOE[L], 3)
                    sp.wait_ge(sem("down_used") if j == 2 else sem("gate_up_used"), E * L + e + 1)

            def load(n, src, cols=512):
                freed(n - RING)
                sp.dma_start(unit(n)[:, :, 0:cols], src).then_inc(unit_loaded[n % RING], 16)

            for t in range(NT):
                sp.dma_start(h[:, t, :], x[0, t * P:t * P + P, :]).then_inc(x_loaded[t], 16)
            for i, (c0, n) in enumerate(ev_cols):
                load(EV_IN + i, w_ev[:, :, c0:c0 + n], n)
            load(EV_OUT, wo_ev[:, :, 0:512])
            sp.wait_ge(sem("zero_row"), 1)
            sp.dma_start(xrows.rearrange("(n p) d -> p n d", p=P),
                         zrow.unsqueeze(1).to_broadcast([P, XROWS // P, D])).then_inc(sem("rows_zeroed"), 16)
            sp.dma_start(yrows[E * CAP:, :].rearrange("(n p) d -> p n d", p=P),
                         zrow.unsqueeze(1).to_broadcast([P, OVR * CAP // P, D])).then_inc(sem("rows_zeroed"), 16)
            load(EV_OUT + 1, wo_ev[:, :, 512:1024])

            def expert(L, i, u, first):
                e = 2 * i + u
                base = MOE[L] + 3 * u
                for j, w in enumerate((moe_w_gate, moe_w_up, moe_w_down)):
                    n = base + j
                    if first:
                        freed(n - RING)
                    else:
                        sp.wait_ge(sem("down_used") if j == 2 else sem("gate_up_used"), E * L + e - 1)
                    if j == 2:
                        src = w[L, bass.ds(e, 1)].rearrange("a (p c) n -> p (a c n)", c=4)
                    else:
                        src = w[L, bass.ds(e, 1)].rearrange("a (p c) n -> p (a c n)", c=8)
                    sp.dma_start(ring[:, n % RING, :], src).then_inc(unit_loaded[n % RING], 16)

            def block_rows(L, e, u):
                sp.dma_start(xin[u][0:CAP, :], xrows[bass.ds(e * CAP, CAP), :]).then_inc(sem(f"block{u}_loaded"), 16)

            def moe(L):
                expert(L, 0, 0, True)
                expert(L, 0, 1, True)
                if L == 1:
                    sp.wait_ge(sem("o_scaled"), 16)
                    for c0, c1, w in ((0, NG, moe_w_group), (NG, NR, moe_w_router)):
                        sp.dma_start(wr[:, :, c0:c1], w[1].rearrange("(p c) n -> p c n", c=8),
                                     allow_slow_non_contiguous=True).then_inc(sem("router_loaded"), 16)
                sp.wait_ge(sem(f"scattered{L}"), 16 * 2 * NT)
                block_rows(L, 0, 0)
                block_rows(L, 1, 1)
                with sp.Fori(1, E // 2) as i:
                    for u in range(2):
                        sp.wait_ge(sem("x_turned"), E * L + 2 * i + u - 1)
                        block_rows(L, 2 * i + u, u)
                        expert(L, i, u, False)
                sp.wait_ge(sem("routed"), L + 1)
                n_over = sp.value_load(ovtab[0:1, OVR:OVR + 1], min_val=0, max_val=MAXOV)
                with sp.If(n_over > 0):
                    sp.wait_ge(sem("down_used"), E * (L + 1))
                    with sp.Fori(0, n_over) as b:
                        e = sp.value_load(ovtab[0:1, bass.ds(b, 1)], min_val=0, max_val=E - 1)
                        sp.dma_start(xin[0][0:CAP, :], xrows[bass.ds(E * CAP + b * CAP, CAP), :]).then_inc(
                            sem(f"over{L}_rows"), 16)
                        for j, w in enumerate((moe_w_gate, moe_w_up, moe_w_down)):
                            src = w[L, bass.ds(e, 1)].rearrange("a (p c) n -> p (a c n)", c=4 if j == 2 else 8)
                            sp.dma_start(ring[:, (MOE[L] + j) % RING, :], src).then_inc(sem(f"over{L}_weights"), 16)
                        sp.wait_ge(sem(f"over{L}_stored"), 32 * b + 32)
                        sp.sem_inc(sem("sp_passed"), 1)

            moe(0)
            for i, c0 in enumerate(od_cols):
                load(OD + i, w_od[:, :, c0:c0 + 512])
            for i in range(4):
                load(OD_OUT + i, wo_od[i % 2, :, :, (i // 2) * 512:(i // 2) * 512 + 512])
            moe(1)
            for t in range(NT):
                sp.wait_ge(sem("final_rows"), t + 1)
                sp.dma_start(out[0, t * P:t * P + P, :], fin_o[:, t, :]).then_inc(sem("out_stored"), 16)
            sp.wait_ge(sem("out_stored"), 16 * NT)

        @block.gpsimd
        def _(pool):
            g = nc.gpsimd
            step = Steps(pool, sem("pool_steps"))
            step(g.memset(ident[:, :], 0.0))
            step(g.affine_select(out=ident[:, :], in_=ident[:, :], compare_op=ALU.not_equal, fill=1.0, base=0,
                                 pattern=[[-1, P]], channel_multiplier=1))
            g.memset(zrow, 0.0).then_inc(sem("zero_row"), 1)
            step(g.memset(qpad, 0.0))
            step(g.memset(qb[64:128], 0.0))
            step(g.memset(qb[64:66], 1.0))
            for m in (tri, upper, ones_b, gmask, ones_f):
                step(g.memset(m[:, :], 1.0))
            step(g.memset(cmask[:, :], 0.0))
            step(g.affine_select(out=tri[:, :], in_=tri[:, :], compare_op=ALU.is_ge, fill=0.0, base=0,
                                 pattern=[[1, P]], channel_multiplier=-1))
            step(g.affine_select(out=gmask[:, :], in_=gmask[:, :], compare_op=ALU.is_ge, fill=0.0, base=0,
                                 pattern=[[1, P]], channel_multiplier=-1))
            step(g.memset(gmask[0:64, 64:128], 0.0))
            step(g.affine_select(out=upper[:, :], in_=upper[:, :], compare_op=ALU.is_gt, fill=0.0, base=0,
                                 pattern=[[1, P]], channel_multiplier=-1))
            step(g.affine_select(out=cmask[:, :], in_=cmask[:, :], compare_op=ALU.is_ge, fill=-BIG, base=0,
                                 pattern=[[-1, P]], channel_multiplier=1))
            step(g.iota(dist[:, :], [[-1, 256]], base=P, channel_multiplier=1, allow_small_or_imprecise_dtypes=True))
            step(g.affine_select(out=dist[:, :], in_=dist[:, :], compare_op=ALU.is_ge, fill=BIG, base=P,
                                 pattern=[[-1, 256]], channel_multiplier=1))
            step(g.affine_select(out=dist[:, :], in_=dist[:, :], compare_op=ALU.is_ge, fill=BIG, base=-1,
                                 pattern=[[1, 256]], channel_multiplier=-1))
            step(g.iota(it32[:, :], [[1, E]], base=0, channel_multiplier=0, allow_small_or_imprecise_dtypes=True))
            step(g.iota(gid32[:, :].rearrange("p (g e) -> p g e", g=NG), [[1, NG], [0, EPG]], base=0,
                        channel_multiplier=0, allow_small_or_imprecise_dtypes=True))
            g.iota(thr[:, :], [[CAP, CR]], base=CAP, channel_multiplier=0,
                   allow_small_or_imprecise_dtypes=True).then_inc(sem("constants"), 1)
            pool.wait_ge(sem("norm_turned"), 8)
            step(g.memset(kb[64:128], 0.0))
            g.memset(kb[64:66], 1.0).then_inc(sem("k_padded"), 1)
            pool.wait_ge(sem("k_padded"), 1)
            pool.wait_ge(sem("gate_sums"), 1)
            for hh in range(HQ):
                pool.dma_start(qb[65:66, hh, :], c8[hh:hh + 1, :]).then_inc(sem("gate_rows"), 16)
                pool.dma_start(kb[64:65, hh, :], cn8[hh:hh + 1, :]).then_inc(sem("gate_rows"), 16)

            pool.wait_ge(sem("b_turned"), 4 * HQ)
            pool.dma_start(h[:, :, :], x[0].rearrange("(t p) d -> p t d", p=P)).then_inc(
                sem("residual_loaded"), 16)

            def moe(L):
                pool.wait_ge(sem("routed"), L + 1)
                if L == 0:
                    pool.wait_ge(sem("rows_zeroed"), 32)
                for i in range(2 * NT):
                    g.indirect_dma_start(out=xrows, out_offset=bass.IndirectOffsetOnAxis(ap=slots[:, i:i + 1], axis=0),
                                         in_=xs[:, i // 2, :], in_offset=None).then_inc(sem(f"scattered{L}"), 16)
                n_over = pool.value_load(ovtab[0:1, OVR:OVR + 1], min_val=0, max_val=MAXOV)
                with pool.If(n_over > 0):
                    pool.wait_ge(sem(f"over{L}_stored"), 32 * n_over)
                    pool.sem_inc(sem("pool_passed"), 1)
                for u in range(2):
                    pool.wait_ge(sem(f"y{u}_stored"), 32 * (E // 2) * (L + 1))
                for i in range(2 * NT):
                    g.indirect_dma_start(out=yg[:, i, :], out_offset=None, in_=yrows,
                                         in_offset=bass.IndirectOffsetOnAxis(ap=slots[:, i:i + 1], axis=0)).then_inc(
                        sem(f"gathered{i // 2}"), 16)

            moe(0)
            pool.wait_ge(sem("h_saved"), 16)
            pool.wait_ge(sem("norm_rows"), 12)
            step(g.memset(m128, 1.0))
            g.memset(m128.rearrange("p (c n) -> p c n", c=NT)[:, :, 0:1], 0.0).then_inc(sem("scan_mask"), 1)
            pool.wait_ge(sem("scan_mask"), 1)
            for q in range(4 * NT):
                c, qq = divmod(q, 4)
                pool.wait_ge(sem("seg_exp"), q + 1)
                if qq == 0:
                    pool.wait_ge(sem("cb_kept"), 2)
                    if c == 0:
                        pool.wait_ge(sem("conv_tkept"), 10)
                    if c >= 2:
                        pool.wait_ge(sem("ydiag"), c - 1)
                g.tensor_tensor(MT[c % 2][:, 4 * qq:4 * qq + 4, :], seg[q % 2],
                                bc_out(CBT[:, qq // 2, c, :], 4), ALU.mult).then_inc(sem("mt_ready"), 1)
            pool.wait_ge(sem("norm_turned"), 32)
            pool.dma_start(gkw[0:16, :], odd_gk_w[0]).then_inc(sem("gk_loaded"), 16)
            step(g.memset(m64, 1.0))
            step(g.memset(ATT, 0.0))
            g.memset(m64.rearrange("p (c n) -> p c n", c=8)[:, :, 0:1], 0.0).then_inc(sem("scan_mask"), 1)
            pool.wait_ge(sem("scan_mask"), 2)
            pool.wait_ge(sem("scores_kept"), 4)
            pool.wait_ge(sem("k_turned_kept"), 4)
            pool.dma_start(h[:, :, :], hsave.rearrange("(t p) d -> p t d", p=P)).then_inc(
                sem("residual_loaded2"), 16)
            moe(1)
            pool.dma_start(fin_g, norm_final.rearrange("(a n) -> a n", a=1).to_broadcast([P, D])).then_inc(
                sem("final_gain"), 16)

        def even_keep(name, bank, copy, done):
            if name[:2] == "qa":
                m = int(name[2])
                kv = 64 * (m // 2)
                copy(qpad[kv:kv + 64, 2 * m, :], bank[0:64, :])
                copy(qpad[kv:kv + 64, 2 * m + 1, :], bank[64:128, :]).then_inc(done, 1)
            elif name == "ka":
                copy(kaT, bank[:, :]).then_inc(done, 1)
            elif name == "va":
                copy(va, bank[:, :].rearrange("p (t n) -> p t n", t=NT)).then_inc(done, 1)
            elif name[:2] in ("qb", "kb"):
                m, dst = int(name[2]), qb if name[0] == "q" else kb
                copy(dst[0:64, 2 * m, :], bank[0:64, :])
                copy(dst[0:64, 2 * m + 1, :], bank[64:128, :]).then_inc(done, 1)
            elif name[:2] == "vb":
                copy(vb[:, int(name[2]), :], bank[:, :]).then_inc(done, 1)
            elif name[:2] == "pt":
                n, m = int(name[2]), int(name[4])
                a = 1 if n == 0 else 0
                copy(PTA[:, 2 * m:2 * m + 2, a:2, :],
                     bank[:, :].rearrange("p (h a q) -> p h a q", h=2, a=2)[:, :, a:2, :]).then_inc(done, 1)
            elif name[:2] == "pv":
                n = int(name[2])
                copy(headsA[:, :, n * P:n * P + P], bank[:, :].rearrange("p (m q) -> p m q", m=4)).then_inc(done, 1)

        @block.scalar
        def _(act):
            s = nc.scalar
            step = Steps(act, sem("act_steps"))
            copy = lambda o, i: s.activation(o, i, ACT.Copy)
            loads = [
                (gmix[:, 0, :], norm_mix[0].rearrange("(p c) -> p c", c=8)),
                (gmix[:, 1, :], norm_mix[1].rearrange("(p c) -> p c", c=8)),
                (gmoe[:, 0, :], norm_moe[0].rearrange("(p c) -> p c", c=8)),
                (gmoe[:, 1, :], norm_moe[1].rearrange("(p c) -> p c", c=8)),
                (wf[:, :, :], even_w_in[0].rearrange("(p c) n -> p c n", c=8)[:, :, 2304:2312]),
                (fbias[:, :], even_forget_bias[0].rearrange("(p c) -> p c", c=1)),
                (sink8[:, :], even_sinks[0:1, :].to_broadcast([P, HQ])),
                (prow[CONVW:CONVW + 48, :], odd_conv_w[0].rearrange("j (c p) -> (j c) p", p=P)),
                (prow[CONVB:CONVB + 12, :], odd_conv_b[0].rearrange("(c p) -> c p", p=P)),
                (prow[GKB:GKB + 4, :], odd_gk_b[0].rearrange("(c p) -> c p", p=P)),
                (prow[SSDN:SSDN + 8, :], odd_ssd_norm[0].rearrange("(c p) -> c p", p=P)),
                (prow[GLAN:GLAN + 2, :], odd_gla_norm[0].rearrange("(c p) -> c p", p=P)),
                (wdg[:, :, 0:16], odd_w_in[0].rearrange("(p c) n -> p c n", c=8)[:, :, 2560:2576]),
                (wdg[:, :, 16:32], odd_w_in[0].rearrange("(p c) n -> p c n", c=8)[:, :, 4624:4640]),
                (rbias[0:NG, 0:1], moe_b_group[0].rearrange("(p c) -> p c", c=1)),
                (rbias[NG:NR, 0:1], moe_b_router[0].rearrange("(p c) -> p c", c=1)),
                (rbias[0:NG, 1:2], moe_b_group[1].rearrange("(p c) -> p c", c=1)),
                (rbias[NG:NR, 1:2], moe_b_router[1].rearrange("(p c) -> p c", c=1)),
                (dskip[:, :], odd_d_skip[0:1, :].to_broadcast([P, 16])),
                (dtb[:, :], odd_dt_bias[0].rearrange("(p c) -> p c", c=1)),
                (acol[:, :], odd_a_log[0].rearrange("(p c) -> p c", c=1)),
                (wr[:, :, 0:NG], moe_w_group[0].rearrange("(p c) n -> p c n", c=8)),
                (wr[:, :, NG:NR], moe_w_router[0].rearrange("(p c) n -> p c n", c=8)),
            ]
            assert len(loads) == NPARAMS
            for dst, src in loads:
                act.dma_start(dst, src, allow_slow_non_contiguous=True).then_inc(sem("params"), 16)

            norm_act(act, 0, h, lambda t: e_xs[:, t, :])
            act.wait_ge(sem("params"), 16 * NPARAMS)
            act.wait_ge(sem("constants"), 1)
            act.wait_ge(sem("pcol_turned"), 1)
            s.activation(pcol[:, 0:74], B[7][:, 0:74], ACT.Copy).then_inc(sem("pcol_kept"), 1)

            def keep(j):
                act.wait_ge(sem("job_done"), j + 1)
                if JOBS[j] == "f":
                    s.activation(fx[0:8], B[j % 4][0:8, :], ACT.Identity,
                                 bias=fbias[:, 0:1]).then_inc(sem("job_kept_act"), 1)
                    act.wait_ge(sem("job_kept_act"), j // 2 + 1)
                    step(s.activation(fe[0:8], fx[0:8], ACT.Abs))
                    step(s.activation(fe[0:8], fe[0:8], ACT.Exp, scale=-1.0))
                    s.activation(fe[0:8], fe[0:8], ACT.Ln, bias=1.0).then_inc(sem("gate_log"), 1)
                    return
                if JOBS[j] == "vb0" or JOBS[j] == "vb1":
                    act.wait_ge(sem("rows_zeroed"), 32)
                even_keep(JOBS[j], B[j % 4], copy, sem("job_kept_act"))

            def window_exp(n):
                k0 = P if n == 0 else 0
                act.wait_ge(sem("a_max"), n + 1)
                for hh in range(HQ):
                    s.activation(SA[:, hh, k0:256], SA[:, hh, k0:256], ACT.Exp,
                                 bias=stat[:, hh // 4, hh % 4:hh % 4 + 1], scale=0.125,
                                 accum_out=ssq[:, hh:hh + 1]).then_inc(sem("a_exp"), 1)
                s.activation(stat[:, 2:4, :], stat[:, 2:4, :], ACT.Exp).then_inc(sem("a_exp"), 1)

            for j, name in enumerate(JOBS):
                if j % 2 == 0:
                    keep(j)
                if name in SCORES_AFTER:
                    window_exp(SCORES_AFTER[name])
            for i in range(4 * HQ + 4):
                if i < 4 * HQ:
                    n = i % 4
                    act.wait_ge(sem("b_negmax"), i + 1)
                    if i >= 4:
                        act.wait_ge(sem("b_turned"), i - 3)
                    s.activation(PB[:, i % 4, 0:(n + 1) * P], B[2 + i % 4][:, 0:(n + 1) * P], ACT.Exp,
                                 bias=stat[:, 0, i % 4:i % 4 + 1], scale=0.125,
                                 accum_out=ssq[:, i % 4:i % 4 + 1]).then_inc(sem("b_exp"), 1)
                if i >= 4:
                    j = i - 4
                    hh, n = divmod(j, 4)
                    act.wait_ge(sem("b_turned"), j + 1)
                    if n == 0 and hh >= 2:
                        act.wait_ge(sem("b_values"), hh - 1)
                    s.activation(PTB[:, hh % 2, 0:n + 1, n * P:n * P + P],
                                 B[6 + j % 2][:, 0:(n + 1) * P].rearrange("p (c n) -> p c n", c=n + 1),
                                 ACT.Copy).then_inc(sem("b_tkept"), 1)

            def moe(L):
                act.wait_ge(sem("mixer_added"), 8 * (L + 1))
                norm_act(act, 1 if L == 0 else 4, h, lambda t: xs[:, t, :])
                act.wait_ge(sem("logits"), L + 1)
                s.activation(lgT[0:NR, :], B[2][0:NR, :], ACT.Identity,
                             bias=rbias[:, L:L + 1]).then_inc(sem("logits_kept"), 1)
                act.wait_ge(sem("route_args"), L + 1)
                step(s.activation(rt_gs, rt_gs, ACT.Exp))
                s.activation(rt_dv, rt_dv, ACT.Exp).then_inc(sem("route_exps"), 1)

                def silu(i, u):
                    act.wait_ge(sem("gate_up_used"), E * L + 2 * i + u + 1)
                    s.activation(sg[64:128, :], B[0][0:64, :], ACT.Silu).then_inc(sem("gated"), 1)

                def y_store(i, u):
                    act.wait_ge(sem("down_used"), E * L + 2 * i + u + 1)
                    s.activation(ysb[u], B[4 + u][:, :], ACT.Copy).then_inc(sem("y_kept"), 1)
                    act.wait_ge(sem("y_kept"), E * L + 2 * i + u + 1)
                    for a in range(2):
                        act.dma_start(yrows[bass.ds((2 * i + u) * CAP, CAP), a * 512:a * 512 + 512],
                                      ysb[u][64 * a:64 * a + 64, :]).then_inc(sem(f"y{u}_stored"), 16)

                silu(0, 0)
                silu(0, 1)
                y_store(0, 0)
                with act.Fori(1, E // 2) as i:
                    silu(i, 0)
                    y_store(i - 1, 1)
                    silu(i, 1)
                    act.wait_ge(sem("y0_stored"), 32 * ((E // 2) * L + i))
                    y_store(i, 0)
                    act.wait_ge(sem("y1_stored"), 32 * ((E // 2) * L + i))
                y_store(E // 2 - 1, 1)

                n_over = act.value_load(ovtab[0:1, OVR:OVR + 1], min_val=0, max_val=MAXOV)
                with act.If(n_over > 0):
                    with act.Fori(0, n_over) as b:
                        act.wait_ge(sem(f"over{L}_steps"), OVS * b + 3)
                        s.activation(sg[64:128, :], B[0][0:64, :], ACT.Silu).then_inc(sem(f"over{L}_steps"), 1)
                        act.wait_ge(sem(f"over{L}_steps"), OVS * b + 8)
                        act.wait_ge(sem("y0_stored"), 32 * (E // 2) * (L + 1))
                        s.activation(ysb[0], B[4][:, :], ACT.Copy).then_inc(sem(f"over{L}_steps"), 1)
                        act.wait_ge(sem(f"over{L}_steps"), OVS * b + 9)
                        for a in range(2):
                            act.dma_start(yrows[bass.ds(E * CAP + b * CAP, CAP), a * 512:a * 512 + 512],
                                          ysb[0][64 * a:64 * a + 64, :]).then_inc(sem(f"over{L}_stored"), 16)

            moe(0)

            act.wait_ge(sem("combined"), NT)
            act.dma_start(hsave.rearrange("(t p) d -> p t d", p=P), h[:, :, :]).then_inc(sem("h_saved"), 16)
            norm_act(act, 2, h, lambda t: xs[:, t, :])
            act.wait_ge(sem("dt_products"), 1)
            act.wait_ge(sem("h_saved"), 16)
            step(s.activation(dtx[0:16], B[4][0:16, :], ACT.Identity, bias=dtb[:, 0:1]))
            step(s.activation(dt2[0:16], dtx[0:16], ACT.Abs))
            step(s.activation(dt2[0:16], dt2[0:16], ACT.Exp, scale=-1.0))
            step(s.activation(dt2[0:16], dt2[0:16], ACT.Ln, bias=1.0))
            s.activation(acol[:, :], acol[:, :], ACT.Exp).then_inc(sem("dt_log"), 1)
            for j in range(CH + 1):
                if j < CH:
                    ch = CONV[j]
                    act.wait_ge(sem("conv_products"), j + 1)
                    s.activation(acc[j % 2], B[j % 2][:, :], ACT.Identity, bias=pcol[:, CONVB + ch:CONVB + ch + 1],
                                 scale=pcol[:, CONVW + 36 + ch:CONVW + 37 + ch]).then_inc(sem("conv_first"), 1)
                if j >= 1:
                    i = j - 1
                    act.wait_ge(sem("conv_summed"), i + 1)
                    if i < 2:
                        dst = BT[:, i, :]
                    elif i < 4:
                        dst = CT[:, i - 2, :]
                    else:
                        dst = cso[i % 2]
                        if i >= 6:
                            act.wait_ge(sem("conv_turned"), i - 3)
                    s.activation(dst, acc[i % 2], ACT.Silu).then_inc(sem("conv_out"), 1)
                    act.wait_ge(sem("conv_out"), i + 1)
            for c in range(NT + 1):
                if c < NT:
                    for qq in range(4):
                        q = 4 * c + qq
                        act.wait_ge(sem("seg_args"), q + 1)
                        s.activation(seg[q % 2], seg[q % 2], ACT.Exp).then_inc(sem("seg_exp"), 1)
                    act.wait_ge(sem("chunk_args"), c + 1)
                    step(s.activation(endb[:, 2, :], endb[:, 2, :], ACT.Exp))
                    step(s.activation(endb[:, 0, :], endb[:, 0, :], ACT.Exp))
                    s.activation(endb[:, 1, :], datok[:, c, 1, :], ACT.Exp).then_inc(sem("chunk_exps"), 1)
            for i in range(8):
                act.wait_ge(sem("z_products"), i + 1)
                if i >= 2:
                    act.wait_ge(sem("z_used"), i - 1)
                s.activation(zt[i % 2], B[4 + i % 2][:, :], ACT.Silu).then_inc(sem("z_gate"), 1)
            act.wait_ge(sem("z_used"), 8)
            norm_act(act, 3, Y, lambda t: at(64, NT, D)[:, t, :])
            act.wait_ge(sem("rank_products"), 1)
            act.wait_ge(sem("norm_turned"), 32)
            s.activation(glrT[0:16], B[4][0:16, :], ACT.Copy).then_inc(sem("rank_kept"), 1)
            for d in range(4):
                act.wait_ge(sem("gla_products"), 3 * d + 1)
                if d:
                    act.wait_ge(sem("gate_keys"), d)
                step(s.activation(g1, B[4 + d % 2][:, :], ACT.Identity, bias=pcol[:, GKB + d:GKB + d + 1]))
                step(s.activation(g2, g1, ACT.Abs))
                step(s.activation(g2, g2, ACT.Exp, scale=-1.0))
                s.activation(g2, g2, ACT.Ln, bias=1.0).then_inc(sem("gla_log"), 1)
                act.wait_ge(sem("gla_sums"), d + 1)
                step(s.activation(g2, g3, ACT.Exp, scale=1.0 / 16))
                step(s.activation(gen, g3, ACT.Exp, scale=-1.0 / 16))
                s.activation(gke, g1, ACT.Exp, scale=1.0 / 16).then_inc(sem("gla_exps"), 1)
            for i in range(0, 8, 2):
                act.wait_ge(sem("v_products"), i + 1)
                half, t = divmod(i, NT)
                copy(V[:, t, half * 512:half * 512 + 512], B[4 + i % 4][:, :]).then_inc(sem("v_kept_act"), 1)
            for t in range(NT):
                act.wait_ge(sem("o_products"), t + 1)
                act.wait_ge(sem("gla_states"), min(2 * t + 2, 7))
                for d in range(4):
                    src = B[2 * (t % 2) + d // 2][:, (d % 2) * 256:(d % 2) * 256 + 256]
                    if t or d:
                        act.wait_ge(sem("o_squares"), 4 * t + d)
                    s.activation(rt[0][:, 0:256], src, ACT.Square,
                                 accum_out=ssq[:, 4 * t + d:4 * t + d + 1]).then_inc(sem("o_squares"), 1)
                for a in range(2):
                    copy(O[:, t, a * 512:a * 512 + 512], B[2 * (t % 2) + a][:, :]).then_inc(sem("o_kept"), 1)
            act.wait_ge(sem("o_recip"), 1)
            s.activation(rstd[:, :], rstd[:, :], ACT.Sqrt).then_inc(sem("o_rstd"), 1)
            act.wait_ge(sem("o_squares"), 16)
            for i in range(8):
                act.wait_ge(sem("r_products"), i + 1)
                if i >= 2:
                    act.wait_ge(sem("o_scaled"), 2 * (i - 1))
                s.activation(rt[i % 2], B[4 + i % 4][:, :], ACT.Silu).then_inc(sem("r_gate"), 1)

            moe(1)
            act.wait_ge(sem("combined"), 2 * NT)
            norm_act(act, 5, h, lambda t: fin_o[:, t, :])

        @block.vector
        def _(dve):
            v = nc.vector
            step = Steps(dve, sem("dve_steps"))
            copy = v.tensor_copy

            norm_dve(dve, step, 0, h, e_xs, hnT, gmix[:, 0, :], first=True)
            dve.wait_ge(sem("params"), 16 * NPARAMS)
            dve.wait_ge(sem("constants"), 1)
            step(v.tensor_scalar(sink8[:, :], sink8[:, :], 8.0, None, ALU.mult))
            dve.wait_ge(sem("pcol_kept"), 1)
            for j in range(4):
                step(copy(gla8[:, 2 * j:2 * j + 2], pcol[:, GLAN:GLAN + 2]))

            def keep(j):
                dve.wait_ge(sem("job_done"), j + 1)
                if JOBS[j] in ("vb0", "vb1"):
                    dve.wait_ge(sem("rows_zeroed"), 32)
                if JOBS[j] == "pv0":
                    dve.wait_ge(sem("gate_rows"), 16 * 2 * HQ)
                even_keep(JOBS[j], B[j % 4], copy, sem("job_kept_dve"))

            def gate_sums():
                dve.wait_ge(sem("gate_log"), 1)
                step(v.scalar_tensor_tensor(out=fx[0:8], in0=fx[0:8], scalar=0.0, in1=fe[0:8],
                                            op0=ALU.min, op1=ALU.subtract))
                step(v.tensor_tensor_scan(cT[0:8], ones_f[0:8, 0:1].to_broadcast([8, 512]), fx[0:8], 0.0,
                                          ALU.mult, ALU.add))
                step(v.tensor_scalar(c8[0:8], cT[0:8], 8.0, None, ALU.mult))
                v.tensor_scalar(cn8[0:8], cT[0:8], -8.0, None, ALU.mult).then_inc(sem("gate_sums"), 1)

            def window_softmax(n):
                k0 = P if n == 0 else 0
                if n:
                    dve.wait_ge(sem("job_done"), JI[f"pt{n - 1}_3"] + 1)
                for g in range(2):
                    dve.wait_ge(sem("a_scores"), 2 * n + g + 1)
                    for hh in range(4 * g, 4 * g + 4):
                        v.scalar_tensor_tensor(out=SA[:, hh, k0:256], in0=dist[:, k0:256],
                                               scalar=-8.0 * 2.0 ** -(hh + 1),
                                               in1=B[4 + hh // 2][:, (hh % 2) * 256 + k0:(hh % 2) * 256 + 256],
                                               op0=ALU.mult, op1=ALU.add).then_inc(sem("a_biased"), 1)
                dve.wait_ge(sem("a_biased"), HQ * (n + 1))
                m8 = stat[:, 2:4, :].rearrange("p a b -> p (a b)")
                neg = stat[:, 0:2, :].rearrange("p a b -> p (a b)")
                den = stat[:, 4:6, :].rearrange("p a b -> p (a b)")
                step(v.tensor_reduce(m8, SA[:, :, k0:256], AX.X, ALU.max))
                step(v.tensor_tensor(m8, m8, sink8[:, :], ALU.max))
                step(v.tensor_scalar(neg, m8, -0.125, None, ALU.mult))
                v.scalar_tensor_tensor(out=m8, in0=sink8[:, :], scalar=0.125, in1=neg, op0=ALU.mult,
                                       op1=ALU.add).then_inc(sem("a_max"), 1)
                dve.wait_ge(sem("a_exp"), (HQ + 1) * (n + 1))
                step(v.tensor_tensor(den, ssq[:, 0:HQ], m8, ALU.add))
                step(v.reciprocal(den, den))
                v.tensor_tensor(SA[:, :, k0:256], SA[:, :, k0:256], bc_in(den, 256 - k0),
                                ALU.mult).then_inc(sem("a_probs"), 1)

            for j, name in enumerate(JOBS):
                if j % 2 == 1:
                    keep(j)
                if name == "f":
                    gate_sums()
                if name in SCORES_AFTER:
                    window_softmax(SCORES_AFTER[name])
            dve.wait_ge(sem("a_probs"), 4)
            for i in range(4 * HQ + 2):
                if i < 4 * HQ:
                    n, bank = i % 4, B[2 + i % 4]
                    dve.wait_ge(sem("b_scores"), i + 1)
                    step(v.tensor_tensor(bank[:, n * P:n * P + P], bank[:, n * P:n * P + P], cmask[:, :], ALU.add))
                    step(v.tensor_reduce(stat[:, 1, i % 4:i % 4 + 1], bank[:, 0:(n + 1) * P], AX.X, ALU.max))
                    v.tensor_scalar(stat[:, 0, i % 4:i % 4 + 1], stat[:, 1, i % 4:i % 4 + 1], -0.125, None,
                                    ALU.mult).then_inc(sem("b_negmax"), 1)
                if 1 <= i <= 4 * HQ:
                    j = i - 1
                    n = j % 4
                    dve.wait_ge(sem("b_exp"), j + 1)
                    step(v.reciprocal(stat[:, 2, j % 4:j % 4 + 1], ssq[:, j % 4:j % 4 + 1]))
                    v.tensor_scalar(PB[:, j % 4, 0:(n + 1) * P], PB[:, j % 4, 0:(n + 1) * P],
                                    stat[:, 2, j % 4:j % 4 + 1], None, ALU.mult).then_inc(sem("b_probs"), 1)
                if i >= 9 and (i - 9) % 8 == 4 or i == 4 * HQ + 1:
                    pair = (i - 9 - 4) // 8 if i <= 4 * HQ else HQ // 2 - 1
                    dve.wait_ge(sem("b_values"), 2 * pair + 2)
                    copy(headsB[:, pair, :], B[pair % 2][:, :]).then_inc(sem("b_heads"), 1)

            def add_out(j0, kg):
                for j in range(8):
                    half, t = divmod(j, NT)
                    dve.wait_ge(sem("out_products"), j0 + j + 1 if kg == 1 else j0 + 8 * half + NT + t + 1)
                    dst = h[:, t, half * 512:half * 512 + 512]
                    bank = B[2 + j % 4] if kg == 1 else B[j]
                    v.tensor_tensor(dst, dst, bank[:, :], ALU.add).then_inc(sem("mixer_added"), 1)

            dve.wait_ge(sem("residual_loaded"), 16)
            add_out(0, 1)

            def moe(L):
                dve.wait_ge(sem("mixer_added"), 8 * (L + 1))
                norm_dve(dve, step, 1 if L == 0 else 4, h, xs, hnT, gmoe[:, L, :])
                dve.wait_ge(sem("logits_turned"), L + 1)
                step(copy(lg, B[3][:, 0:NT * NR].rearrange("p (t e) -> p t e", t=NT)))
                step(v.memset(gp, -BIG))
                step(copy(gp[:, :, 0:NG], lg[:, :, 0:NG]))
                for t in range(NT):
                    step(v.max(gm8[:, t, :], gp[:, t, :]))
                    step(v.max_index(gi8[:, t, :], gm8[:, t, :], gp[:, t, :]))
                step(copy(gf, gi8[:, :, 0]))
                step(v.tensor_tensor(geq, bc_out(gid32[:, :], NT), bc_in(gf, E), ALU.is_equal))
                step(v.tensor_scalar(geq, geq, BIG, -BIG, ALU.mult, ALU.add))
                step(v.tensor_tensor(em, lg[:, :, NG:NR], geq, ALU.add))
                for t in range(NT):
                    step(v.max(em8[:, t, :], em[:, t, :]))
                    step(v.max_index(ei8[:, t, :], em8[:, t, :], em[:, t, :]))
                for k in range(2):
                    step(copy(ef[:, k, :], ei8[:, :, k]))
                step(v.tensor_tensor(rt_gs, lg[:, :, 0:NG], bc_in(gm8[:, :, 0], NG), ALU.subtract))
                v.tensor_tensor(rt_dv, em8[:, :, 1], em8[:, :, 0], ALU.subtract).then_inc(sem("route_args"), 1)
                for k in range(2):
                    step(v.tensor_tensor(onehot[k], bc_out(it32[:, :], NT), bc_in(ef[:, k, :], E), ALU.is_equal))
                v.tensor_tensor(cntb, onehot[0], onehot[1], ALU.add).then_inc(sem("picks"), 1)
                dve.wait_ge(sem("route_exps"), L + 1)
                step(v.tensor_reduce(gw, rt_gs, AX.X, ALU.add))
                step(v.reciprocal(gw, gw))
                step(v.tensor_scalar(rden, rt_dv, 1.0, None, ALU.add))
                step(v.reciprocal(rden, rden))
                step(v.tensor_tensor(gates[:, :, 0], gw, rden, ALU.mult))
                step(v.tensor_tensor(gates[:, :, 1], gates[:, :, 0], rt_dv, ALU.mult))
                dve.wait_ge(sem("ranks"), L + 1)
                step(copy(rank, B[2][:, 0:NT * E].rearrange("p (t e) -> p t e", t=NT)))
                step(copy(cnt32, B[2][:, NT * E:NT * E + E]))
                step(v.tensor_tensor(cmp, bc_in(cnt32, CR - 1), bc_out(thr[:, 0:CR - 1], E), ALU.is_gt))
                step(v.tensor_reduce(nover, cmp, AX.X, ALU.add))
                step(v.tensor_tensor_scan(oend, ones_f[:, 0:1].to_broadcast([P, E]), nover, 0.0, ALU.mult, ALU.add))
                step(v.tensor_tensor(oexcl, oend, nover, ALU.subtract))
                slot_v = slots[:, :].rearrange("p (t k) -> p t k", k=2)
                for k in range(2):
                    step(v.tensor_tensor(picked, onehot[k], rank, ALU.mult))
                    step(v.tensor_reduce(rk, picked, AX.X, ALU.add))
                    step(v.tensor_tensor(picked, onehot[k], bc_out(oexcl, NT), ALU.mult))
                    step(v.tensor_reduce(ok, picked, AX.X, ALU.add))
                    step(v.scalar_tensor_tensor(out=ef[:, k, :], in0=ef[:, k, :], scalar=float(CAP), in1=rk,
                                                op0=ALU.mult, op1=ALU.add))
                    step(v.scalar_tensor_tensor(out=ok, in0=ok, scalar=float(CAP), in1=rk,
                                                op0=ALU.mult, op1=ALU.add))
                    step(v.scalar_tensor_tensor(out=ok, in0=ok, scalar=float(E * CAP - CAP), in1=ef[:, k, :],
                                                op0=ALU.add, op1=ALU.subtract))
                    step(v.tensor_scalar(rk, rk, float(CAP), None, ALU.is_ge))
                    step(v.tensor_tensor(ok, ok, rk, ALU.mult))
                    step(v.tensor_tensor(rsl, ok, ef[:, k, :], ALU.add))
                    step(copy(slot_v[:, :, k], rsl))
                step(v.tensor_tensor(cmp2[0:1], bc_out(oend[0:1, :], OVR), bc_in(it32[0:1, 0:OVR], E), ALU.is_le))
                step(v.tensor_reduce(ovf[0:1, :], cmp2[0:1], AX.X, ALU.add))
                step(copy(ovtab[:, 0:OVR], ovf[0:1, :]))
                copy(ovtab[:, OVR:OVR + 1], oend[0:1, E - 1:E]).then_inc(sem("routed"), 1)

                def x_kept(i, u):
                    dve.wait_ge(sem("x_turned"), E * L + 2 * i + u + 1)
                    v.tensor_tensor(xT[u], B[2][:, :].rearrange("p (c n) -> p c n", c=8),
                                    bc_in(gmoe[:, L, :], CAP), ALU.mult).then_inc(sem("x_kept"), 1)

                def hidden(i, u):
                    dve.wait_ge(sem("gated"), E * L + 2 * i + u + 1)
                    v.tensor_tensor(hb[64:128, :], sg[64:128, :], B[1][64:128, :],
                                    ALU.mult).then_inc(sem("hidden"), 1)

                def h_kept(i, u):
                    dve.wait_ge(sem("h_turned"), E * L + 2 * i + u + 1)
                    copy(hT[u], B[3][:, 0:4 * CAP].rearrange("p (c n) -> p c n", c=4)).then_inc(sem("h_kept"), 1)

                x_kept(0, 0)
                hidden(0, 0)
                x_kept(0, 1)
                h_kept(0, 0)
                hidden(0, 1)
                with dve.Fori(1, E // 2) as i:
                    x_kept(i, 0)
                    h_kept(i - 1, 1)
                    hidden(i, 0)
                    x_kept(i, 1)
                    h_kept(i, 0)
                    hidden(i, 1)
                h_kept(E // 2 - 1, 1)

                n_over = dve.value_load(ovtab[0:1, OVR:OVR + 1], min_val=0, max_val=MAXOV)
                with dve.If(n_over > 0):
                    with dve.Fori(0, n_over) as b:
                        dve.wait_ge(sem(f"over{L}_steps"), OVS * b + 1)
                        v.tensor_tensor(xT[0], B[2][:, :].rearrange("p (c n) -> p c n", c=8),
                                        bc_in(gmoe[:, L, :], CAP), ALU.mult).then_inc(sem(f"over{L}_steps"), 1)
                        dve.wait_ge(sem(f"over{L}_steps"), OVS * b + 4)
                        v.tensor_tensor(hb[64:128, :], sg[64:128, :], B[1][64:128, :],
                                        ALU.mult).then_inc(sem(f"over{L}_steps"), 1)
                        dve.wait_ge(sem(f"over{L}_steps"), OVS * b + 6)
                        copy(hT[0], B[3][:, 0:4 * CAP].rearrange("p (c n) -> p c n", c=4)).then_inc(
                            sem(f"over{L}_steps"), 1)

                for t in range(NT):
                    dve.wait_ge(sem(f"gathered{t}"), 32 * (L + 1))
                    step(v.scalar_tensor_tensor(out=h[:, t, :], in0=yg[:, 2 * t, :], scalar=gates[:, t, 0:1],
                                                in1=h[:, t, :], op0=ALU.mult, op1=ALU.add))
                    v.scalar_tensor_tensor(out=h[:, t, :], in0=yg[:, 2 * t + 1, :], scalar=gates[:, t, 1:2],
                                           in1=h[:, t, :], op0=ALU.mult, op1=ALU.add).then_inc(sem("combined"), 1)
                dve.wait_ge(sem("combined"), NT * (L + 1))

            moe(0)

            norm_dve(dve, step, 2, h, xs, hnT, gmix[:, 1, :])
            dve.wait_ge(sem("dt_log"), 1)
            dve.wait_ge(sem("scan_mask"), 1)
            step(v.tensor_scalar(acol[:, :], acol[:, :], -1.0, None, ALU.mult))
            step(v.scalar_tensor_tensor(out=dtx[0:16], in0=dtx[0:16], scalar=0.0, in1=dt2[0:16],
                                        op0=ALU.max, op1=ALU.add))
            step(v.tensor_scalar(dt2[0:16], dtx[0:16], acol[:, 0:1], None, ALU.mult))
            v.tensor_tensor_scan(acsT[0:16], m128[0:16], dt2[0:16], 0.0, ALU.mult, ALU.add).then_inc(sem("decays"), 1)
            for j in range(CH + 2):
                if j < CH:
                    ch, bank, a = CONV[j], B[j % 2], acc[j % 2]
                    dve.wait_ge(sem("conv_first"), j + 1)
                    for back in (1, 2, 3):
                        row = CONVW + 12 * (3 - back) + ch
                        ins = v.scalar_tensor_tensor(out=a[:, back:512], in0=bank[:, 0:512 - back],
                                                     scalar=pcol[:, row:row + 1], in1=a[:, back:512],
                                                     op0=ALU.mult, op1=ALU.add)
                        if back < 3:
                            step(ins)
                        else:
                            ins.then_inc(sem("conv_summed"), 1)
                if j >= 2:
                    i = TURNED.index(j - 2) if j - 2 in TURNED else None
                    if i is not None:
                        dve.wait_ge(sem("conv_turned"), i + 1)
                        src = B[2 + i % 2][:, :].rearrange("p (t n) -> p t n", t=NT)
                        dst = Btok[:, :, i, :] if i < 2 else XS[:, :, (i - 2) * P:(i - 2) * P + P]
                        copy(dst, src).then_inc(sem("conv_tkept"), 1)
            dve.wait_ge(sem("decays_turned"), 1)
            step(copy(datok[:, :, :, :], B[5][:, 0:NT * 32].rearrange("p (t w h) -> p t w h", t=NT, w=2)))
            for g in range(2):
                dve.wait_ge(sem("cb_products"), g + 1)
                v.tensor_tensor(CBT[:, g, :, :], B[6 + g][:, :].rearrange("p (c n) -> p c n", c=NT),
                                bc_out(tri[:, :], NT), ALU.mult).then_inc(sem("cb_kept"), 1)
            dve.wait_ge(sem("cb_kept"), 2)
            dve.wait_ge(sem("conv_tkept"), 10)

            def seg_args(c):
                if c:
                    dve.wait_ge(sem("chunk_exps"), c)
                    dve.wait_ge(sem("states_kept"), c)
                    dve.wait_ge(sem("y_summed"), 2 * c)
                for qq in range(4):
                    q = 4 * c + qq
                    bank = B[4 + q % 2]
                    dve.wait_ge(sem("sums_spread"), q + 1)
                    if q >= 2:
                        dve.wait_ge(sem("mt_ready"), q - 1)
                    step(copy(endb[:, 0, 4 * qq:4 * qq + 4],
                              bank[:, :].rearrange("p (h n) -> p h n", h=4)[:, :, P - 1]))
                    for j in range(4):
                        hh = 4 * qq + j
                        ins = v.tensor_scalar(seg[q % 2][:, j, :], bank[:, j * P:j * P + P],
                                              datok[:, c, 1, hh:hh + 1], 0.0, ALU.subtract, ALU.min)
                    ins.then_inc(sem("seg_args"), 1)
                v.tensor_tensor(endb[:, 2, :], endb[:, 0, :], datok[:, c, 1, :],
                                ALU.subtract).then_inc(sem("chunk_args"), 1)

            def heads_of(row):
                return row.rearrange("p (h n) -> p h n", n=64)

            for c in range(NT):
                seg_args(c)
                xc = heads_of(XS[:, c, :])
                step(v.tensor_tensor(heads_of(Y[:, c, :]), xc, bc_in(dskip[:, :], 64), ALU.mult))
                step(v.tensor_tensor(xc, xc, bc_in(datok[:, c, 0, :], 64), ALU.mult))
                dve.wait_ge(sem("chunk_exps"), c + 1)
                v.tensor_tensor(heads_of(xdec), xc, bc_in(endb[:, 2, :], 64), ALU.mult).then_inc(sem("x_decayed"), 1)
                if c < NT - 1:
                    dve.wait_ge(sem("state_products"), c + 1)
                    for g in range(2):
                        pg = prev[:, g * 512:g * 512 + 512]
                        if c == 0:
                            ins = copy(pg, B[2 + g][:, :])
                        else:
                            step(v.tensor_tensor(heads_of(pg), heads_of(pg), bc_in(endb[:, 0, 8 * g:8 * g + 8], 64),
                                                 ALU.mult))
                            ins = v.tensor_tensor(pg, pg, B[2 + g][:, :], ALU.add)
                    ins.then_inc(sem("states_kept"), 1)
                dve.wait_ge(sem("ydiag"), c + 1)
                for g in range(2):
                    yc = Y[:, c, g * 512:g * 512 + 512]
                    if c:
                        step(v.tensor_tensor(heads_of(tmp), heads_of(B[g][:, :]),
                                             bc_in(endb[:, 1, 8 * g:8 * g + 8], 64), ALU.mult))
                        step(v.tensor_tensor(yc, yc, tmp, ALU.add))
                    v.tensor_tensor(yc, yc, B[6 + g][:, :], ALU.add).then_inc(sem("y_summed"), 1)
            for i in range(8):
                half, t = divmod(i, NT)
                dve.wait_ge(sem("z_gate"), i + 1)
                yc = Y[:, t, half * 512:half * 512 + 512]
                v.tensor_tensor(yc, yc, zt[i % 2], ALU.mult).then_inc(sem("z_used"), 1)
            dve.wait_ge(sem("z_used"), 8)
            norm_dve(dve, step, 3, Y, Y, yT, pcol[:, SSDN:SSDN + 8])

            dve.wait_ge(sem("scan_mask"), 2)
            for d in range(4):
                dve.wait_ge(sem("gla_log"), d + 1)
                step(v.scalar_tensor_tensor(out=g1, in0=g1, scalar=0.0, in1=g2, op0=ALU.min, op1=ALU.subtract))
                step(v.tensor_tensor_scan(g3, m64, g1, 0.0, ALU.mult, ALU.add))
                ends = g3.rearrange("p (c n) -> p c n", n=64)[:, :, 63]
                v.tensor_tensor(g1.rearrange("p (c n) -> p c n", n=64), bc_in(ends, 64),
                                g3.rearrange("p (c n) -> p c n", n=64), ALU.subtract).then_inc(sem("gla_sums"), 1)
                dve.wait_ge(sem("gla_exps"), d + 1)
                step(copy(odec[:, d, :], g2.rearrange("p (c n) -> p c n", n=64)[:, :, 63]))
                dve.wait_ge(sem("gla_products"), 3 * d + 3)
                step(v.scalar_tensor_tensor(out=QD[:, d, :], in0=B[6 if d % 2 == 0 else 2][:, :], scalar=P ** -0.5, in1=g2,
                                            op0=ALU.mult, op1=ALU.mult))
                if d:
                    dve.wait_ge(sem("head_scores"), d)
                step(v.tensor_tensor(gki, gen, B[7 if d % 2 == 0 else 3][:, :], ALU.mult))
                v.tensor_tensor(gkd, gke, B[7 if d % 2 == 0 else 3][:, :], ALU.mult).then_inc(sem("gate_keys"), 1)
                dve.wait_ge(sem("head_scores"), d + 1)
                v.copy_predicated(ATT[:, d, :].rearrange("p (t n) -> p t n", t=NT),
                                  bc_out(gmask[:, :].bitcast(U32), NT),
                                  B[0][:, :].rearrange("p (t n) -> p t n", t=NT)).then_inc(sem("scores_kept"), 1)
                copy(KTOK[:, :, d * P:d * P + P],
                     B[1][:, :].rearrange("p (t n) -> p t n", t=NT)).then_inc(sem("k_turned_kept"), 1)
            for i in range(1, 8, 2):
                dve.wait_ge(sem("v_products"), i + 1)
                half, t = divmod(i, NT)
                copy(V[:, t, half * 512:half * 512 + 512], B[4 + i % 4][:, :]).then_inc(sem("v_kept_dve"), 1)
            for c in range(7):
                dve.wait_ge(sem("gla_states"), c + 1)
                for d in range(4):
                    src = B[4 + d // 2][:, (d % 2) * 256:(d % 2) * 256 + 256]
                    if c == 0:
                        ins = copy(ST[:, d, :], src)
                    else:
                        ins = v.scalar_tensor_tensor(out=ST[:, d, :], in0=ST[:, d, :], scalar=odec[:, d, c:c + 1],
                                                     in1=src, op0=ALU.mult, op1=ALU.add)
                ins.then_inc(sem("gla_states_kept"), 1)
                dve.wait_ge(sem("gla_states_kept"), c + 1)
            dve.wait_ge(sem("o_squares"), 16)
            step(v.tensor_scalar(ssq[:, :], ssq[:, :], 1.0 / 256, EPS, ALU.mult, ALU.add))
            v.reciprocal(rstd[:, :], ssq[:, :]).then_inc(sem("o_recip"), 1)
            dve.wait_ge(sem("o_rstd"), 1)
            dve.wait_ge(sem("o_kept"), 8)
            for i in range(8):
                half, t = divmod(i, NT)
                dve.wait_ge(sem("r_gate"), i + 1)
                for a in range(2):
                    d = 2 * half + a
                    oc = O[:, t, d * 256:d * 256 + 256]
                    v.scalar_tensor_tensor(out=oc, in0=oc, scalar=rstd[:, 4 * t + d:4 * t + d + 1],
                                           in1=rt[i % 2][:, a * 256:a * 256 + 256],
                                           op0=ALU.mult, op1=ALU.mult).then_inc(sem("o_scaled"), 1)
            for i in range(2 * NT):
                t, g = i // 2, i % 2
                dve.wait_ge(sem("o_turned"), i + 1)
                v.tensor_tensor(oT[:, 4 * g:4 * g + 4, t * P:t * P + P],
                                B[i % 2][:, :].rearrange("p (c n) -> p c n", c=4),
                                bc_in(gla8[:, 4 * g:4 * g + 4], P), ALU.mult).then_inc(sem("o_tkept"), 1)
            dve.wait_ge(sem("residual_loaded2"), 16)
            add_out(8, 2)

            moe(1)
            norm_dve(dve, step, 5, h, fin_o, None, None)
            dve.wait_ge(sem("final_gain"), 16)
            dve.wait_ge(sem("norm_rows"), 6 * NT)
            for t in range(NT):
                v.tensor_tensor(fin_o[:, t, :], fin_o[:, t, :], fin_g, ALU.mult).then_inc(sem("final_rows"), 1)

        @block.tensor
        def _(pe):
            mm, turn = nc.tensor.matmul, nc.tensor.transpose
            pe.wait_ge(sem("constants"), 1)
            norm_pe(pe, 0, e_xs, True)
            pe.wait_ge(sem("params"), 16 * NPARAMS)
            turn(B[7][:, 0:74], prow[0:74, :], ident[0:74, 0:74]).then_inc(sem("pcol_turned"), 1)

            def job_bank(j):
                if j >= 4:
                    pe.wait_ge(sem("job_kept_act") if j % 2 == 0 else sem("job_kept_dve"), (j - 4) // 2 + 1)
                return B[j % 4]

            def window_scores(n):
                k0 = P if n == 0 else 0
                if n == 0:
                    pe.wait_ge(sem("pcol_kept"), 1)
                    pe.wait_ge(sem("job_kept_act"), JI["ka"] // 2 + 1)
                    pe.wait_ge(sem("job_kept_dve"), 2)
                for g in range(2):
                    if n:
                        pe.wait_ge(sem("a_biased"), HQ * (n - 1) + 4 * g + 4)
                    for hh in range(4 * g, 4 * g + 4):
                        last = mm(B[4 + hh // 2][:, (hh % 2) * 256 + k0:(hh % 2) * 256 + 256],
                                  qpad[:, hh, n * P:n * P + P], kaT[:, (n - 1) * P + k0:(n + 1) * P],
                                  start=True, stop=True)
                    last.then_inc(sem("a_scores"), 1)

            for j, name in enumerate(JOBS):
                bank = job_bank(j)
                if name[:2] == "qa":
                    if name == "qa0":
                        loaded(pe, EV_IN)
                    last = project_T(bank[:, :], unit(EV_IN), int(name[2]) * P, P)
                elif name == "ka":
                    loaded(pe, EV_IN + 1)
                    last = project_T(bank[:, :], unit(EV_IN + 1), 0, P)
                elif name == "va":
                    for t in range(NT):
                        last = project(bank[:, t * P:t * P + P], t, unit(EV_IN + 1), P, P)
                elif name == "f":
                    for c in range(KC):
                        last = mm(bank[0:8, :], wf[:, c, :], hnT[:, c, :], start=c == 0, stop=c == KC - 1)
                elif name[:2] in ("qb", "kb"):
                    n = EV_IN + (2 if name[0] == "q" else 3)
                    if name[2] == "0":
                        loaded(pe, n)
                    last = project_T(bank[:, :], unit(n), int(name[2]) * P, P)
                elif name[:2] == "vb":
                    if name == "vb0":
                        loaded(pe, EV_IN + 4)
                    last = project(bank[:, :], int(name[2]), unit(EV_IN + 4), 0, 512)
                elif name[:2] == "pt":
                    n, m = int(name[2]), int(name[4])
                    if m == 0:
                        pe.wait_ge(sem("a_probs"), n + 1)
                    for b in range(2):
                        for a in range(1 if n == 0 else 0, 2):
                            last = turn(bank[:, b * 256 + a * P:b * 256 + a * P + P],
                                        SA[:, 2 * m + b, a * P:a * P + P], ident[:, :])
                elif name[:2] == "pv":
                    n = int(name[2])
                    pe.wait_ge(sem("job_kept_act"), kept_before(j, 0))
                    pe.wait_ge(sem("job_kept_dve"), kept_before(j, 1))
                    for hh in range(HQ):
                        lo = 64 * (hh % 2)
                        o = bank[lo:lo + 64, (hh // 2) * P:(hh // 2) * P + P]
                        kv = 64 * (hh // 4)
                        if n:
                            mm(o, va[:, n - 1, kv:kv + 64], PTA[:, hh, 0, :], start=True, stop=False)
                        last = mm(o, va[:, n, kv:kv + 64], PTA[:, hh, 1, :], start=n == 0, stop=True)
                last.then_inc(sem("job_done"), 1)
                if name in SCORES_AFTER:
                    window_scores(SCORES_AFTER[name])

            pe.wait_ge(sem("gate_rows"), 16 * 2 * HQ)
            pe.wait_ge(sem("k_padded"), 1)
            pe.wait_ge(sem("job_kept_act"), kept_before(len(JOBS), 0))
            pe.wait_ge(sem("job_kept_dve"), kept_before(len(JOBS), 1))
            pe.wait_ge(sem("a_biased"), 4 * HQ)

            def values(hh):
                pe.wait_ge(sem("b_tkept"), 4 * hh + 4)
                pair, lo = hh // 2, 64 * (hh % 2)
                if pair >= 2:
                    pe.wait_ge(sem("b_heads"), pair - 1)
                for j in range(NT):
                    last = mm(B[pair % 2][lo:lo + 64, j * P:512], vb[:, j, hh * 64:hh * 64 + 64],
                              PTB[:, hh % 2, j, j * P:512], start=j == 0, stop=j == NT - 1)
                last.then_inc(sem("b_values"), 1)

            for i in range(4 * HQ + 3):
                if i < 4 * HQ:
                    hh, n = divmod(i, 4)
                    if i >= 4:
                        pe.wait_ge(sem("b_exp"), i - 3)
                    mm(B[2 + i % 4][:, 0:(n + 1) * P], qb[:, hh, n * P:n * P + P], kb[:, hh, 0:(n + 1) * P],
                       start=True, stop=True).then_inc(sem("b_scores"), 1)
                if i >= 3:
                    j = i - 3
                    n = j % 4
                    pe.wait_ge(sem("b_probs"), j + 1)
                    if j >= 2:
                        pe.wait_ge(sem("b_tkept"), j - 1)
                    for a in range(n + 1):
                        last = turn(B[6 + j % 2][:, a * P:a * P + P], PB[:, j % 4, a * P:a * P + P], ident[:, :])
                    last.then_inc(sem("b_turned"), 1)
                    if n == 0 and j:
                        values(j // 4 - 1)
            values(HQ - 1)

            pe.wait_ge(sem("b_heads"), 4)
            for j in range(8):
                half, t = divmod(j, NT)
                if t == 0:
                    loaded(pe, EV_OUT + half)
                if j >= 4:
                    pe.wait_ge(sem("mixer_added"), j - 3)
                for c in range(KC):
                    hT_c = headsA[:, c, t * P:t * P + P] if c < 4 else headsB[:, c - 4, t * P:t * P + P]
                    last = mm(B[2 + j % 4][:, :], hT_c, unit(EV_OUT + half)[:, c, :], start=c == 0, stop=c == KC - 1)
                last.then_inc(sem("out_products"), 1)

            def turn_rows(u):
                pe.sem_inc(sem("pe_passed"), 1)
                for c in range(KC):
                    last = turn(B[2][:, c * CAP:c * CAP + CAP],
                                xin[u][0:CAP, :].rearrange("p (q c) -> p c q", c=KC)[:, c, :], ident[0:CAP, 0:CAP])
                return last

            def turn_hidden():
                pe.sem_inc(sem("pe_passed"), 1)
                for c in range(4):
                    last = turn(B[3][:, c * CAP:c * CAP + CAP],
                                hb[64:128, :].rearrange("p (q c) -> p c q", c=4)[:, c, :], ident[64:128, 64:128])
                return last

            def gate_up_products(u, n):
                for c in range(KC):
                    mm(B[0][0:64, :], xT[u][:, c, :], unit(n)[:, c, :], start=c == 0, stop=c == KC - 1)
                    last = mm(B[1][64:128, :], xT[u][:, c, :], unit(n + 1)[:, c, :], start=c == 0, stop=c == KC - 1)
                return last

            def down_products(u, n, bank):
                w = ring[:, n % RING, :].rearrange("p (c n) -> p c n", c=4)
                for c in range(4):
                    for a in range(2):
                        last = mm(bank[64 * a:64 * a + 64, :], hT[u][:, c, :], w[:, c, a * 512:a * 512 + 512],
                                  start=c == 0, stop=c == 3)
                return last

            def moe(L):
                norm_pe(pe, 1 if L == 0 else 4, xs, True)
                if L == 1:
                    pe.wait_ge(sem("router_loaded"), 32)
                for c in range(KC):
                    last = mm(B[2][0:NR, :], wr[:, c, :], hnT[:, c, :], start=c == 0, stop=c == KC - 1)
                last.then_inc(sem("logits"), 1)
                pe.wait_ge(sem("logits_kept"), L + 1)
                for t in range(NT):
                    last = turn(B[3][:, t * NR:t * NR + NR], lgT[0:NR, t * P:t * P + P], ident[0:NR, 0:NR])
                last.then_inc(sem("logits_turned"), 1)
                pe.wait_ge(sem("picks"), L + 1)
                for t in range(NT):
                    for j in range(t):
                        mm(B[2][:, t * E:t * E + E], ones_b[:, :], cntb[:, j, :], start=j == 0, stop=False)
                    mm(B[2][:, t * E:t * E + E], upper[:, :], cntb[:, t, :], start=t == 0, stop=True)
                for j in range(NT):
                    last = mm(B[2][:, NT * E:NT * E + E], ones_b[:, :], cntb[:, j, :], start=j == 0, stop=j == NT - 1)
                last.then_inc(sem("ranks"), 1)

                base = MOE[L]

                def unit_ready(i, n):
                    pe.wait_ge(unit_loaded[n % RING], 16 * i + 16 * (n // RING + 1))

                def rows(i, u):
                    pe.wait_ge(sem(f"block{u}_loaded"), 16 * ((E // 2) * L + i + 1))
                    pe.wait_ge(sem("x_kept"), E * L + 2 * i + u)
                    turn_rows(u).then_inc(sem("x_turned"), 1)

                def gate_up(i, u):
                    pe.wait_ge(sem("x_kept"), E * L + 2 * i + u + 1)
                    unit_ready(i, base + 3 * u)
                    unit_ready(i, base + 3 * u + 1)
                    gate_up_products(u, base + 3 * u).then_inc(sem("gate_up_used"), 1)

                def down(i, u):
                    pe.wait_ge(sem("h_kept"), E * L + 2 * i + u + 1)
                    unit_ready(i, base + 3 * u + 2)
                    down_products(u, base + 3 * u + 2, B[4 + u]).then_inc(sem("down_used"), 1)

                def hidden_rows(i, u):
                    pe.wait_ge(sem("hidden"), E * L + 2 * i + u + 1)
                    turn_hidden().then_inc(sem("h_turned"), 1)

                rows(0, 0)
                gate_up(0, 0)
                rows(0, 1)
                hidden_rows(0, 0)
                gate_up(0, 1)
                down(0, 0)
                with pe.Fori(1, E // 2) as i:
                    rows(i, 0)
                    hidden_rows(i - 1, 1)
                    gate_up(i, 0)
                    pe.wait_ge(sem("y_kept"), E * L + 2 * i - 1)
                    down(i - 1, 1)
                    rows(i, 1)
                    hidden_rows(i, 0)
                    gate_up(i, 1)
                    pe.wait_ge(sem("y_kept"), E * L + 2 * i)
                    down(i, 0)
                hidden_rows(E // 2 - 1, 1)
                pe.wait_ge(sem("y_kept"), E * L + E - 2)
                down(E // 2 - 1, 1)

                n_over = pe.value_load(ovtab[0:1, OVR:OVR + 1], min_val=0, max_val=MAXOV)
                with pe.If(n_over > 0):
                    pe.wait_ge(sem("y_kept"), E * (L + 1))
                    with pe.Fori(0, n_over) as b:
                        pe.wait_ge(sem(f"over{L}_rows"), 16 * b + 16)
                        turn_rows(0).then_inc(sem(f"over{L}_steps"), 1)
                        pe.wait_ge(sem(f"over{L}_steps"), OVS * b + 2)
                        pe.wait_ge(sem(f"over{L}_weights"), 48 * b + 48)
                        gate_up_products(0, base).then_inc(sem(f"over{L}_steps"), 1)
                        pe.wait_ge(sem(f"over{L}_steps"), OVS * b + 5)
                        turn_hidden().then_inc(sem(f"over{L}_steps"), 1)
                        pe.wait_ge(sem(f"over{L}_steps"), OVS * b + 7)
                        down_products(0, base + 2, B[4]).then_inc(sem(f"over{L}_steps"), 1)

            moe(0)

            norm_pe(pe, 2, xs, True)
            for c in range(KC):
                last = mm(B[4][0:16, :], wdg[:, c, 0:16], hnT[:, c, :], start=c == 0, stop=c == KC - 1)
            last.then_inc(sem("dt_products"), 1)
            for j in range(CH + 1):
                if j < CH:
                    n = OD_BC + j // 4
                    if j % 4 == 0:
                        loaded(pe, n)
                    if j >= 2:
                        pe.wait_ge(sem("conv_summed"), j - 1)
                    project_T(B[j % 2][:, :], unit(n), (j % 4) * P, P).then_inc(sem("conv_products"), 1)
                if j >= 1 and j - 1 in TURNED:
                    i = TURNED.index(j - 1)
                    pe.wait_ge(sem("conv_out"), j)
                    if i >= 2:
                        pe.wait_ge(sem("conv_tkept"), i - 1)
                    src = BT[:, i, :] if i < 2 else cso[(j - 1) % 2]
                    for t in range(NT):
                        last = turn(B[2 + i % 2][:, t * P:t * P + P], src[:, t * P:t * P + P], ident[:, :])
                    last.then_inc(sem("conv_turned"), 1)
            pe.wait_ge(sem("decays"), 1)
            for t in range(NT):
                turn(B[5][:, t * 32:t * 32 + 16], dtx[0:16, t * P:t * P + P], ident[0:16, 0:16])
                last = turn(B[5][:, t * 32 + 16:t * 32 + 32], acsT[0:16, t * P:t * P + P], ident[0:16, 0:16])
            last.then_inc(sem("decays_turned"), 1)
            for g in range(2):
                for c in range(NT):
                    last = mm(B[6 + g][:, c * P:c * P + P], BT[:, g, c * P:c * P + P], CT[:, g, c * P:c * P + P],
                              start=True, stop=True)
                last.then_inc(sem("cb_products"), 1)
            pe.wait_ge(sem("cb_kept"), 2)

            for c in range(NT):
                for qq in range(4):
                    q = 4 * c + qq
                    if q >= 2:
                        pe.wait_ge(sem("seg_args"), q - 1)
                    for j in range(4):
                        hh = 4 * qq + j
                        last = mm(B[4 + q % 2][:, j * P:j * P + P], ident[0:16, hh:hh + 1].to_broadcast([16, P]),
                                  acsT[0:16, c * P:c * P + P], start=True, stop=True)
                    last.then_inc(sem("sums_spread"), 1)
                pe.wait_ge(sem("x_decayed"), c + 1)
                if c:
                    pe.wait_ge(sem("states_kept"), c)
                    pe.wait_ge(sem("y_summed"), 2 * c)
                    for g in range(2):
                        mm(B[g][:, :], CT[:, g, c * P:c * P + P], prev[:, g * 512:g * 512 + 512], start=True, stop=True)
                if c < NT - 1:
                    for g in range(2):
                        last = mm(B[2 + g][:, :], Btok[:, c, g, :], xdec[:, g * 512:g * 512 + 512],
                                  start=True, stop=True)
                    last.then_inc(sem("state_products"), 1)
                pe.wait_ge(sem("mt_ready"), 4 * c + 4)
                for hh in range(16):
                    last = mm(B[6 + hh // 8][:, (hh % 8) * 64:(hh % 8) * 64 + 64], MT[c % 2][:, hh, :],
                              XS[:, c, hh * 64:hh * 64 + 64], start=True, stop=True)
                last.then_inc(sem("ydiag"), 1)
            pe.wait_ge(sem("seg_args"), 4 * NT)
            for i in range(8):
                half, t = divmod(i, NT)
                if t == 0:
                    loaded(pe, OD_Z + half)
                if i >= 2:
                    pe.wait_ge(sem("z_gate"), i - 1)
                project(B[4 + i % 2][:, :], t, unit(OD_Z + half), 0, 512).then_inc(sem("z_products"), 1)
            norm_pe(pe, 3, Y, False)

            pe.wait_ge(sem("z_gate"), 8)
            for c in range(KC):
                last = mm(B[4][0:16, :], wdg[:, c, 16:32], hnT[:, c, :], start=c == 0, stop=c == KC - 1)
            last.then_inc(sem("rank_products"), 1)
            pe.wait_ge(sem("gk_loaded"), 16)
            pe.wait_ge(sem("rank_kept"), 1)
            loaded(pe, OD_Q)
            loaded(pe, OD_K)
            for d in range(5):
                if d < 4:
                    if d >= 2:
                        pe.wait_ge(sem("gla_log"), d - 1)
                        pe.wait_ge(sem("gate_keys"), d - 1)
                    q = 6 if d % 2 == 0 else 2
                    mm(B[4 + d % 2][:, :], gkw[0:16, d * P:d * P + P], glrT[0:16, :],
                       start=True, stop=True).then_inc(sem("gla_products"), 1)
                    project_T(B[q][:, :], unit(OD_Q), d * P, P).then_inc(sem("gla_products"), 1)
                    project_T(B[q + 1][:, :], unit(OD_K), d * P, P).then_inc(sem("gla_products"), 1)
                if d:
                    e = d - 1
                    pe.wait_ge(sem("gate_keys"), e + 1)
                    pe.wait_ge(sem("scores_kept"), e)
                    pe.wait_ge(sem("k_turned_kept"), e)
                    for t in range(NT):
                        mm(B[0][:, t * P:t * P + P], gki[:, t * P:t * P + P], QD[:, e, t * P:t * P + P],
                           start=True, stop=True)
                    for t in range(NT):
                        last = turn(B[1][:, t * P:t * P + P], gkd[:, t * P:t * P + P], ident[:, :])
                    last.then_inc(sem("head_scores"), 1)
            pe.wait_ge(sem("gla_log"), 4)
            for i in range(8):
                half, t = divmod(i, NT)
                if t == 0:
                    loaded(pe, OD_V + half)
                if i >= 4:
                    pe.wait_ge(sem("v_kept_act") if i % 2 == 0 else sem("v_kept_dve"), (i - 4) // 2 + 1)
                project(B[4 + i % 4][:, :], t, unit(OD_V + half), 0, 512).then_inc(sem("v_products"), 1)
            pe.wait_ge(sem("scores_kept"), 4)
            pe.wait_ge(sem("k_turned_kept"), 4)
            pe.wait_ge(sem("v_kept_act"), 4)
            pe.wait_ge(sem("v_kept_dve"), 4)
            for t in range(NT):
                if t >= 2:
                    pe.wait_ge(sem("o_kept"), 2 * (t - 1))

                def o_bank(d):
                    return B[2 * (t % 2) + d // 2]

                for d in range(4):
                    mm(o_bank(d)[:, (d % 2) * 256:(d % 2) * 256 + 256], ATT[:, d, t * P:t * P + P],
                       V[:, t, d * 256:d * 256 + 256], start=d % 2 == 0, stop=True, skip_group_check=True)
                for j in range(2):
                    c, lo = 2 * t + j, 64 * j
                    if c:
                        pe.wait_ge(sem("gla_states_kept"), c)
                        for d in range(4):
                            last = mm(o_bank(d)[lo:lo + 64, (d % 2) * 256:(d % 2) * 256 + 256],
                                      QD[:, d, c * 64:c * 64 + 64], ST[:, d, :], start=False, stop=True,
                                      skip_group_check=True)
                        if j:
                            last.then_inc(sem("o_products"), 1)
                    if c < 7:
                        for d in range(4):
                            last = mm(B[4 + d // 2][:, (d % 2) * 256:(d % 2) * 256 + 256],
                                      KTOK[lo:lo + 64, t, d * P:d * P + P], V[lo:lo + 64, t, d * 256:d * 256 + 256],
                                      start=True, stop=True)
                        last.then_inc(sem("gla_states"), 1)
            pe.wait_ge(sem("gla_states_kept"), 7)
            for i in range(8):
                half, t = divmod(i, NT)
                if t == 0:
                    loaded(pe, OD_R + half)
                if i >= 4:
                    pe.wait_ge(sem("r_gate"), i - 3)
                project(B[4 + i % 4][:, :], t, unit(OD_R + half), 0, 512).then_inc(sem("r_products"), 1)
            pe.wait_ge(sem("o_scaled"), 16)
            for i in range(2 * NT):
                t, g = i // 2, i % 2
                if i >= 2:
                    pe.wait_ge(sem("o_tkept"), i - 1)
                for j in range(4):
                    c = 4 * g + j
                    last = turn(B[i % 2][:, j * P:j * P + P], O[:, t, c * P:c * P + P], ident[:, :])
                last.then_inc(sem("o_turned"), 1)
            pe.wait_ge(sem("o_tkept"), 8)
            for half in range(2):
                for kg in range(2):
                    n = OD_OUT + 2 * half + kg
                    loaded(pe, n)
                    for t in range(NT):
                        for c in range(KC):
                            src = (yT, oT)[kg]
                            last = mm(B[4 * half + t][:, :], src[:, c, t * P:t * P + P], unit(n)[:, c, :],
                                      start=kg == 0 and c == 0, stop=kg == 1 and c == KC - 1)
                        last.then_inc(sem("out_products"), 1)
            moe(1)


_INS = ['x', 'norm_mix', 'norm_moe', 'norm_final', 'even_w_in', 'even_sinks', 'even_forget_bias', 'even_w_out',
        'odd_w_in', 'odd_conv_w', 'odd_conv_b', 'odd_dt_bias', 'odd_a_log', 'odd_d_skip', 'odd_ssd_norm',
        'odd_gk_w', 'odd_gk_b', 'odd_gla_norm', 'odd_w_out', 'moe_w_group', 'moe_b_group', 'moe_w_router',
        'moe_b_router', 'moe_w_gate', 'moe_w_up', 'moe_w_down']


def kernel(**inputs):
    import numpy as _np
    import concourse.bacc as _bacc
    from concourse import mybir as _mybir
    from concourse.bass_utils import run_bass_kernel_spmd as _run

    nc = _bacc.Bacc("TRN2", target_bir_lowering=False, num_devices=1)
    arrays, args = {}, []
    for name in _INS:
        a = _np.ascontiguousarray(inputs[name])
        arrays[f"in_{name}"] = a
        args.append(nc.dram_tensor(f"in_{name}", a.shape, _mybir.dt.from_np(a.dtype), kind="ExternalInput").ap())
    x = arrays["in_x"]
    out = nc.dram_tensor("out", x.shape, _mybir.dt.from_np(x.dtype), kind="ExternalOutput").ap()
    build(nc, *args, out)
    r = _run(nc, [arrays], core_ids=[0])
    return r.results[0]["out"]
```

```python
from contextlib import ExitStack

import numpy as np

import concourse.bass as bass
from concourse import mybir
from concourse.alu_op_type import AluOpType as ALU

ACT = mybir.ActivationFunctionType
AX = mybir.AxisListType
F32 = mybir.dt.float32
BF16 = mybir.dt.bfloat16
U32 = mybir.dt.uint32
I32 = mybir.dt.int32

P = 128
EPS = 1e-6
BIG = 1e30
CAP = 64


class Steps:

    def __init__(self, eng, sem):
        self.eng, self.sem, self.count = eng, sem, 0

    def __call__(self, instruction):
        self.count += 1
        instruction.then_inc(self.sem, 1)
        self.eng.wait_ge(self.sem, self.count)


def build(nc, x, norm_mix, norm_moe, norm_final, even_w_in, even_sinks, even_forget_bias, even_w_out,
          odd_w_in, odd_conv_w, odd_conv_b, odd_dt_bias, odd_a_log, odd_d_skip, odd_ssd_norm,
          odd_gk_w, odd_gk_b, odd_gla_norm, odd_w_out, moe_w_group, moe_b_group, moe_w_router,
          moe_b_router, moe_w_gate, moe_w_up, moe_w_down, out):
    T, D = x.shape[1:]
    NT, KC = T // P, D // P
    E, FF = moe_w_gate.shape[1], moe_w_gate.shape[3]
    NG = moe_w_group.shape[2]
    EPG = E // NG
    NR = NG + E
    NB = 2 * T
    MAXOV = NB // (CAP + 1)
    OVR = MAXOV + 1
    CR = T // CAP
    XROWS = E * CAP + OVR * CAP
    HQ = 8
    NC_IN = 1024 + 2 * 256
    CH = NC_IN // P
    RING = 6
    OVS = 9
    NPARAMS = 17

    EV_IN, EV_OUT = 0, 5
    MOE0 = 7
    OD = MOE0 + 3 * E
    OD_BC, OD_XS, OD_Z, OD_Q, OD_K, OD_V, OD_R = OD, OD + 1, OD + 3, OD + 5, OD + 6, OD + 7, OD + 11
    OD_OUT = (OD + 9, OD + 13)
    MOE1 = OD + 15
    MOE = (MOE0, MOE1)

    ctx = ExitStack()
    with ctx:
        def sb(name, shape, dt=F32):
            return ctx.enter_context(nc.sbuf_tensor(name, shape, dt))

        made = {}

        def sem(name):
            if name not in made:
                made[name] = ctx.enter_context(nc.semaphore(name))
            return made[name]

        xrows = nc.dram_tensor("xrows", [XROWS, D], F32).ap()
        yrows = nc.dram_tensor("yrows", [XROWS, D], F32).ap()
        sums_d = nc.dram_tensor("sums_d", [16, T], F32).ap()
        hsave = nc.dram_tensor("hsave", [T, D], F32).ap()

        ring = sb("ring", [P, RING, 8 * 512])
        arena = sb("arena", [P, 104 * 256])

        def at(kb, *shape, dt=F32):
            n = int(np.prod(shape))
            a = arena[:, int(kb * 256):int(kb * 256) + n]
            names = "abcd"[:len(shape)]
            if len(shape) == 1:
                return a
            pat = "p (" + " ".join(names) + ") -> p " + " ".join(names)
            return a.rearrange(pat, **{k: v for k, v in zip(names[1:], shape[1:])})

        def unit(n):
            return ring[:, n % RING, :].rearrange("p (c n) -> p c n", c=8)

        ident = sb("ident", [P, P])
        upper = sb("upper", [P, P], BF16)
        ones_b = sb("ones_b", [P, P], BF16)
        dist = sb("dist", [P, 256])
        cmask = sb("cmask", [P, P])
        tri = sb("tri", [P, P])
        gmask = sb("gmask", [P, P])
        wf = sb("wf", [P, 8, 8])
        wdg = sb("wdg", [P, 8, 48])
        pcol = sb("pcol", [P, 80])
        gmix = sb("gmix", [P, 2, 8])
        gmoe = sb("gmoe", [P, 2, 8])
        fbias = sb("fbias", [8, 1])
        sink8 = sb("sink8", [P, HQ])
        dskip = sb("dskip", [P, 16])
        dtb = sb("dtb", [16, 1])
        acol = sb("acol", [16, 1])
        gla8 = sb("gla8", [P, 8])
        ssq = sb("ssq", [P, 16])
        rstd = sb("rstd", [P, 16])
        stat = sb("stat", [P, 8, 4])
        datok = sb("datok", [P, NT, 2, 16])
        endb = sb("endb", [P, 3, 16])
        slots = sb("slots", [P, 2 * NT], U32)
        gates = sb("gates", [P, NT, 2])
        ovtab = sb("ovtab", [1, OVR + 1], I32)
        ones_f = sb("ones_f", [P, 1])
        it32 = sb("it32", [P, E])
        gid32 = sb("gid32", [P, E])
        thr = sb("thr", [P, CR])
        CONVW, CONVB, GKB, SSDN, GLAN = 0, 48, 60, 64, 72

        B = [ctx.enter_context(nc.psum_tensor(f"bank{i}", [P, 512], F32)) for i in range(8)]

        hnT = at(0, 8, 512)
        h = at(88, NT, D)
        xs = at(16, NT, D)

        def bc_in(col, n):
            return col.unsqueeze(2).to_broadcast([col.shape[0], col.shape[1], n])

        def bc_out(row, n):
            return row.unsqueeze(1).to_broadcast([row.shape[0], n, row.shape[1]])

        x_loaded = [sem(f"x_loaded{t}") for t in range(NT)]
        unit_loaded = [sem(f"unit_loaded{i}") for i in range(RING)]
        n_params = [0]

        def loaded(eng, n):
            eng.wait_ge(unit_loaded[n % RING], 16 * (n // RING + 1))

        block = ctx.enter_context(nc.Block())

        qpad = at(16, HQ, 512)
        qb, kb = at(32, HQ, 512), at(48, HQ, 512)
        kaT, va, vb = at(64, 512), at(66, NT, P), at(68, NT, 512)
        headsA, headsB = at(76, 4, 512), at(0, 4, 512)
        e_xs = at(48, NT, D)
        SA, PTA = at(88, HQ, 256), at(96, HQ, 2, P)
        PB, PTB = at(88, 4, 512), at(16, 2, 4, 512)
        fx, fe, cT, c8, cn8 = at(76, 512), at(78, 512), at(80, 512), at(82, 512), at(84, 512)
        zrow = at(68, D)
        JOBS = (["qa0", "qa1", "qa2", "qa3", "ka", "va", "f", "qb0", "qb1", "qb2", "qb3",
                 "pt0_0", "pt0_1", "pt0_2", "pt0_3", "pv0", "kb0", "kb1", "kb2", "kb3",
                 "pt1_0", "pt1_1", "pt1_2", "pt1_3", "pv1", "vb0", "vb1", "vb2", "vb3",
                 "pt2_0", "pt2_1", "pt2_2", "pt2_3", "pv2", "pt3_0", "pt3_1", "pt3_2", "pt3_3", "pv3"])
        JI = {name: i for i, name in enumerate(JOBS)}

        def kept_before(j, parity):
            return (j + 1) // 2 if parity == 0 else j // 2

        SCORES_AFTER = {"f": 0, "qb3": 1, "kb3": 2, "vb3": 3}

        xin = [at(32, D), at(36, D)]
        mhT = at(32, 8, 512)
        xT = [at(40, 8, CAP), at(42, 8, CAP)]
        sg, hb = at(44, 512), at(46, 512)
        hT = [at(48, 4, CAP), at(49, 4, CAP)]
        ysb = [at(50, 512), at(52, 512)]
        yg = at(54, 8, D)
        wr = at(86, 8, NR)
        brow = at(87.75, NR)
        prow = at(87.25, P)[0:80]
        lgT = at(56, 512)
        lg = at(58, NT, NR)
        gp, gm8, gi8 = at(59, NT, 8), at(59.125, NT, 8), at(59.25, NT, 8).bitcast(U32)
        em8, ei8 = at(59.375, NT, 8), at(59.5, NT, 8).bitcast(U32)
        gf, rt_dv, rt_gs = at(59.625, NT), at(59.65625, NT), at(59.6875, NT, NG)
        ef, gw, rden = at(59.75, 2, NT), at(59.78125, NT), at(59.8125, NT)
        rk, ok, rsl = at(59.84375, 2, NT), at(59.875, 2, NT), at(59.90625, 2, NT)
        geq, em, onehot = at(60, NT, E), at(60.5, NT, E), at(61, 2, NT, E)
        nover, oend, oexcl = at(63.125, E), at(63.25, E), at(63.375, E)
        ovf = at(63.5, OVR)
        cntb = at(64, NT * E // 2).bitcast(BF16).rearrange("p (t e) -> p t e", t=NT)
        cmp = at(65, E, CR - 1)
        cmp2 = at(67, OVR, E)
        picked, picked2 = at(70, 2 * NT, E), at(71, 2 * NT, E)

        XS, Y = at(16, NT, D), at(32, NT, D)
        BT, CT = at(48, 2, 512), at(52, 2, 512)
        Btok, CBT = at(56, NT, 2, P), at(60, 2, NT, P)
        MT = [at(64, 16, P), at(72, 16, P)]
        acc = [at(32, 512), at(34, 512)]
        cso = [at(36, 512), at(38, 512)]
        zt = [at(80, 512), at(82, 512)]
        xdec, prev = at(84, D), at(88, D)
        tmp = at(92, 512)
        dtx, dt2, acsT, m128 = at(96, 512), at(98, 512), at(100, 512), at(102, 512)
        CONV = [8, 9, 10, 11, 0, 1, 2, 3, 4, 5, 6, 7]
        TURNED = [0, 1, 4, 5, 6, 7, 8, 9, 10, 11]
        yT = at(16, 8, 512)
        V = at(32, NT, D)
        O = V
        QD, ATT, KTOK, ST = at(48, 4, 512), at(56, 4, 512), at(64, NT, 512), at(72, 4, 256)
        g1, g2, g3, gen, gke, gki, gkd = (at(76 + 2 * i, 512) for i in range(7))
        glrT, gkw, m64 = at(94, 512), at(90, 512), at(92, 512)
        oT = at(56, 8, 512)
        rt = [at(76, 512), at(78, 512)]
        fin_g = at(0, D)
        fin_o = at(16, NT, D)
        odec = sb("odec", [P, 4, 8])

        def norm_act(act, k, src, junk, ready=None):
            for t in range(NT):
                if ready:
                    act.wait_ge(*ready(t))
                nc.scalar.activation(junk(t), src[:, t, :], ACT.Square,
                                     accum_out=ssq[:, t:t + 1]).then_inc(sem("norm_squares"), 1)
            act.wait_ge(sem("norm_recip"), k + 1)
            nc.scalar.activation(rstd[:, 0:NT], rstd[:, 0:NT], ACT.Sqrt).then_inc(sem("norm_rstd"), 1)

        def norm_dve(dve, step, k, src, dst, dstT, gain, first=False):
            dve.wait_ge(sem("norm_squares"), NT * (k + 1))
            step(nc.vector.tensor_scalar(ssq[:, 0:NT], ssq[:, 0:NT], 1.0 / D, EPS, ALU.mult, ALU.add))
            nc.vector.reciprocal(rstd[:, 0:NT], ssq[:, 0:NT]).then_inc(sem("norm_recip"), 1)
            dve.wait_ge(sem("norm_rstd"), k + 1)
            for t in range(NT):
                nc.vector.tensor_scalar(dst[:, t, :], src[:, t, :], rstd[:, t:t + 1], None,
                                        ALU.mult).then_inc(sem("norm_rows"), 1)
            if dstT is None:
                return
            if first:
                dve.wait_ge(sem("gains_loaded"), 64)
            for i in range(2 * NT):
                t, g = i // 2, i % 2
                dve.wait_ge(sem("norm_turned"), 8 * k + i + 1)
                nc.vector.tensor_tensor(dstT[:, 4 * g:4 * g + 4, t * P:t * P + P],
                                        B[i % 2][:, :].rearrange("p (c n) -> p c n", c=4),
                                        bc_in(gain[:, 4 * g:4 * g + 4], P),
                                        ALU.mult).then_inc(sem("norm_kept"), 1)
            dve.wait_ge(sem("norm_kept"), 8 * k + 8)

        def norm_pe(pe, k, rows, strided):
            for i in range(2 * NT):
                t, g = i // 2, i % 2
                pe.wait_ge(sem("norm_rows"), NT * k + t + 1)
                if i >= 2:
                    pe.wait_ge(sem("norm_kept"), 8 * k + i - 1)
                for j in range(4):
                    c = 4 * g + j
                    if strided:
                        src = rows[:, t, :].rearrange("p (q c) -> p c q", c=KC)[:, c, :]
                    else:
                        src = rows[:, t, c * P:c * P + P]
                    last = nc.tensor.transpose(B[i % 2][:, j * P:j * P + P], src, ident[:, :])
                last.then_inc(sem("norm_turned"), 1)
            pe.wait_ge(sem("norm_kept"), 8 * k + 8)

        def project_T(dst, w, col, m):
            for c in range(KC):
                last = nc.tensor.matmul(dst, w[:, c, col:col + m], hnT[:, c, :], start=c == 0, stop=c == KC - 1)
            return last

        def project(dst, t, w, col, n):
            for c in range(KC):
                last = nc.tensor.matmul(dst, hnT[:, c, t * P:t * P + P], w[:, c, col:col + n],
                                        start=c == 0, stop=c == KC - 1)
            return last

        @block.sync
        def _(sp):
            w_ev = even_w_in[0].rearrange("(p c) n -> p c n", c=8)
            w_od = odd_w_in[0].rearrange("(p c) n -> p c n", c=8)
            wo_ev = even_w_out[0].rearrange("(c p) n -> p c n", p=P)
            wo_od = odd_w_out[0].rearrange("(k c p) n -> k p c n", k=2, p=P)
            ev_cols = [(0, 512), (512, 256), (768, 512), (1280, 512), (1792, 512)]
            od_cols = [2048, 1024, 1536, 0, 512, 2576, 3088, 3600, 4112]

            last_use = {EV_IN: ("job_done", JI["qa3"] + 1), EV_IN + 1: ("job_done", JI["va"] + 1),
                        EV_IN + 2: ("job_done", JI["qb3"] + 1), EV_IN + 3: ("job_done", JI["kb3"] + 1),
                        EV_IN + 4: ("job_done", JI["vb3"] + 1), EV_OUT: ("out_products", 4),
                        EV_OUT + 1: ("out_products", 8),
                        OD_BC: ("conv_products", 4), OD_XS: ("conv_products", 8), OD_XS + 1: ("conv_products", 12),
                        OD_Z: ("z_products", 7), OD_Z + 1: ("z_products", 8),
                        OD_Q: ("qk_products", 7), OD_K: ("qk_products", 8),
                        OD_V: ("v_products", 4), OD_V + 1: ("v_products", 8),
                        OD_R: ("r_products", 4), OD_R + 1: ("r_products", 8)}
            last_use.update({OD_OUT[kg] + half: ("out_products", 8 + 8 * kg + 4 * (half + 1))
                             for kg in range(2) for half in range(2)})

            def freed(n):
                if n in last_use:
                    name, count = last_use[n]
                    sp.wait_ge(sem(name), count)
                elif n >= 0:
                    L = 0 if n < OD else 1
                    e, j = divmod(n - MOE[L], 3)
                    sp.wait_ge(sem("down_used") if j == 2 else sem("gate_up_used"), E * L + e + 1)

            def load(n, src, cols=512):
                freed(n - RING)
                sp.dma_start(unit(n)[:, :, 0:cols], src).then_inc(unit_loaded[n % RING], 16)

            for t in range(NT):
                sp.dma_start(h[:, t, :], x[0, t * P:t * P + P, :]).then_inc(x_loaded[t], 16)
            for dst, src in ((gmix, norm_mix), (gmoe, norm_moe)):
                for layer in range(2):
                    sp.dma_start(dst[:, layer, :], src[layer].rearrange("(p c) -> p c", c=8)).then_inc(
                        sem("gains_loaded"), 16)
            for i, (c0, n) in enumerate(ev_cols):
                load(EV_IN + i, w_ev[:, :, c0:c0 + n], n)
            load(EV_OUT, wo_ev[:, :, 0:512])
            sp.wait_ge(sem("params"), 16 * NPARAMS)
            sp.wait_ge(sem("zero_row"), 1)
            sp.dma_start(xrows.rearrange("(n p) d -> p n d", p=P),
                         zrow.unsqueeze(1).to_broadcast([P, XROWS // P, D])).then_inc(sem("rows_zeroed"), 16)
            sp.dma_start(yrows[E * CAP:, :].rearrange("(n p) d -> p n d", p=P),
                         zrow.unsqueeze(1).to_broadcast([P, OVR * CAP // P, D])).then_inc(sem("rows_zeroed"), 16)
            load(EV_OUT + 1, wo_ev[:, :, 512:1024])

            def expert(L, i, u, first):
                e = 2 * i + u
                base = MOE[L] + 3 * u
                for j, w in enumerate((moe_w_gate, moe_w_up, moe_w_down)):
                    n = base + j
                    if first:
                        freed(n - RING)
                    else:
                        sp.wait_ge(sem("down_used") if j == 2 else sem("gate_up_used"), E * L + e - 1)
                    if j == 2:
                        src = w[L, bass.ds(e, 1)].rearrange("a (p c) n -> p (a c n)", c=4)
                    else:
                        src = w[L, bass.ds(e, 1)].rearrange("a (p c) n -> p (a c n)", c=8)
                    sp.dma_start(ring[:, n % RING, :], src).then_inc(unit_loaded[n % RING], 16)

            def block_rows(L, e, u):
                sp.dma_start(xin[u][0:CAP, :], xrows[bass.ds(e * CAP, CAP), :]).then_inc(sem(f"block{u}_loaded"), 16)

            def moe(L):
                expert(L, 0, 0, True)
                expert(L, 0, 1, True)
                if L == 1:
                    sp.wait_ge(sem("o_scaled"), 16)
                    for c0, c1, w, bias in ((0, NG, moe_w_group, moe_b_group), (NG, NR, moe_w_router, moe_b_router)):
                        sp.dma_start(wr[:, :, c0:c1], w[1].rearrange("(p c) n -> p c n", c=8),
                                     allow_slow_non_contiguous=True).then_inc(sem("router_loaded"), 16)
                        sp.dma_start(brow[:, c0:c1], bias[1:2, :].to_broadcast([P, c1 - c0])).then_inc(
                            sem("router_loaded"), 16)
                sp.wait_ge(sem(f"scattered{L}"), 16 * 2 * NT)
                block_rows(L, 0, 0)
                block_rows(L, 1, 1)
                with sp.Fori(1, E // 2) as i:
                    for u in range(2):
                        sp.wait_ge(sem("x_turned"), E * L + 2 * i + u - 1)
                        block_rows(L, 2 * i + u, u)
                        expert(L, i, u, False)
                sp.wait_ge(sem("routed"), L + 1)
                n_over = sp.value_load(ovtab[0:1, OVR:OVR + 1], min_val=0, max_val=MAXOV)
                with sp.If(n_over > 0):
                    sp.wait_ge(sem("down_used"), E * (L + 1))
                    with sp.Fori(0, n_over) as b:
                        e = sp.value_load(ovtab[0:1, bass.ds(b, 1)], min_val=0, max_val=E - 1)
                        sp.dma_start(xin[0][0:CAP, :], xrows[bass.ds(E * CAP + b * CAP, CAP), :]).then_inc(
                            sem(f"over{L}_rows"), 16)
                        for j, w in enumerate((moe_w_gate, moe_w_up, moe_w_down)):
                            src = w[L, bass.ds(e, 1)].rearrange("a (p c) n -> p (a c n)", c=4 if j == 2 else 8)
                            sp.dma_start(ring[:, (MOE[L] + j) % RING, :], src).then_inc(sem(f"over{L}_weights"), 16)
                        sp.wait_ge(sem(f"over{L}_stored"), 32 * b + 32)
                        sp.sem_inc(sem("sp_passed"), 1)

            moe(0)
            for i, c0 in enumerate(od_cols):
                load(OD + i, w_od[:, :, c0:c0 + 512])
                if i == 0:
                    for t in range(NT):
                        sp.wait_ge(sem(f"gathered{t}"), 32)
            for kg in range(2):
                if kg == 1:
                    for half in range(2):
                        load(OD_R + half, w_od[:, :, 4640 + half * 512:5152 + half * 512])
                for half in range(2):
                    load(OD_OUT[kg] + half, wo_od[kg, :, :, half * 512:half * 512 + 512])
            moe(1)
            for t in range(NT):
                sp.wait_ge(sem("final_rows"), t + 1)
                sp.dma_start(out[0, t * P:t * P + P, :], fin_o[:, t, :]).then_inc(sem("out_stored"), 16)
            sp.wait_ge(sem("out_stored"), 16 * NT)

        @block.gpsimd
        def _(pool):
            g = nc.gpsimd
            step = Steps(pool, sem("pool_steps"))
            step(g.memset(ident[:, :], 0.0))
            step(g.affine_select(out=ident[:, :], in_=ident[:, :], compare_op=ALU.not_equal, fill=1.0, base=0,
                                 pattern=[[-1, P]], channel_multiplier=1))
            g.memset(zrow, 0.0).then_inc(sem("zero_row"), 1)
            step(g.memset(wdg[:, :, 16:32], 0.0))
            step(g.memset(qpad, 0.0))
            step(g.memset(qb[64:128], 0.0))
            step(g.memset(qb[64:66], 1.0))
            for m in (tri, upper, ones_b, gmask, ones_f):
                step(g.memset(m[:, :], 1.0))
            step(g.memset(cmask[:, :], 0.0))
            step(g.affine_select(out=tri[:, :], in_=tri[:, :], compare_op=ALU.is_ge, fill=0.0, base=0,
                                 pattern=[[1, P]], channel_multiplier=-1))
            step(g.affine_select(out=gmask[:, :], in_=gmask[:, :], compare_op=ALU.is_ge, fill=0.0, base=0,
                                 pattern=[[1, P]], channel_multiplier=-1))
            step(g.memset(gmask[0:64, 64:128], 0.0))
            step(g.affine_select(out=upper[:, :], in_=upper[:, :], compare_op=ALU.is_gt, fill=0.0, base=0,
                                 pattern=[[1, P]], channel_multiplier=-1))
            step(g.affine_select(out=cmask[:, :], in_=cmask[:, :], compare_op=ALU.is_ge, fill=-BIG, base=0,
                                 pattern=[[-1, P]], channel_multiplier=1))
            step(g.iota(dist[:, :], [[-1, 256]], base=P, channel_multiplier=1, allow_small_or_imprecise_dtypes=True))
            step(g.affine_select(out=dist[:, :], in_=dist[:, :], compare_op=ALU.is_ge, fill=BIG, base=P,
                                 pattern=[[-1, 256]], channel_multiplier=1))
            step(g.affine_select(out=dist[:, :], in_=dist[:, :], compare_op=ALU.is_ge, fill=BIG, base=-1,
                                 pattern=[[1, 256]], channel_multiplier=-1))
            step(g.iota(it32[:, :], [[1, E]], base=0, channel_multiplier=0, allow_small_or_imprecise_dtypes=True))
            step(g.iota(gid32[:, :].rearrange("p (g e) -> p g e", g=NG), [[1, NG], [0, EPG]], base=0,
                        channel_multiplier=0, allow_small_or_imprecise_dtypes=True))
            g.iota(thr[:, :], [[CAP, CR]], base=CAP, channel_multiplier=0,
                   allow_small_or_imprecise_dtypes=True).then_inc(sem("constants"), 1)
            pool.wait_ge(sem("norm_turned"), 8)
            step(g.memset(kb[64:128], 0.0))
            g.memset(kb[64:66], 1.0).then_inc(sem("k_padded"), 1)
            pool.wait_ge(sem("k_padded"), 1)
            pool.wait_ge(sem("gate_sums"), 1)
            for hh in range(HQ):
                pool.dma_start(qb[65:66, hh, :], c8[hh:hh + 1, :]).then_inc(sem("gate_rows"), 16)
                pool.dma_start(kb[64:65, hh, :], cn8[hh:hh + 1, :]).then_inc(sem("gate_rows"), 16)

            pool.wait_ge(sem("b_turned"), 4 * HQ)
            pool.dma_start(h[:, :, :], x[0].rearrange("(t p) d -> p t d", p=P)).then_inc(
                sem("residual_loaded"), 16)

            def moe(L):
                pool.wait_ge(sem("slots_ready"), L + 1)
                if L == 0:
                    pool.wait_ge(sem("rows_zeroed"), 32)
                for i in range(2 * NT):
                    g.indirect_dma_start(out=xrows, out_offset=bass.IndirectOffsetOnAxis(ap=slots[:, i:i + 1], axis=0),
                                         in_=xs[:, i // 2, :], in_offset=None).then_inc(sem(f"scattered{L}"), 16)
                pool.wait_ge(sem("routed"), L + 1)
                n_over = pool.value_load(ovtab[0:1, OVR:OVR + 1], min_val=0, max_val=MAXOV)
                with pool.If(n_over > 0):
                    pool.wait_ge(sem(f"over{L}_stored"), 32 * n_over)
                    pool.sem_inc(sem("pool_passed"), 1)
                for u in range(2):
                    pool.wait_ge(sem(f"y{u}_stored"), 32 * (E // 2) * (L + 1))
                for i in range(2 * NT):
                    g.indirect_dma_start(out=yg[:, i, :], out_offset=None, in_=yrows,
                                         in_offset=bass.IndirectOffsetOnAxis(ap=slots[:, i:i + 1], axis=0)).then_inc(
                        sem(f"gathered{i // 2}"), 16)

            moe(0)
            pool.wait_ge(sem("h_saved"), 16)
            pool.wait_ge(sem("norm_rows"), 8)
            step(g.memset(m128, 1.0))
            g.memset(m128.rearrange("p (c n) -> p c n", c=NT)[:, :, 0:1], 0.0).then_inc(sem("scan_mask"), 1)
            pool.wait_ge(sem("scan_mask"), 1)
            for q in range(4 * NT):
                c, qq = divmod(q, 4)
                pool.wait_ge(sem("seg_exp"), q + 1)
                if q == 0:
                    pool.wait_ge(sem("cb_kept"), 2)
                g.tensor_tensor(MT[c % 2][:, 4 * qq:4 * qq + 4, :], MT[c % 2][:, 4 * qq:4 * qq + 4, :],
                                bc_out(CBT[:, qq // 2, c, :], 4), ALU.mult).then_inc(sem("mt_ready"), 1)
            pool.wait_ge(sem("ydiag"), NT)
            pool.dma_start(gkw[0:16, :], odd_gk_w[0]).then_inc(sem("gk_loaded"), 16)
            pool.wait_ge(sem("norm_turned"), 24)
            step(g.memset(m64, 1.0))
            step(g.memset(ATT, 0.0))
            g.memset(m64.rearrange("p (c n) -> p c n", c=8)[:, :, 0:1], 0.0).then_inc(sem("scan_mask"), 1)
            pool.wait_ge(sem("scan_mask"), 2)
            pool.wait_ge(sem("scores_kept"), 4)
            pool.wait_ge(sem("k_turned_kept"), 4)
            pool.dma_start(h[:, :, :], hsave.rearrange("(t p) d -> p t d", p=P)).then_inc(
                sem("residual_loaded2"), 16)
            moe(1)
            pool.dma_start(fin_g, norm_final.rearrange("(a n) -> a n", a=1).to_broadcast([P, D])).then_inc(
                sem("final_gain"), 16)

        def even_keep(name, bank, copy, done):
            if name[:2] == "qa":
                m = int(name[2])
                kv = 64 * (m // 2)
                copy(qpad[kv:kv + 64, 2 * m, :], bank[0:64, :])
                copy(qpad[kv:kv + 64, 2 * m + 1, :], bank[64:128, :]).then_inc(done, 1)
            elif name == "ka":
                copy(kaT, bank[:, :]).then_inc(done, 1)
            elif name == "va":
                copy(va, bank[:, :].rearrange("p (t n) -> p t n", t=NT)).then_inc(done, 1)
            elif name[:2] in ("qb", "kb"):
                m, dst = int(name[2]), qb if name[0] == "q" else kb
                copy(dst[0:64, 2 * m, :], bank[0:64, :])
                copy(dst[0:64, 2 * m + 1, :], bank[64:128, :]).then_inc(done, 1)
            elif name[:2] == "vb":
                copy(vb[:, int(name[2]), :], bank[:, :]).then_inc(done, 1)
            elif name[:2] == "pt":
                n, m = int(name[2]), int(name[4])
                a = 1 if n == 0 else 0
                copy(PTA[:, 2 * m:2 * m + 2, a:2, :],
                     bank[:, :].rearrange("p (h a q) -> p h a q", h=2, a=2)[:, :, a:2, :]).then_inc(done, 1)
            elif name[:2] == "pv":
                n = int(name[2])
                copy(headsA[:, :, n * P:n * P + P], bank[:, :].rearrange("p (m q) -> p m q", m=4)).then_inc(done, 1)

        @block.scalar
        def _(act):
            s = nc.scalar
            step = Steps(act, sem("act_steps"))
            copy = lambda o, i: s.activation(o, i, ACT.Copy)
            loads = [
                (wf[:, :, :], even_w_in[0].rearrange("(p c) n -> p c n", c=8)[:, :, 2304:2312]),
                (fbias[:, :], even_forget_bias[0].rearrange("(p c) -> p c", c=1)),
                (sink8[:, :], even_sinks[0:1, :].to_broadcast([P, HQ])),
                (prow[CONVW:CONVW + 48, :], odd_conv_w[0].rearrange("j (c p) -> (j c) p", p=P)),
                (prow[CONVB:CONVB + 12, :], odd_conv_b[0].rearrange("(c p) -> c p", p=P)),
                (prow[GKB:GKB + 4, :], odd_gk_b[0].rearrange("(c p) -> c p", p=P)),
                (prow[SSDN:SSDN + 8, :], odd_ssd_norm[0].rearrange("(c p) -> c p", p=P)),
                (prow[GLAN:GLAN + 2, :], odd_gla_norm[0].rearrange("(c p) -> c p", p=P)),
                (wdg[:, :, 0:16], odd_w_in[0].rearrange("(p c) n -> p c n", c=8)[:, :, 2560:2576]),
                (wdg[:, :, 32:48], odd_w_in[0].rearrange("(p c) n -> p c n", c=8)[:, :, 4624:4640]),
                (brow[:, 0:NG], moe_b_group[0:1, :].to_broadcast([P, NG])),
                (brow[:, NG:NR], moe_b_router[0:1, :].to_broadcast([P, E])),
                (dskip[:, :], odd_d_skip[0:1, :].to_broadcast([P, 16])),
                (dtb[:, :], odd_dt_bias[0].rearrange("(p c) -> p c", c=1)),
                (acol[:, :], odd_a_log[0].rearrange("(p c) -> p c", c=1)),
                (wr[:, :, 0:NG], moe_w_group[0].rearrange("(p c) n -> p c n", c=8)),
                (wr[:, :, NG:NR], moe_w_router[0].rearrange("(p c) n -> p c n", c=8)),
            ]
            assert len(loads) == NPARAMS
            norm_act(act, 0, h, lambda t: e_xs[:, t, :], lambda t: (x_loaded[t], 16))
            for dst, src in loads:
                act.dma_start(dst, src, allow_slow_non_contiguous=True).then_inc(sem("params"), 16)

            def keep(j):
                act.wait_ge(sem("job_done"), j + 1)
                if JOBS[j] == "f":
                    act.wait_ge(sem("params"), 16 * NPARAMS)
                    s.activation(fx[0:8], B[j % 4][0:8, :], ACT.Identity,
                                 bias=fbias[:, 0:1]).then_inc(sem("job_kept_act"), 1)
                    act.wait_ge(sem("job_kept_act"), j // 2 + 1)
                    step(s.activation(fe[0:8], fx[0:8], ACT.Abs))
                    step(s.activation(fe[0:8], fe[0:8], ACT.Exp, scale=-1.0))
                    s.activation(fe[0:8], fe[0:8], ACT.Ln, bias=1.0).then_inc(sem("gate_log"), 1)
                    return
                if JOBS[j] == "vb0" or JOBS[j] == "vb1":
                    act.wait_ge(sem("rows_zeroed"), 32)
                even_keep(JOBS[j], B[j % 4], copy, sem("job_kept_act"))

            def window_exp(n):
                k0 = P if n == 0 else 0
                act.wait_ge(sem("a_max"), n + 1)
                for hh in range(HQ):
                    s.activation(SA[:, hh, k0:256], SA[:, hh, k0:256], ACT.Exp,
                                 bias=stat[:, hh // 4, hh % 4:hh % 4 + 1], scale=0.125,
                                 accum_out=ssq[:, hh:hh + 1]).then_inc(sem("a_exp"), 1)
                s.activation(stat[:, 2:4, :], stat[:, 2:4, :], ACT.Exp).then_inc(sem("a_exp"), 1)

            for j, name in enumerate(JOBS):
                if j % 2 == 0:
                    keep(j)
                if name in SCORES_AFTER:
                    window_exp(SCORES_AFTER[name])
            for i in range(4 * HQ + 4):
                if i < 4 * HQ:
                    n = i % 4
                    act.wait_ge(sem("b_negmax"), i + 1)
                    if i >= 4:
                        act.wait_ge(sem("b_turned"), i - 3)
                    s.activation(PB[:, i % 4, 0:(n + 1) * P], B[2 + i % 4][:, 0:(n + 1) * P], ACT.Exp,
                                 bias=stat[:, 0, i % 4:i % 4 + 1], scale=0.125,
                                 accum_out=ssq[:, i % 4:i % 4 + 1]).then_inc(sem("b_exp"), 1)
                if i >= 4:
                    j = i - 4
                    hh, n = divmod(j, 4)
                    act.wait_ge(sem("b_turned"), j + 1)
                    if n == 0 and hh >= 2:
                        act.wait_ge(sem("b_values"), hh - 1)
                    s.activation(PTB[:, hh % 2, 0:n + 1, n * P:n * P + P],
                                 B[6 + j % 2][:, 0:(n + 1) * P].rearrange("p (c n) -> p c n", c=n + 1),
                                 ACT.Copy).then_inc(sem("b_tkept"), 1)

            def moe(L):
                for t in range(NT):
                    act.wait_ge(sem("mixer_added"), (0, 16)[L] + NT + t + 1)
                    s.activation(xs[:, t, :], h[:, t, :], ACT.Square,
                                 accum_out=ssq[:, t:t + 1]).then_inc(sem("moe_squares"), 1)
                act.wait_ge(sem("moe_recip"), L + 1)
                s.activation(rstd[:, 0:NT], rstd[:, 0:NT], ACT.Sqrt).then_inc(sem("moe_rstd"), 1)
                act.wait_ge(sem("logits"), L + 1)
                s.activation(lgT[0:NR, :], B[2][0:NR, :], ACT.Copy).then_inc(sem("logits_kept"), 1)
                act.wait_ge(sem("route_args"), L + 1)
                step(s.activation(rt_gs, rt_gs, ACT.Exp))
                s.activation(rt_dv, rt_dv, ACT.Exp).then_inc(sem("route_exps"), 1)

                def silu(i, u):
                    act.wait_ge(sem("gate_up_used"), E * L + 2 * i + u + 1)
                    s.activation(sg[64:128, :], B[0][0:64, :], ACT.Silu).then_inc(sem("gated"), 1)

                def y_store(i, u):
                    act.wait_ge(sem("down_used"), E * L + 2 * i + u + 1)
                    s.activation(ysb[u], B[4 + u][:, :], ACT.Copy).then_inc(sem("y_kept"), 1)
                    act.wait_ge(sem("y_kept"), E * L + 2 * i + u + 1)
                    for a in range(2):
                        act.dma_start(yrows[bass.ds((2 * i + u) * CAP, CAP), a * 512:a * 512 + 512],
                                      ysb[u][64 * a:64 * a + 64, :]).then_inc(sem(f"y{u}_stored"), 16)

                silu(0, 0)
                silu(0, 1)
                y_store(0, 0)
                with act.Fori(1, E // 2) as i:
                    silu(i, 0)
                    y_store(i - 1, 1)
                    silu(i, 1)
                    act.wait_ge(sem("y0_stored"), 32 * ((E // 2) * L + i))
                    y_store(i, 0)
                    act.wait_ge(sem("y1_stored"), 32 * ((E // 2) * L + i))
                y_store(E // 2 - 1, 1)

                act.wait_ge(sem("routed"), L + 1)
                n_over = act.value_load(ovtab[0:1, OVR:OVR + 1], min_val=0, max_val=MAXOV)
                with act.If(n_over > 0):
                    with act.Fori(0, n_over) as b:
                        act.wait_ge(sem(f"over{L}_steps"), OVS * b + 3)
                        s.activation(sg[64:128, :], B[0][0:64, :], ACT.Silu).then_inc(sem(f"over{L}_steps"), 1)
                        act.wait_ge(sem(f"over{L}_steps"), OVS * b + 8)
                        act.wait_ge(sem("y0_stored"), 32 * (E // 2) * (L + 1))
                        s.activation(ysb[0], B[4][:, :], ACT.Copy).then_inc(sem(f"over{L}_steps"), 1)
                        act.wait_ge(sem(f"over{L}_steps"), OVS * b + 9)
                        for a in range(2):
                            act.dma_start(yrows[bass.ds(E * CAP + b * CAP, CAP), a * 512:a * 512 + 512],
                                          ysb[0][64 * a:64 * a + 64, :]).then_inc(sem(f"over{L}_stored"), 16)

            moe(0)

            norm_act(act, 1, h, lambda t: xs[:, t, :], lambda t: (sem("combined"), t + 1))
            act.dma_start(hsave.rearrange("(t p) d -> p t d", p=P), h[:, :, :]).then_inc(sem("h_saved"), 16)
            act.wait_ge(sem("pcol_turned"), 1)
            s.activation(pcol[:, 0:74], B[7][:, 0:74], ACT.Copy).then_inc(sem("pcol_kept"), 1)
            act.wait_ge(sem("pcol_kept"), 1)
            act.wait_ge(sem("dt_products"), 1)
            act.wait_ge(sem("h_saved"), 16)
            step(s.activation(dtx[0:16], B[4][0:16, :], ACT.Identity, bias=dtb[:, 0:1]))
            step(s.activation(dt2[0:16], dtx[0:16], ACT.Abs))
            step(s.activation(dt2[0:16], dt2[0:16], ACT.Exp, scale=-1.0))
            step(s.activation(dt2[0:16], dt2[0:16], ACT.Ln, bias=1.0))
            s.activation(acol[:, :], acol[:, :], ACT.Exp).then_inc(sem("dt_log"), 1)
            s.activation(glrT[0:16], B[4][32:48, :], ACT.Copy).then_inc(sem("rank_kept"), 1)

            def spread(c):
                act.dma_start(MT[c % 2], sums_d[:, c * P:c * P + P].unsqueeze(0).to_broadcast([P, 16, P])).then_inc(
                    sem(f"spread{c % 2}"), 16)

            for j in range(CH):
                if j == 1:
                    act.wait_ge(sem("decays"), 1)
                    act.dma_start(sums_d, acsT[0:16]).then_inc(sem("sums_saved"), 16)
                if j == 4:
                    act.wait_ge(sem("sums_saved"), 16)
                    spread(0)
                    spread(1)
                ch = CONV[j]
                act.wait_ge(sem("conv_products"), j + 1)
                s.activation(acc[j % 2], B[j % 2][:, :], ACT.Identity, bias=pcol[:, CONVB + ch:CONVB + ch + 1],
                             scale=pcol[:, CONVW + 36 + ch:CONVW + 37 + ch]).then_inc(sem("conv_first"), 1)
                act.wait_ge(sem("conv_summed"), j + 1)
                if j < 2:
                    dst = BT[:, j, :]
                elif j < 4:
                    dst = CT[:, j - 2, :]
                else:
                    dst = cso[j % 2]
                    if j >= 6:
                        act.wait_ge(sem("conv_turned"), j - 3)
                s.activation(dst, acc[j % 2], ACT.Silu).then_inc(sem("conv_out"), 1)
            for c in range(NT):
                for qq in range(4):
                    q = 4 * c + qq
                    act.wait_ge(sem("seg_args"), q + 1)
                    part = MT[c % 2][:, 4 * qq:4 * qq + 4, :]
                    s.activation(part, part, ACT.Exp).then_inc(sem("seg_exp"), 1)
                act.wait_ge(sem("chunk_args"), c + 1)
                step(s.activation(endb[:, 2, :], endb[:, 2, :], ACT.Exp))
                step(s.activation(endb[:, 0, :], endb[:, 0, :], ACT.Exp))
                s.activation(endb[:, 1, :], datok[:, c, 1, :], ACT.Exp).then_inc(sem("chunk_exps"), 1)
                for half in range(2):
                    i = 2 * c + half
                    act.wait_ge(sem("z_products"), i + 1)
                    if i >= 2:
                        act.wait_ge(sem("z_used"), i - 1)
                    s.activation(zt[half], B[4 + half][:, :], ACT.Silu).then_inc(sem("z_gate"), 1)
                if 1 <= c < NT - 1:
                    act.wait_ge(sem("ydiag"), c)
                    spread(c + 1)
            act.wait_ge(sem("ydiag"), NT)
            act.wait_ge(sem("z_used"), 8)
            norm_act(act, 2, Y, lambda t: at(16, NT, D)[:, t, :])
            for d in range(4):
                act.wait_ge(sem("gate_products"), d + 1)
                if d:
                    act.wait_ge(sem("gate_keys"), d)
                step(s.activation(g1, B[4 + d % 2][:, :], ACT.Identity, bias=pcol[:, GKB + d:GKB + d + 1]))
                step(s.activation(g2, g1, ACT.Abs))
                step(s.activation(g2, g2, ACT.Exp, scale=-1.0))
                s.activation(g2, g2, ACT.Ln, bias=1.0).then_inc(sem("gla_log"), 1)
                act.wait_ge(sem("gla_sums"), d + 1)
                step(s.activation(g2, g3, ACT.Exp, scale=1.0 / 16))
                step(s.activation(gen, g3, ACT.Exp, scale=-1.0 / 16))
                s.activation(gke, g1, ACT.Exp, scale=1.0 / 16).then_inc(sem("gla_exps"), 1)
            for i in range(0, 8, 2):
                act.wait_ge(sem("v_products"), i + 1)
                half, t = divmod(i, NT)
                copy(V[:, t, half * 512:half * 512 + 512], B[4 + i % 4][:, :]).then_inc(sem("v_kept_act"), 1)
            for t in range(NT):
                act.wait_ge(sem("o_products"), t + 1)
                act.wait_ge(sem("gla_states"), min(2 * t + 2, 7))
                for d in range(4):
                    src = B[2 * (t % 2) + d // 2][:, (d % 2) * 256:(d % 2) * 256 + 256]
                    if t or d:
                        act.wait_ge(sem("o_squares"), 4 * t + d)
                    s.activation(rt[0][:, 0:256], src, ACT.Square,
                                 accum_out=ssq[:, 4 * t + d:4 * t + d + 1]).then_inc(sem("o_squares"), 1)
                for a in range(2):
                    copy(O[:, t, a * 512:a * 512 + 512], B[2 * (t % 2) + a][:, :]).then_inc(sem("o_kept"), 1)
            act.wait_ge(sem("o_recip"), 1)
            s.activation(rstd[:, :], rstd[:, :], ACT.Sqrt).then_inc(sem("o_rstd"), 1)
            act.wait_ge(sem("o_squares"), 16)
            for i in range(8):
                act.wait_ge(sem("r_products"), i + 1)
                if i >= 2:
                    act.wait_ge(sem("o_scaled"), 2 * (i - 1))
                s.activation(rt[i % 2], B[4 + i % 4][:, :], ACT.Silu).then_inc(sem("r_gate"), 1)

            moe(1)
            norm_act(act, 3, h, lambda t: fin_o[:, t, :], lambda t: (sem("combined"), NT + t + 1))

        @block.vector
        def _(dve):
            v = nc.vector
            step = Steps(dve, sem("dve_steps"))
            copy = v.tensor_copy

            norm_dve(dve, step, 0, h, e_xs, hnT, gmix[:, 0, :], first=True)

            def keep(j):
                dve.wait_ge(sem("job_done"), j + 1)
                if JOBS[j] in ("vb0", "vb1"):
                    dve.wait_ge(sem("rows_zeroed"), 32)
                if JOBS[j] == "pv0":
                    dve.wait_ge(sem("gate_rows"), 16 * 2 * HQ)
                even_keep(JOBS[j], B[j % 4], copy, sem("job_kept_dve"))

            def gate_sums():
                dve.wait_ge(sem("gate_log"), 1)
                step(v.scalar_tensor_tensor(out=fx[0:8], in0=fx[0:8], scalar=0.0, in1=fe[0:8],
                                            op0=ALU.min, op1=ALU.subtract))
                step(v.tensor_tensor_scan(cT[0:8], ones_f[0:8, 0:1].to_broadcast([8, 512]), fx[0:8], 0.0,
                                          ALU.mult, ALU.add))
                step(v.tensor_scalar(c8[0:8], cT[0:8], 8.0, None, ALU.mult))
                v.tensor_scalar(cn8[0:8], cT[0:8], -8.0, None, ALU.mult).then_inc(sem("gate_sums"), 1)

            def window_softmax(n):
                k0 = P if n == 0 else 0
                if n == 0:
                    dve.wait_ge(sem("params"), 16 * NPARAMS)
                    dve.wait_ge(sem("constants"), 1)
                    step(v.tensor_scalar(sink8[:, :], sink8[:, :], 8.0, None, ALU.mult))
                if n:
                    dve.wait_ge(sem("job_done"), JI[f"pt{n - 1}_3"] + 1)
                for g in range(2):
                    dve.wait_ge(sem("a_scores"), 2 * n + g + 1)
                    for hh in range(4 * g, 4 * g + 4):
                        v.scalar_tensor_tensor(out=SA[:, hh, k0:256], in0=dist[:, k0:256],
                                               scalar=-8.0 * 2.0 ** -(hh + 1),
                                               in1=B[4 + hh // 2][:, (hh % 2) * 256 + k0:(hh % 2) * 256 + 256],
                                               op0=ALU.mult, op1=ALU.add).then_inc(sem("a_biased"), 1)
                dve.wait_ge(sem("a_biased"), HQ * (n + 1))
                m8 = stat[:, 2:4, :].rearrange("p a b -> p (a b)")
                neg = stat[:, 0:2, :].rearrange("p a b -> p (a b)")
                den = stat[:, 4:6, :].rearrange("p a b -> p (a b)")
                step(v.tensor_reduce(m8, SA[:, :, k0:256], AX.X, ALU.max))
                step(v.tensor_tensor(m8, m8, sink8[:, :], ALU.max))
                step(v.tensor_scalar(neg, m8, -0.125, None, ALU.mult))
                v.scalar_tensor_tensor(out=m8, in0=sink8[:, :], scalar=0.125, in1=neg, op0=ALU.mult,
                                       op1=ALU.add).then_inc(sem("a_max"), 1)
                dve.wait_ge(sem("a_exp"), (HQ + 1) * (n + 1))
                step(v.tensor_tensor(den, ssq[:, 0:HQ], m8, ALU.add))
                step(v.reciprocal(den, den))
                v.tensor_tensor(SA[:, :, k0:256], SA[:, :, k0:256], bc_in(den, 256 - k0),
                                ALU.mult).then_inc(sem("a_probs"), 1)

            for j, name in enumerate(JOBS):
                if j % 2 == 1:
                    keep(j)
                if name == "f":
                    gate_sums()
                if name in SCORES_AFTER:
                    window_softmax(SCORES_AFTER[name])
            dve.wait_ge(sem("a_probs"), 4)
            for i in range(4 * HQ + 2):
                if i < 4 * HQ:
                    n, bank = i % 4, B[2 + i % 4]
                    dve.wait_ge(sem("b_scores"), i + 1)
                    step(v.tensor_tensor(bank[:, n * P:n * P + P], bank[:, n * P:n * P + P], cmask[:, :], ALU.add))
                    step(v.tensor_reduce(stat[:, 1, i % 4:i % 4 + 1], bank[:, 0:(n + 1) * P], AX.X, ALU.max))
                    v.tensor_scalar(stat[:, 0, i % 4:i % 4 + 1], stat[:, 1, i % 4:i % 4 + 1], -0.125, None,
                                    ALU.mult).then_inc(sem("b_negmax"), 1)
                if 1 <= i <= 4 * HQ:
                    j = i - 1
                    n = j % 4
                    dve.wait_ge(sem("b_exp"), j + 1)
                    step(v.reciprocal(stat[:, 2, j % 4:j % 4 + 1], ssq[:, j % 4:j % 4 + 1]))
                    v.tensor_scalar(PB[:, j % 4, 0:(n + 1) * P], PB[:, j % 4, 0:(n + 1) * P],
                                    stat[:, 2, j % 4:j % 4 + 1], None, ALU.mult).then_inc(sem("b_probs"), 1)
                if i >= 9 and (i - 9) % 8 == 4 or i == 4 * HQ + 1:
                    pair = (i - 9 - 4) // 8 if i <= 4 * HQ else HQ // 2 - 1
                    dve.wait_ge(sem("b_values"), 2 * pair + 2)
                    copy(headsB[:, pair, :], B[pair % 2][:, :]).then_inc(sem("b_heads"), 1)

            def add_out(count, j, bank):
                half, t = divmod(j, NT)
                dve.wait_ge(sem("out_products"), count)
                dst = h[:, t, half * 512:half * 512 + 512]
                v.tensor_tensor(dst, dst, bank[:, :], ALU.add).then_inc(sem("mixer_added"), 1)

            def keep_tile(L, t):
                for g in range(2):
                    dve.wait_ge(sem("moe_turned"), 8 * L + 2 * t + g + 1)
                    v.tensor_tensor(mhT[:, 4 * g:4 * g + 4, t * P:t * P + P],
                                    B[g][:, :].rearrange("p (c n) -> p c n", c=4),
                                    bc_in(gmoe[:, L, 4 * g:4 * g + 4], P), ALU.mult).then_inc(sem("moe_kept"), 1)

            dve.wait_ge(sem("residual_loaded"), 16)
            for j in range(8):
                add_out(j + 1, j, B[2 + j % 4])
                if j > NT:
                    keep_tile(0, j - NT - 1)

            def moe(L):
                keep_tile(L, NT - 1)
                dve.wait_ge(sem("moe_squares"), NT * (L + 1))
                step(v.tensor_scalar(ssq[:, 0:NT], ssq[:, 0:NT], 1.0 / D, EPS, ALU.mult, ALU.add))
                v.reciprocal(rstd[:, 0:NT], ssq[:, 0:NT]).then_inc(sem("moe_recip"), 1)
                v.memset(gp, -BIG)
                dve.wait_ge(sem("moe_rstd"), L + 1)
                dve.wait_ge(sem("mixer_added"), (8, 24)[L])
                for t in range(NT):
                    ins = v.tensor_scalar(xs[:, t, :], h[:, t, :], rstd[:, t:t + 1], None, ALU.mult)
                step(ins)
                if L == 1:
                    dve.wait_ge(sem("router_loaded"), 64)
                dve.wait_ge(sem("logits_turned"), L + 1)
                for t in range(NT):
                    ins = v.scalar_tensor_tensor(out=lg[:, t, :], in0=B[3][:, t * NR:t * NR + NR],
                                                 scalar=rstd[:, t:t + 1], in1=brow, op0=ALU.mult, op1=ALU.add)
                step(ins)
                step(copy(gp[:, :, 0:NG], lg[:, :, 0:NG]))
                for t in range(NT):
                    ins = v.max(gm8[:, t, :], gp[:, t, :])
                step(ins)
                for t in range(NT):
                    ins = v.max_index(gi8[:, t, :], gm8[:, t, :], gp[:, t, :])
                step(ins)
                step(copy(gf, gi8[:, :, 0]))
                step(v.tensor_tensor(geq, bc_out(gid32[:, :], NT), bc_in(gf, E), ALU.is_equal))
                step(v.tensor_scalar(geq, geq, BIG, -BIG, ALU.mult, ALU.add))
                step(v.tensor_tensor(em, lg[:, :, NG:NR], geq, ALU.add))
                for t in range(NT):
                    ins = v.max(em8[:, t, :], em[:, t, :])
                step(ins)
                for t in range(NT):
                    ins = v.max_index(ei8[:, t, :], em8[:, t, :], em[:, t, :])
                step(ins)
                step(copy(ef, ei8[:, :, 0:2].rearrange("p t k -> p k t")))
                for k in range(2):
                    ins = v.tensor_tensor(onehot[:, k], bc_out(it32[:, :], NT), bc_in(ef[:, k, :], E), ALU.is_equal)
                step(ins)
                v.tensor_tensor(cntb, onehot[:, 0], onehot[:, 1], ALU.add).then_inc(sem("picks"), 1)
                v.tensor_tensor(rt_gs, lg[:, :, 0:NG], bc_in(gm8[:, :, 0], NG), ALU.subtract)
                v.tensor_tensor(rt_dv, em8[:, :, 1], em8[:, :, 0], ALU.subtract).then_inc(sem("route_args"), 1)
                dve.wait_ge(sem("ranks"), L + 1)
                step(v.tensor_tensor(cmp, bc_in(B[2][:, NT * E:NT * E + E], CR - 1), bc_out(thr[:, 0:CR - 1], E),
                                     ALU.is_gt))
                step(v.tensor_reduce(nover, cmp, AX.X, ALU.add))
                step(v.tensor_tensor_scan(oend, ones_f[:, 0:1].to_broadcast([P, E]), nover, 0.0, ALU.mult, ALU.add))
                for k in range(2):
                    v.tensor_tensor(picked[:, k * NT:k * NT + NT, :], onehot[:, k],
                                    B[2][:, 0:NT * E].rearrange("p (t e) -> p t e", t=NT), ALU.mult)
                step(v.tensor_tensor(oexcl, oend, nover, ALU.subtract))
                both = onehot.rearrange("p k t e -> p (k t) e")
                flat = lambda a: a.rearrange("p k t -> p (k t)")
                v.tensor_reduce(flat(rk), picked, AX.X, ALU.add)
                step(v.tensor_tensor(picked2, both, bc_out(oexcl, 2 * NT), ALU.mult))
                step(v.tensor_reduce(flat(ok), picked2, AX.X, ALU.add))
                v.scalar_tensor_tensor(out=ef, in0=ef, scalar=float(CAP), in1=rk, op0=ALU.mult, op1=ALU.add)
                step(v.scalar_tensor_tensor(out=ok, in0=ok, scalar=float(CAP), in1=rk, op0=ALU.mult, op1=ALU.add))
                step(v.scalar_tensor_tensor(out=ok, in0=ok, scalar=float(E * CAP - CAP), in1=ef,
                                            op0=ALU.add, op1=ALU.subtract))
                step(v.scalar_tensor_tensor(out=ok, in0=rk, scalar=float(CAP), in1=ok, op0=ALU.is_ge, op1=ALU.mult))
                step(v.tensor_tensor(rsl, ok, ef, ALU.add))
                copy(slots[:, :].rearrange("p (t k) -> p k t", k=2), rsl).then_inc(sem("slots_ready"), 1)
                step(v.tensor_tensor(cmp2[0:1], bc_out(oend[0:1, :], OVR), bc_in(it32[0:1, 0:OVR], E), ALU.is_le))
                step(v.tensor_reduce(ovf[0:1, :], cmp2[0:1], AX.X, ALU.add))
                copy(ovtab[:, 0:OVR], ovf[0:1, :])
                step(copy(ovtab[:, OVR:OVR + 1], oend[0:1, E - 1:E]))
                dve.wait_ge(sem("route_exps"), L + 1)
                v.tensor_scalar(rden, rt_dv, 1.0, None, ALU.add)
                step(v.tensor_reduce(gw, rt_gs, AX.X, ALU.add))
                v.reciprocal(gw, gw)
                step(v.reciprocal(rden, rden))
                step(v.tensor_tensor(gates[:, :, 0], gw, rden, ALU.mult))
                v.tensor_tensor(gates[:, :, 1], gates[:, :, 0], rt_dv, ALU.mult).then_inc(sem("routed"), 1)

                def x_kept(i, u):
                    dve.wait_ge(sem("x_turned"), E * L + 2 * i + u + 1)
                    v.tensor_tensor(xT[u], B[2][:, :].rearrange("p (c n) -> p c n", c=8),
                                    bc_in(gmoe[:, L, :], CAP), ALU.mult).then_inc(sem("x_kept"), 1)

                def hidden(i, u):
                    dve.wait_ge(sem("gated"), E * L + 2 * i + u + 1)
                    v.tensor_tensor(hb[64:128, :], sg[64:128, :], B[1][64:128, :],
                                    ALU.mult).then_inc(sem("hidden"), 1)

                def h_kept(i, u):
                    dve.wait_ge(sem("h_turned"), E * L + 2 * i + u + 1)
                    copy(hT[u], B[3][:, 0:4 * CAP].rearrange("p (c n) -> p c n", c=4)).then_inc(sem("h_kept"), 1)

                x_kept(0, 0)
                hidden(0, 0)
                x_kept(0, 1)
                h_kept(0, 0)
                hidden(0, 1)
                with dve.Fori(1, E // 2) as i:
                    x_kept(i, 0)
                    h_kept(i - 1, 1)
                    hidden(i, 0)
                    x_kept(i, 1)
                    h_kept(i, 0)
                    hidden(i, 1)
                h_kept(E // 2 - 1, 1)

                n_over = dve.value_load(ovtab[0:1, OVR:OVR + 1], min_val=0, max_val=MAXOV)
                with dve.If(n_over > 0):
                    with dve.Fori(0, n_over) as b:
                        dve.wait_ge(sem(f"over{L}_steps"), OVS * b + 1)
                        v.tensor_tensor(xT[0], B[2][:, :].rearrange("p (c n) -> p c n", c=8),
                                        bc_in(gmoe[:, L, :], CAP), ALU.mult).then_inc(sem(f"over{L}_steps"), 1)
                        dve.wait_ge(sem(f"over{L}_steps"), OVS * b + 4)
                        v.tensor_tensor(hb[64:128, :], sg[64:128, :], B[1][64:128, :],
                                        ALU.mult).then_inc(sem(f"over{L}_steps"), 1)
                        dve.wait_ge(sem(f"over{L}_steps"), OVS * b + 6)
                        copy(hT[0], B[3][:, 0:4 * CAP].rearrange("p (c n) -> p c n", c=4)).then_inc(
                            sem(f"over{L}_steps"), 1)

                for t in range(NT):
                    dve.wait_ge(sem(f"gathered{t}"), 32 * (L + 1))
                    step(v.scalar_tensor_tensor(out=h[:, t, :], in0=yg[:, 2 * t, :], scalar=gates[:, t, 0:1],
                                                in1=h[:, t, :], op0=ALU.mult, op1=ALU.add))
                    v.scalar_tensor_tensor(out=h[:, t, :], in0=yg[:, 2 * t + 1, :], scalar=gates[:, t, 1:2],
                                           in1=h[:, t, :], op0=ALU.mult, op1=ALU.add).then_inc(sem("combined"), 1)
                dve.wait_ge(sem("combined"), NT * (L + 1))

            moe(0)

            norm_dve(dve, step, 1, h, xs, hnT, gmix[:, 1, :])
            dve.wait_ge(sem("pcol_kept"), 1)
            for j in range(4):
                step(copy(gla8[:, 2 * j:2 * j + 2], pcol[:, GLAN:GLAN + 2]))
            dve.wait_ge(sem("dt_log"), 1)
            dve.wait_ge(sem("scan_mask"), 1)
            step(v.tensor_scalar(acol[:, :], acol[:, :], -1.0, None, ALU.mult))
            step(v.scalar_tensor_tensor(out=dtx[0:16], in0=dtx[0:16], scalar=0.0, in1=dt2[0:16],
                                        op0=ALU.max, op1=ALU.add))
            step(v.tensor_scalar(dt2[0:16], dtx[0:16], acol[:, 0:1], None, ALU.mult))
            v.tensor_tensor_scan(acsT[0:16], m128[0:16], dt2[0:16], 0.0, ALU.mult, ALU.add).then_inc(sem("decays"), 1)
            for j in range(CH + 2):
                if j < CH:
                    ch, bank, a = CONV[j], B[j % 2], acc[j % 2]
                    dve.wait_ge(sem("conv_first"), j + 1)
                    for back in (1, 2, 3):
                        row = CONVW + 12 * (3 - back) + ch
                        ins = v.scalar_tensor_tensor(out=a[:, back:512], in0=bank[:, 0:512 - back],
                                                     scalar=pcol[:, row:row + 1], in1=a[:, back:512],
                                                     op0=ALU.mult, op1=ALU.add)
                        if back < 3:
                            step(ins)
                        else:
                            ins.then_inc(sem("conv_summed"), 1)
                if j >= 2:
                    i = TURNED.index(j - 2) if j - 2 in TURNED else None
                    if i is not None:
                        dve.wait_ge(sem("conv_turned"), i + 1)
                        src = B[2 + i % 2][:, :].rearrange("p (t n) -> p t n", t=NT)
                        dst = Btok[:, :, i, :] if i < 2 else XS[:, :, (i - 2) * P:(i - 2) * P + P]
                        copy(dst, src).then_inc(sem("conv_tkept"), 1)
            dve.wait_ge(sem("decays_turned"), 1)
            step(copy(datok[:, :, :, :], B[5][:, 0:NT * 32].rearrange("p (t w h) -> p t w h", t=NT, w=2)))
            for g in range(2):
                dve.wait_ge(sem("cb_products"), g + 1)
                v.tensor_tensor(CBT[:, g, :, :], B[6 + g][:, :].rearrange("p (c n) -> p c n", c=NT),
                                bc_out(tri[:, :], NT), ALU.mult).then_inc(sem("cb_kept"), 1)
            dve.wait_ge(sem("cb_kept"), 2)
            dve.wait_ge(sem("conv_tkept"), 10)

            def seg_args(c):
                if c:
                    dve.wait_ge(sem("chunk_exps"), c)
                    dve.wait_ge(sem("states_kept"), c)
                    dve.wait_ge(sem("y_summed"), 2 * c)
                dve.wait_ge(sem(f"spread{c % 2}"), 16 * (c // 2) + 16)
                step(copy(endb[:, 0, :], MT[c % 2][:, :, P - 1]))
                for hh in range(16):
                    ins = v.tensor_scalar(MT[c % 2][:, hh, :], MT[c % 2][:, hh, :],
                                          datok[:, c, 1, hh:hh + 1], 0.0, ALU.subtract, ALU.min)
                    if hh % 4 == 3:
                        ins.then_inc(sem("seg_args"), 1)
                v.tensor_tensor(endb[:, 2, :], endb[:, 0, :], datok[:, c, 1, :],
                                ALU.subtract).then_inc(sem("chunk_args"), 1)

            def heads_of(row):
                return row.rearrange("p (h n) -> p h n", n=64)

            for c in range(NT):
                seg_args(c)
                xc = heads_of(XS[:, c, :])
                step(v.tensor_tensor(heads_of(Y[:, c, :]), xc, bc_in(dskip[:, :], 64), ALU.mult))
                step(v.tensor_tensor(xc, xc, bc_in(datok[:, c, 0, :], 64), ALU.mult))
                dve.wait_ge(sem("chunk_exps"), c + 1)
                v.tensor_tensor(heads_of(xdec), xc, bc_in(endb[:, 2, :], 64), ALU.mult).then_inc(sem("x_decayed"), 1)
                if c < NT - 1:
                    dve.wait_ge(sem("state_products"), c + 1)
                    for g in range(2):
                        pg = prev[:, g * 512:g * 512 + 512]
                        if c == 0:
                            ins = copy(pg, B[2 + g][:, :])
                        else:
                            step(v.tensor_tensor(heads_of(pg), heads_of(pg), bc_in(endb[:, 0, 8 * g:8 * g + 8], 64),
                                                 ALU.mult))
                            ins = v.tensor_tensor(pg, pg, B[2 + g][:, :], ALU.add)
                    ins.then_inc(sem("states_kept"), 1)
                dve.wait_ge(sem("ydiag"), c + 1)
                for g in range(2):
                    yc = Y[:, c, g * 512:g * 512 + 512]
                    if c:
                        step(v.tensor_tensor(heads_of(tmp), heads_of(B[g][:, :]),
                                             bc_in(endb[:, 1, 8 * g:8 * g + 8], 64), ALU.mult))
                        step(v.tensor_tensor(yc, yc, tmp, ALU.add))
                    v.tensor_tensor(yc, yc, B[6 + g][:, :], ALU.add).then_inc(sem("y_summed"), 1)
                for half in range(2):
                    dve.wait_ge(sem("y_summed"), 2 * c + half + 1)
                    dve.wait_ge(sem("z_gate"), 2 * c + half + 1)
                    yc = Y[:, c, half * 512:half * 512 + 512]
                    v.tensor_tensor(yc, yc, zt[half], ALU.mult).then_inc(sem("z_used"), 1)
            dve.wait_ge(sem("z_used"), 8)
            norm_dve(dve, step, 2, Y, Y, yT, pcol[:, SSDN:SSDN + 8])

            dve.wait_ge(sem("scan_mask"), 2)
            for d in range(4):
                dve.wait_ge(sem("gla_log"), d + 1)
                step(v.scalar_tensor_tensor(out=g1, in0=g1, scalar=0.0, in1=g2, op0=ALU.min, op1=ALU.subtract))
                step(v.tensor_tensor_scan(g3, m64, g1, 0.0, ALU.mult, ALU.add))
                ends = g3.rearrange("p (c n) -> p c n", n=64)[:, :, 63]
                v.tensor_tensor(g1.rearrange("p (c n) -> p c n", n=64), bc_in(ends, 64),
                                g3.rearrange("p (c n) -> p c n", n=64), ALU.subtract).then_inc(sem("gla_sums"), 1)
                dve.wait_ge(sem("gla_exps"), d + 1)
                step(copy(odec[:, d, :], g2.rearrange("p (c n) -> p c n", n=64)[:, :, 63]))
                dve.wait_ge(sem("qk_products"), max(2 * d + 2, 4))
                step(v.scalar_tensor_tensor(out=QD[:, d, :], in0=B[6 if d % 2 == 0 else 2][:, :], scalar=P ** -0.5, in1=g2,
                                            op0=ALU.mult, op1=ALU.mult))
                if d:
                    dve.wait_ge(sem("head_scores"), d)
                step(v.tensor_tensor(gki, gen, B[7 if d % 2 == 0 else 3][:, :], ALU.mult))
                v.tensor_tensor(gkd, gke, B[7 if d % 2 == 0 else 3][:, :], ALU.mult).then_inc(sem("gate_keys"), 1)
                dve.wait_ge(sem("head_scores"), d + 1)
                v.copy_predicated(ATT[:, d, :].rearrange("p (t n) -> p t n", t=NT),
                                  bc_out(gmask[:, :].bitcast(U32), NT),
                                  B[0][:, :].rearrange("p (t n) -> p t n", t=NT)).then_inc(sem("scores_kept"), 1)
                copy(KTOK[:, :, d * P:d * P + P],
                     B[1][:, :].rearrange("p (t n) -> p t n", t=NT)).then_inc(sem("k_turned_kept"), 1)
            for i in range(1, 8, 2):
                dve.wait_ge(sem("v_products"), i + 1)
                half, t = divmod(i, NT)
                copy(V[:, t, half * 512:half * 512 + 512], B[4 + i % 4][:, :]).then_inc(sem("v_kept_dve"), 1)
            dve.wait_ge(sem("residual_loaded2"), 16)
            for c in range(7):
                dve.wait_ge(sem("gla_states"), c + 1)
                for d in range(4):
                    src = B[4 + d // 2][:, (d % 2) * 256:(d % 2) * 256 + 256]
                    if c == 0:
                        ins = copy(ST[:, d, :], src)
                    else:
                        ins = v.scalar_tensor_tensor(out=ST[:, d, :], in0=ST[:, d, :], scalar=odec[:, d, c:c + 1],
                                                     in1=src, op0=ALU.mult, op1=ALU.add)
                ins.then_inc(sem("gla_states_kept"), 1)
                add_out(8 + c + 1, c, B[6 + c % 2])
                dve.wait_ge(sem("gla_states_kept"), c + 1)
            add_out(16, 7, B[7])
            dve.wait_ge(sem("o_squares"), 16)
            step(v.tensor_scalar(ssq[:, :], ssq[:, :], 1.0 / 256, EPS, ALU.mult, ALU.add))
            v.reciprocal(rstd[:, :], ssq[:, :]).then_inc(sem("o_recip"), 1)
            dve.wait_ge(sem("o_rstd"), 1)
            dve.wait_ge(sem("o_kept"), 8)
            for i in range(8):
                half, t = divmod(i, NT)
                dve.wait_ge(sem("r_gate"), i + 1)
                for a in range(2):
                    d = 2 * half + a
                    oc = O[:, t, d * 256:d * 256 + 256]
                    v.scalar_tensor_tensor(out=oc, in0=oc, scalar=rstd[:, 4 * t + d:4 * t + d + 1],
                                           in1=rt[i % 2][:, a * 256:a * 256 + 256],
                                           op0=ALU.mult, op1=ALU.mult).then_inc(sem("o_scaled"), 1)
            for i in range(2 * NT):
                t, g = i // 2, i % 2
                dve.wait_ge(sem("o_turned"), i + 1)
                v.tensor_tensor(oT[:, 4 * g:4 * g + 4, t * P:t * P + P],
                                B[i % 2][:, :].rearrange("p (c n) -> p c n", c=4),
                                bc_in(gla8[:, 4 * g:4 * g + 4], P), ALU.mult).then_inc(sem("o_tkept"), 1)
            dve.wait_ge(sem("mixer_added"), 16)
            for j in range(8):
                add_out(16 + j + 1, j, B[j])
                if j > NT:
                    keep_tile(1, j - NT - 1)

            moe(1)
            norm_dve(dve, step, 3, h, fin_o, None, None)
            dve.wait_ge(sem("final_gain"), 16)
            dve.wait_ge(sem("norm_rows"), 4 * NT)
            for t in range(NT):
                v.tensor_tensor(fin_o[:, t, :], fin_o[:, t, :], fin_g, ALU.mult).then_inc(sem("final_rows"), 1)

        @block.tensor
        def _(pe):
            mm, turn = nc.tensor.matmul, nc.tensor.transpose
            pe.wait_ge(sem("constants"), 1)
            norm_pe(pe, 0, e_xs, True)

            def job_bank(j):
                if j >= 4:
                    pe.wait_ge(sem("job_kept_act") if j % 2 == 0 else sem("job_kept_dve"), (j - 4) // 2 + 1)
                return B[j % 4]

            def window_scores(n):
                k0 = P if n == 0 else 0
                if n == 0:
                    pe.wait_ge(sem("job_kept_act"), JI["ka"] // 2 + 1)
                    pe.wait_ge(sem("job_kept_dve"), 2)
                for g in range(2):
                    if n:
                        pe.wait_ge(sem("a_biased"), HQ * (n - 1) + 4 * g + 4)
                    for hh in range(4 * g, 4 * g + 4):
                        last = mm(B[4 + hh // 2][:, (hh % 2) * 256 + k0:(hh % 2) * 256 + 256],
                                  qpad[:, hh, n * P:n * P + P], kaT[:, (n - 1) * P + k0:(n + 1) * P],
                                  start=True, stop=True)
                    last.then_inc(sem("a_scores"), 1)

            for j, name in enumerate(JOBS):
                bank = job_bank(j)
                if name[:2] == "qa":
                    if name == "qa0":
                        loaded(pe, EV_IN)
                    last = project_T(bank[:, :], unit(EV_IN), int(name[2]) * P, P)
                elif name == "ka":
                    loaded(pe, EV_IN + 1)
                    last = project_T(bank[:, :], unit(EV_IN + 1), 0, P)
                elif name == "va":
                    for t in range(NT):
                        last = project(bank[:, t * P:t * P + P], t, unit(EV_IN + 1), P, P)
                elif name == "f":
                    pe.wait_ge(sem("params"), 16 * NPARAMS)
                    for c in range(KC):
                        last = mm(bank[0:8, :], wf[:, c, :], hnT[:, c, :], start=c == 0, stop=c == KC - 1)
                elif name[:2] in ("qb", "kb"):
                    n = EV_IN + (2 if name[0] == "q" else 3)
                    if name[2] == "0":
                        loaded(pe, n)
                    last = project_T(bank[:, :], unit(n), int(name[2]) * P, P)
                elif name[:2] == "vb":
                    if name == "vb0":
                        loaded(pe, EV_IN + 4)
                    last = project(bank[:, :], int(name[2]), unit(EV_IN + 4), 0, 512)
                elif name[:2] == "pt":
                    n, m = int(name[2]), int(name[4])
                    if m == 0:
                        pe.wait_ge(sem("a_probs"), n + 1)
                    for b in range(2):
                        for a in range(1 if n == 0 else 0, 2):
                            last = turn(bank[:, b * 256 + a * P:b * 256 + a * P + P],
                                        SA[:, 2 * m + b, a * P:a * P + P], ident[:, :])
                elif name[:2] == "pv":
                    n = int(name[2])
                    pe.wait_ge(sem("job_kept_act"), kept_before(j, 0))
                    pe.wait_ge(sem("job_kept_dve"), kept_before(j, 1))
                    for hh in range(HQ):
                        lo = 64 * (hh % 2)
                        o = bank[lo:lo + 64, (hh // 2) * P:(hh // 2) * P + P]
                        kv = 64 * (hh // 4)
                        if n:
                            mm(o, va[:, n - 1, kv:kv + 64], PTA[:, hh, 0, :], start=True, stop=False)
                        last = mm(o, va[:, n, kv:kv + 64], PTA[:, hh, 1, :], start=n == 0, stop=True)
                last.then_inc(sem("job_done"), 1)
                if name in SCORES_AFTER:
                    window_scores(SCORES_AFTER[name])

            pe.wait_ge(sem("gate_rows"), 16 * 2 * HQ)
            pe.wait_ge(sem("k_padded"), 1)
            pe.wait_ge(sem("job_kept_act"), kept_before(len(JOBS), 0))
            pe.wait_ge(sem("job_kept_dve"), kept_before(len(JOBS), 1))
            pe.wait_ge(sem("a_biased"), 4 * HQ)

            def values(hh):
                pe.wait_ge(sem("b_tkept"), 4 * hh + 4)
                pair, lo = hh // 2, 64 * (hh % 2)
                if pair >= 2:
                    pe.wait_ge(sem("b_heads"), pair - 1)
                for j in range(NT):
                    last = mm(B[pair % 2][lo:lo + 64, j * P:512], vb[:, j, hh * 64:hh * 64 + 64],
                              PTB[:, hh % 2, j, j * P:512], start=j == 0, stop=j == NT - 1)
                last.then_inc(sem("b_values"), 1)

            for i in range(4 * HQ + 3):
                if i < 4 * HQ:
                    hh, n = divmod(i, 4)
                    if i >= 4:
                        pe.wait_ge(sem("b_exp"), i - 3)
                    mm(B[2 + i % 4][:, 0:(n + 1) * P], qb[:, hh, n * P:n * P + P], kb[:, hh, 0:(n + 1) * P],
                       start=True, stop=True).then_inc(sem("b_scores"), 1)
                if i >= 3:
                    j = i - 3
                    n = j % 4
                    pe.wait_ge(sem("b_probs"), j + 1)
                    if j >= 2:
                        pe.wait_ge(sem("b_tkept"), j - 1)
                    for a in range(n + 1):
                        last = turn(B[6 + j % 2][:, a * P:a * P + P], PB[:, j % 4, a * P:a * P + P], ident[:, :])
                    last.then_inc(sem("b_turned"), 1)
                    if n == 0 and j:
                        values(j // 4 - 1)
            values(HQ - 1)

            def turn_tile(L, t):
                pe.wait_ge(sem("mixer_added"), (0, 16)[L] + NT + t + 1)
                for g in range(2):
                    if t:
                        pe.wait_ge(sem("moe_kept"), 8 * L + 2 * t + g - 1)
                    for j in range(4):
                        src = h[:, t, :].rearrange("p (q c) -> p c q", c=KC)[:, 4 * g + j, :]
                        last = turn(B[g][:, j * P:j * P + P], src, ident[:, :])
                    last.then_inc(sem("moe_turned"), 1)

            pe.wait_ge(sem("b_heads"), 4)
            for j in range(8):
                half, t = divmod(j, NT)
                if t == 0:
                    loaded(pe, EV_OUT + half)
                if j >= 4:
                    pe.wait_ge(sem("mixer_added"), j - 3)
                for c in range(KC):
                    hT_c = headsA[:, c, t * P:t * P + P] if c < 4 else headsB[:, c - 4, t * P:t * P + P]
                    last = mm(B[2 + j % 4][:, :], hT_c, unit(EV_OUT + half)[:, c, :], start=c == 0, stop=c == KC - 1)
                last.then_inc(sem("out_products"), 1)
                if j > NT:
                    turn_tile(0, j - NT - 1)

            def turn_rows(u):
                pe.sem_inc(sem("pe_passed"), 1)
                for c in range(KC):
                    last = turn(B[2][:, c * CAP:c * CAP + CAP],
                                xin[u][0:CAP, :].rearrange("p (q c) -> p c q", c=KC)[:, c, :], ident[0:CAP, 0:CAP])
                return last

            def turn_hidden():
                pe.sem_inc(sem("pe_passed"), 1)
                for c in range(4):
                    last = turn(B[3][:, c * CAP:c * CAP + CAP],
                                hb[64:128, :].rearrange("p (q c) -> p c q", c=4)[:, c, :], ident[64:128, 64:128])
                return last

            def gate_up_products(u, n):
                for c in range(KC):
                    mm(B[0][0:64, :], xT[u][:, c, :], unit(n)[:, c, :], start=c == 0, stop=c == KC - 1)
                    last = mm(B[1][64:128, :], xT[u][:, c, :], unit(n + 1)[:, c, :], start=c == 0, stop=c == KC - 1)
                return last

            def down_products(u, n, bank):
                w = ring[:, n % RING, :].rearrange("p (c n) -> p c n", c=4)
                for c in range(4):
                    for a in range(2):
                        last = mm(bank[64 * a:64 * a + 64, :], hT[u][:, c, :], w[:, c, a * 512:a * 512 + 512],
                                  start=c == 0, stop=c == 3)
                return last

            def moe(L):
                turn_tile(L, NT - 1)
                pe.wait_ge(sem("moe_kept"), 8 * (L + 1))
                if L == 1:
                    pe.wait_ge(sem("router_loaded"), 64)
                for c in range(KC):
                    last = mm(B[2][0:NR, :], wr[:, c, :], mhT[:, c, :], start=c == 0, stop=c == KC - 1)
                last.then_inc(sem("logits"), 1)
                pe.wait_ge(sem("logits_kept"), L + 1)
                for t in range(NT):
                    last = turn(B[3][:, t * NR:t * NR + NR], lgT[0:NR, t * P:t * P + P], ident[0:NR, 0:NR])
                last.then_inc(sem("logits_turned"), 1)
                pe.wait_ge(sem("picks"), L + 1)
                for t in range(NT):
                    for j in range(t):
                        mm(B[2][:, t * E:t * E + E], ones_b[:, :], cntb[:, j, :], start=j == 0, stop=False)
                    mm(B[2][:, t * E:t * E + E], upper[:, :], cntb[:, t, :], start=t == 0, stop=True)
                for j in range(NT):
                    last = mm(B[2][:, NT * E:NT * E + E], ones_b[:, :], cntb[:, j, :], start=j == 0, stop=j == NT - 1)
                last.then_inc(sem("ranks"), 1)

                base = MOE[L]

                def unit_ready(i, n):
                    pe.wait_ge(unit_loaded[n % RING], 16 * i + 16 * (n // RING + 1))

                def rows(i, u):
                    pe.wait_ge(sem(f"block{u}_loaded"), 16 * ((E // 2) * L + i + 1))
                    pe.wait_ge(sem("x_kept"), E * L + 2 * i + u)
                    turn_rows(u).then_inc(sem("x_turned"), 1)

                def gate_up(i, u):
                    pe.wait_ge(sem("x_kept"), E * L + 2 * i + u + 1)
                    unit_ready(i, base + 3 * u)
                    unit_ready(i, base + 3 * u + 1)
                    gate_up_products(u, base + 3 * u).then_inc(sem("gate_up_used"), 1)

                def down(i, u):
                    pe.wait_ge(sem("h_kept"), E * L + 2 * i + u + 1)
                    unit_ready(i, base + 3 * u + 2)
                    down_products(u, base + 3 * u + 2, B[4 + u]).then_inc(sem("down_used"), 1)

                def hidden_rows(i, u):
                    pe.wait_ge(sem("hidden"), E * L + 2 * i + u + 1)
                    turn_hidden().then_inc(sem("h_turned"), 1)

                rows(0, 0)
                gate_up(0, 0)
                rows(0, 1)
                hidden_rows(0, 0)
                gate_up(0, 1)
                down(0, 0)
                with pe.Fori(1, E // 2) as i:
                    rows(i, 0)
                    hidden_rows(i - 1, 1)
                    gate_up(i, 0)
                    pe.wait_ge(sem("y_kept"), E * L + 2 * i - 1)
                    down(i - 1, 1)
                    rows(i, 1)
                    hidden_rows(i, 0)
                    gate_up(i, 1)
                    pe.wait_ge(sem("y_kept"), E * L + 2 * i)
                    down(i, 0)
                hidden_rows(E // 2 - 1, 1)
                pe.wait_ge(sem("y_kept"), E * L + E - 2)
                down(E // 2 - 1, 1)

                pe.wait_ge(sem("routed"), L + 1)
                n_over = pe.value_load(ovtab[0:1, OVR:OVR + 1], min_val=0, max_val=MAXOV)
                with pe.If(n_over > 0):
                    pe.wait_ge(sem("y_kept"), E * (L + 1))
                    with pe.Fori(0, n_over) as b:
                        pe.wait_ge(sem(f"over{L}_rows"), 16 * b + 16)
                        turn_rows(0).then_inc(sem(f"over{L}_steps"), 1)
                        pe.wait_ge(sem(f"over{L}_steps"), OVS * b + 2)
                        pe.wait_ge(sem(f"over{L}_weights"), 48 * b + 48)
                        gate_up_products(0, base).then_inc(sem(f"over{L}_steps"), 1)
                        pe.wait_ge(sem(f"over{L}_steps"), OVS * b + 5)
                        turn_hidden().then_inc(sem(f"over{L}_steps"), 1)
                        pe.wait_ge(sem(f"over{L}_steps"), OVS * b + 7)
                        down_products(0, base + 2, B[4]).then_inc(sem(f"over{L}_steps"), 1)

            moe(0)

            norm_pe(pe, 1, xs, True)
            turn(B[7][:, 0:74], prow[0:74, :], ident[0:74, 0:74]).then_inc(sem("pcol_turned"), 1)
            for c in range(KC):
                last = mm(B[4][0:48, :], wdg[:, c, :], hnT[:, c, :], start=c == 0, stop=c == KC - 1)
            last.then_inc(sem("dt_products"), 1)
            for j in range(CH + 1):
                if j < CH:
                    n = OD_BC + j // 4
                    if j % 4 == 0:
                        loaded(pe, n)
                    if j >= 2:
                        pe.wait_ge(sem("conv_summed"), j - 1)
                    project_T(B[j % 2][:, :], unit(n), (j % 4) * P, P).then_inc(sem("conv_products"), 1)
                if j >= 1 and j - 1 in TURNED:
                    i = TURNED.index(j - 1)
                    pe.wait_ge(sem("conv_out"), j)
                    if i >= 2:
                        pe.wait_ge(sem("conv_tkept"), i - 1)
                    src = BT[:, i, :] if i < 2 else cso[(j - 1) % 2]
                    for t in range(NT):
                        last = turn(B[2 + i % 2][:, t * P:t * P + P], src[:, t * P:t * P + P], ident[:, :])
                    last.then_inc(sem("conv_turned"), 1)
            pe.wait_ge(sem("decays"), 1)
            for t in range(NT):
                turn(B[5][:, t * 32:t * 32 + 16], dtx[0:16, t * P:t * P + P], ident[0:16, 0:16])
                last = turn(B[5][:, t * 32 + 16:t * 32 + 32], acsT[0:16, t * P:t * P + P], ident[0:16, 0:16])
            last.then_inc(sem("decays_turned"), 1)
            for g in range(2):
                for c in range(NT):
                    last = mm(B[6 + g][:, c * P:c * P + P], BT[:, g, c * P:c * P + P], CT[:, g, c * P:c * P + P],
                              start=True, stop=True)
                last.then_inc(sem("cb_products"), 1)
            pe.wait_ge(sem("cb_kept"), 2)

            pe.wait_ge(sem("rank_kept"), 1)
            for c in range(NT):
                for half in range(2):
                    if c == 0:
                        loaded(pe, OD_Z + half)
                    else:
                        pe.wait_ge(sem("z_gate"), 2 * c + half - 1)
                    project(B[4 + half][:, :], c, unit(OD_Z + half), 0, 512).then_inc(sem("z_products"), 1)
                pe.wait_ge(sem("x_decayed"), c + 1)
                if c:
                    pe.wait_ge(sem("states_kept"), c)
                    pe.wait_ge(sem("y_summed"), 2 * c)
                    for g in range(2):
                        mm(B[g][:, :], CT[:, g, c * P:c * P + P], prev[:, g * 512:g * 512 + 512], start=True, stop=True)
                if c < NT - 1:
                    for g in range(2):
                        last = mm(B[2 + g][:, :], Btok[:, c, g, :], xdec[:, g * 512:g * 512 + 512],
                                  start=True, stop=True)
                    last.then_inc(sem("state_products"), 1)
                pe.wait_ge(sem("mt_ready"), 4 * c + 4)
                for hh in range(16):
                    last = mm(B[6 + hh // 8][:, (hh % 8) * 64:(hh % 8) * 64 + 64], MT[c % 2][:, hh, :],
                              XS[:, c, hh * 64:hh * 64 + 64], start=True, stop=True)
                last.then_inc(sem("ydiag"), 1)

            def qk_products(d):
                q = 6 if d % 2 == 0 else 2
                for a, n in enumerate((OD_Q, OD_K)):
                    loaded(pe, n)
                    project_T(B[q + a][:, :], unit(n), d * P, P).then_inc(sem("qk_products"), 1)

            def gate_product(d):
                mm(B[4 + d % 2][:, :], gkw[0:16, d * P:d * P + P], glrT[0:16, :],
                   start=True, stop=True).then_inc(sem("gate_products"), 1)

            pe.wait_ge(sem("states_kept"), NT - 1)
            qk_products(1)
            pe.wait_ge(sem("z_gate"), 8)
            pe.wait_ge(sem("gk_loaded"), 16)
            gate_product(0)
            gate_product(1)
            norm_pe(pe, 2, Y, False)
            pe.wait_ge(sem("y_summed"), 2 * NT)
            qk_products(0)

            for d in range(1, 5):
                if 2 <= d < 4:
                    pe.wait_ge(sem("gla_log"), d - 1)
                    gate_product(d)
                    pe.wait_ge(sem("gate_keys"), d - 1)
                    qk_products(d)
                if d:
                    e = d - 1
                    pe.wait_ge(sem("gate_keys"), e + 1)
                    pe.wait_ge(sem("scores_kept"), e)
                    pe.wait_ge(sem("k_turned_kept"), e)
                    for t in range(NT):
                        mm(B[0][:, t * P:t * P + P], gki[:, t * P:t * P + P], QD[:, e, t * P:t * P + P],
                           start=True, stop=True)
                    for t in range(NT):
                        last = turn(B[1][:, t * P:t * P + P], gkd[:, t * P:t * P + P], ident[:, :])
                    last.then_inc(sem("head_scores"), 1)
            pe.wait_ge(sem("gla_log"), 4)
            for i in range(8):
                half, t = divmod(i, NT)
                if t == 0:
                    loaded(pe, OD_V + half)
                if i >= 4:
                    pe.wait_ge(sem("v_kept_act") if i % 2 == 0 else sem("v_kept_dve"), (i - 4) // 2 + 1)
                project(B[4 + i % 4][:, :], t, unit(OD_V + half), 0, 512).then_inc(sem("v_products"), 1)
            pe.wait_ge(sem("scores_kept"), 4)
            pe.wait_ge(sem("k_turned_kept"), 4)
            pe.wait_ge(sem("v_kept_act"), 4)
            pe.wait_ge(sem("v_kept_dve"), 4)
            for t in range(NT):
                if t >= 2:
                    pe.wait_ge(sem("o_kept"), 2 * (t - 1))

                def o_bank(d):
                    return B[2 * (t % 2) + d // 2]

                for d in range(4):
                    mm(o_bank(d)[:, (d % 2) * 256:(d % 2) * 256 + 256], ATT[:, d, t * P:t * P + P],
                       V[:, t, d * 256:d * 256 + 256], start=d % 2 == 0, stop=True, skip_group_check=True)
                for j in range(2):
                    c, lo = 2 * t + j, 64 * j
                    if c:
                        pe.wait_ge(sem("gla_states_kept"), c)
                        for d in range(4):
                            last = mm(o_bank(d)[lo:lo + 64, (d % 2) * 256:(d % 2) * 256 + 256],
                                      QD[:, d, c * 64:c * 64 + 64], ST[:, d, :], start=False, stop=True,
                                      skip_group_check=True)
                        if j:
                            last.then_inc(sem("o_products"), 1)
                    if c < 7:
                        for d in range(4):
                            last = mm(B[4 + d // 2][:, (d % 2) * 256:(d % 2) * 256 + 256],
                                      KTOK[lo:lo + 64, t, d * P:d * P + P], V[lo:lo + 64, t, d * 256:d * 256 + 256],
                                      start=True, stop=True)
                        last.then_inc(sem("gla_states"), 1)
                    half, tt = divmod(c, NT)
                    if tt == 0:
                        loaded(pe, OD_OUT[0] + half)
                    if c < 2:
                        pe.wait_ge(sem("v_kept_act"), 4)
                        pe.wait_ge(sem("v_kept_dve"), 4)
                    else:
                        pe.wait_ge(sem("mixer_added"), 8 + c - 1)
                    for k in range(KC):
                        last = mm(B[6 + c % 2][:, :], yT[:, k, tt * P:tt * P + P], unit(OD_OUT[0] + half)[:, k, :],
                                  start=k == 0, stop=k == KC - 1)
                    last.then_inc(sem("out_products"), 1)
            pe.wait_ge(sem("gla_states_kept"), 7)
            pe.wait_ge(sem("mixer_added"), 16)
            for i in range(8):
                half, t = divmod(i, NT)
                if t == 0:
                    loaded(pe, OD_R + half)
                if i >= 4:
                    pe.wait_ge(sem("r_gate"), i - 3)
                project(B[4 + i % 4][:, :], t, unit(OD_R + half), 0, 512).then_inc(sem("r_products"), 1)
            pe.wait_ge(sem("o_scaled"), 16)
            for i in range(2 * NT):
                t, g = i // 2, i % 2
                if i >= 2:
                    pe.wait_ge(sem("o_tkept"), i - 1)
                for j in range(4):
                    c = 4 * g + j
                    last = turn(B[i % 2][:, j * P:j * P + P], O[:, t, c * P:c * P + P], ident[:, :])
                last.then_inc(sem("o_turned"), 1)
            pe.wait_ge(sem("o_tkept"), 8)
            for j in range(8):
                half, t = divmod(j, NT)
                if t == 0:
                    loaded(pe, OD_OUT[1] + half)
                for c in range(KC):
                    last = mm(B[j][:, :], oT[:, c, t * P:t * P + P], unit(OD_OUT[1] + half)[:, c, :],
                              start=c == 0, stop=c == KC - 1)
                last.then_inc(sem("out_products"), 1)
                if j > NT:
                    turn_tile(1, j - NT - 1)
            moe(1)


_INS = ['x', 'norm_mix', 'norm_moe', 'norm_final', 'even_w_in', 'even_sinks', 'even_forget_bias', 'even_w_out',
        'odd_w_in', 'odd_conv_w', 'odd_conv_b', 'odd_dt_bias', 'odd_a_log', 'odd_d_skip', 'odd_ssd_norm',
        'odd_gk_w', 'odd_gk_b', 'odd_gla_norm', 'odd_w_out', 'moe_w_group', 'moe_b_group', 'moe_w_router',
        'moe_b_router', 'moe_w_gate', 'moe_w_up', 'moe_w_down']


def kernel(**inputs):
    import numpy as _np
    import concourse.bacc as _bacc
    from concourse import mybir as _mybir
    from concourse.bass_utils import run_bass_kernel_spmd as _run

    nc = _bacc.Bacc("TRN2", target_bir_lowering=False, num_devices=1)
    arrays, args = {}, []
    for name in _INS:
        a = _np.ascontiguousarray(inputs[name])
        arrays[f"in_{name}"] = a
        args.append(nc.dram_tensor(f"in_{name}", a.shape, _mybir.dt.from_np(a.dtype), kind="ExternalInput").ap())
    x = arrays["in_x"]
    out = nc.dram_tensor("out", x.shape, _mybir.dt.from_np(x.dtype), kind="ExternalOutput").ap()
    build(nc, *args, out)
    r = _run(nc, [arrays], core_ids=[0])
    return r.results[0]["out"]
```

```python
from contextlib import ExitStack

import numpy as np

import concourse.bass as bass
from concourse import mybir
from concourse.alu_op_type import AluOpType as ALU

ACT = mybir.ActivationFunctionType
AX = mybir.AxisListType
F32 = mybir.dt.float32
BF16 = mybir.dt.bfloat16
F32R = mybir.dt.float32r
U32 = mybir.dt.uint32
I32 = mybir.dt.int32

P = 128
EPS = 1e-6
BIG = 1e30
CAP = 64


class Steps:

    def __init__(self, eng, sem):
        self.eng, self.sem, self.count = eng, sem, 0

    def __call__(self, instruction):
        self.count += 1
        instruction.then_inc(self.sem, 1)
        self.eng.wait_ge(self.sem, self.count)


def build(nc, x, norm_mix, norm_moe, norm_final, even_w_in, even_sinks, even_forget_bias, even_w_out,
          odd_w_in, odd_conv_w, odd_conv_b, odd_dt_bias, odd_a_log, odd_d_skip, odd_ssd_norm,
          odd_gk_w, odd_gk_b, odd_gla_norm, odd_w_out, moe_w_group, moe_b_group, moe_w_router,
          moe_b_router, moe_w_gate, moe_w_up, moe_w_down, out):
    T, D = x.shape[1:]
    NT, KC = T // P, D // P
    E, FF = moe_w_gate.shape[1], moe_w_gate.shape[3]
    NG = moe_w_group.shape[2]
    EPG = E // NG
    NR = NG + E
    NB = 2 * T
    MAXOV = NB // (CAP + 1)
    OVR = MAXOV + 1
    CR = T // CAP
    XROWS = E * CAP + OVR * CAP
    HQ = 8
    NC_IN = 1024 + 2 * 256
    CH = NC_IN // P
    RING = 6
    SLOTS = 9
    OVS = 9
    NPARAMS = 17

    EV_IN, EV_OUT = 0, 5
    MOE0 = 7
    OD = MOE0 + 3 * E
    OD_BC, OD_XS, OD_Z, OD_Q, OD_K, OD_V, OD_R = OD, OD + 1, OD + 3, OD + 5, OD + 6, OD + 7, OD + 9
    OD_OUT = (OD + 11, OD + 13)
    MOE1 = OD + 15
    MOE = (MOE0, MOE1)

    slot = {n: n % 2 for n in range(EV_IN, MOE0)}
    slot.update({OD + k: k % 2 for k in range(15)})
    slot.update({MOE[L] + k: k for L in range(2) for k in range(SLOTS)})
    turn_of, turns = {}, [0] * SLOTS
    for n in sorted(slot):
        turns[slot[n]] += 1
        turn_of[n] = turns[slot[n]]
        if n - MOE0 in range(SLOTS) or n - MOE1 in range(SLOTS):
            turns[slot[n]] += len(range(slot[n] // 3, E, 3)) - 1
    PIECES = [(EV_IN, 0), (EV_IN, 256), (EV_IN + 1, 0)]
    for n in (EV_IN + 2, EV_IN + 3, EV_IN + 4, EV_OUT, EV_OUT + 1, OD_BC, OD_XS, OD_XS + 1, OD_Z, OD_Z + 1):
        PIECES += [(n, 0), (n, 256)]
    PIECES += [(OD_Q, 0), (OD_K, 0), (OD_Q, 256), (OD_K, 256)]
    for n in (OD_V, OD_V + 1, OD_R, OD_R + 1, OD_OUT[0], OD_OUT[0] + 1, OD_OUT[1], OD_OUT[1] + 1):
        PIECES += [(n, 0), (n, 256)]
    piece = {key: k for k, key in enumerate(PIECES)}
    PIECE_DONE = {}
    for k, (n, c0) in enumerate(PIECES):
        b = c0 // 256
        if n == EV_IN:
            PIECE_DONE[k] = ("job_done", (2, 4)[b])
        elif n == EV_IN + 1:
            PIECE_DONE[k] = ("job_done", 6)
        elif n < EV_OUT:
            name = ("qb", "kb", "vb")[n - EV_IN - 2] + ("1", "3")[b]
            PIECE_DONE[k] = ("job_done", name)
        elif n < MOE0:
            PIECE_DONE[k] = ("out_products", 4 * (n - EV_OUT) + 2 * b + 2)
        elif n < OD_Z:
            PIECE_DONE[k] = ("conv_products", 4 * (n - OD_BC) + 2 * b + 2)
        elif n < OD_Q:
            PIECE_DONE[k] = ("z_products", 4 * (n - OD_Z) + 2 * b + 2)
        elif n < OD_V:
            PIECE_DONE[k] = ("qk_products", 4 * b + 2 * (n - OD_Q) + 2)
        elif n < OD_R:
            PIECE_DONE[k] = ("v_products", 4 * (n - OD_V) + 2 * b + 2)
        elif n < OD_OUT[0]:
            PIECE_DONE[k] = ("r_products", 4 * (n - OD_R) + 2 * b + 2)
        else:
            PIECE_DONE[k] = ("out_products", 8 + 4 * (n - OD_OUT[0]) + 2 * b + 2)

    ctx = ExitStack()
    with ctx:
        def sb(name, shape, dt=F32):
            return ctx.enter_context(nc.sbuf_tensor(name, shape, dt))

        made = {}

        def sem(name):
            if name not in made:
                made[name] = ctx.enter_context(nc.semaphore(name))
            return made[name]

        xrows = nc.dram_tensor("xrows", [XROWS, D], F32).ap()
        yrows = nc.dram_tensor("yrows", [XROWS, D], F32).ap()
        sums_d = nc.dram_tensor("sums_d", [16, T], F32).ap()
        hsave = nc.dram_tensor("hsave", [T, D], F32).ap()

        with nc.sbuf_tensor("ring", [P, RING, 8 * 512], F32) as ring:
            pass
        sb("ring_front", [P, 2, 8 * 512])
        xhi, xlo = sb("xhi", [P, 8, 512], F32R), sb("xlo", [P, 8, 512], F32R)
        whi, wlo = sb("whi", [P, 2, 8, 256], F32R), sb("wlo", [P, 2, 8, 256], F32R)
        arena = sb("arena", [P, 104 * 256])

        def at(kb, *shape, dt=F32):
            n = int(np.prod(shape))
            a = arena[:, int(kb * 256):int(kb * 256) + n]
            names = "abcd"[:len(shape)]
            if len(shape) == 1:
                return a
            pat = "p (" + " ".join(names) + ") -> p " + " ".join(names)
            return a.rearrange(pat, **{k: v for k, v in zip(names[1:], shape[1:])})

        def unit(n):
            return ring[:, slot[n], :].rearrange("p (c n) -> p c n", c=8)

        def place(k):
            return ring[:, k, :] if k < RING else at((0, 54, 70)[k - RING], 8 * 512)

        ident = sb("ident", [P, P])
        upper = sb("upper", [P, P], BF16)
        ones_b = sb("ones_b", [P, P], BF16)
        dist = sb("dist", [P, 256])
        cmask = sb("cmask", [P, P])
        tri = sb("tri", [P, P])
        gmask = sb("gmask", [P, P])
        wf = sb("wf", [P, 8, 8])
        wdg = sb("wdg", [P, 8, 48])
        pcol = sb("pcol", [P, 80])
        gmix = sb("gmix", [P, 2, 8])
        gmoe = sb("gmoe", [P, 2, 8])
        fbias = sb("fbias", [8, 1])
        sink8 = sb("sink8", [P, HQ])
        dskip = sb("dskip", [P, 16])
        dtb = sb("dtb", [16, 1])
        acol = sb("acol", [16, 1])
        gla8 = sb("gla8", [P, 8])
        ssq = sb("ssq", [P, 16])
        rstd = sb("rstd", [P, 16])
        stat = sb("stat", [P, 8, 4])
        datok = sb("datok", [P, NT, 2, 16])
        endb = sb("endb", [P, 3, 16])
        slots = sb("slots", [P, 2 * NT], U32)
        gates = sb("gates", [P, NT, 2])
        ovtab = sb("ovtab", [1, OVR + 1], I32)
        ones_f = sb("ones_f", [P, 1])
        it32 = sb("it32", [P, E])
        gid32 = sb("gid32", [P, E])
        thr = sb("thr", [P, CR])
        CONVW, CONVB, GKB, SSDN, GLAN = 0, 48, 60, 64, 72

        B = [ctx.enter_context(nc.psum_tensor(f"bank{i}", [P, 512], F32)) for i in range(8)]

        hnT = at(0, 8, 512)
        h = at(88, NT, D)
        xs = at(16, NT, D)

        def bc_in(col, n):
            return col.unsqueeze(2).to_broadcast([col.shape[0], col.shape[1], n])

        def bc_out(row, n):
            return row.unsqueeze(1).to_broadcast([row.shape[0], n, row.shape[1]])

        x_loaded = [sem(f"x_loaded{t}") for t in range(NT)]
        unit_loaded = [sem(f"unit_loaded{i}") for i in range(SLOTS)]

        def loaded(eng, n):
            eng.wait_ge(unit_loaded[slot[n]], 16 * turn_of[n])

        def wait_done(eng, k):
            name, count = PIECE_DONE[k]
            eng.wait_ge(sem(name), JI[count] + 1 if isinstance(count, str) else count)

        def weight_high(act, k):
            n, c0 = PIECES[k]
            loaded(act, n)
            if k >= 2:
                wait_done(act, k - 2)
            nc.scalar.activation(whi[:, k % 2], unit(n)[:, :, c0:c0 + 256], ACT.Copy).then_inc(sem("w_high"), 1)

        def weight_low(eng, k):
            n, c0 = PIECES[k]
            eng.wait_ge(sem("w_high"), k + 1)
            eng.tensor_tensor(wlo[:, k % 2], unit(n)[:, :, c0:c0 + 256], whi[:, k % 2].bitcast(F32),
                              ALU.subtract).then_inc(sem("w_low"), 1)

        def x_high(src, dst):
            nc.scalar.activation(dst(xhi), src, ACT.Copy).then_inc(sem("x_high"), 1)

        def x_low(dve, k, src, dst):
            dve.wait_ge(sem("x_high"), k)
            nc.vector.tensor_tensor(dst(xlo), src, dst(xhi).bitcast(F32), ALU.subtract).then_inc(sem("x_low"), 1)

        def tile_of(t):
            return lambda a: a[:, :, t * P:t * P + P]

        def chunks_of(c0, c1):
            return lambda a: a[:, c0:c1, :]

        X_EVEN, X_HEADS, X_ODD, X_Y, X_O = 0, 4, 9, 13, 17

        JI = {}

        block = ctx.enter_context(nc.Block())

        qpad = at(16, HQ, 512)
        qb, kb = at(32, HQ, 512), at(48, HQ, 512)
        kaT, va, vb = at(64, 512), at(66, NT, P), at(68, NT, 512)
        headsA, headsB = at(76, 4, 512), at(0, 4, 512)
        e_xs = at(48, NT, D)
        SA, PTA = at(88, HQ, 256), at(96, HQ, 2, P)
        PB, PTB = at(88, 4, 512), at(16, 2, 4, 512)
        fx, fe, cT, c8, cn8 = at(76, 512), at(78, 512), at(80, 512), at(82, 512), at(84, 512)
        zrow = at(68, D)
        JOBS = (["qa0", "qa1", "qa2", "qa3", "ka", "va", "f", "qb0", "qb1", "qb2",
                 "pt0_0", "pt0_1", "pt0_2", "pt0_3", "pv0", "qb3", "kb0", "kb1",
                 "pt1_0", "pt1_1", "pt1_2", "pt1_3", "pv1", "kb2", "kb3", "vb0",
                 "pt2_0", "pt2_1", "pt2_2", "pt2_3", "pv2", "vb1", "vb2", "vb3",
                 "pt3_0", "pt3_1", "pt3_2", "pt3_3", "pv3"])
        JI.update({name: i for i, name in enumerate(JOBS)})

        def kept_before(j, parity):
            return (j + 1) // 2 if parity == 0 else j // 2

        SCORES_AFTER = {"f": 0, "qb2": 1, "kb1": 2, "vb0": 3}
        MAX_AFTER = {"f": 0, "pv0": 1, "pv1": 2, "pv2": 3}
        EXP_AFTER = {"f": 0, "qb3": 1, "kb2": 2, "vb1": 3}
        PROBS_AFTER = {"qb0": 0, "kb0": 1, "kb3": 2, "vb2": 3}
        PIECE_AFTER = {"qa1": 2, "qa3": 3, "va": 4, "qb1": 5, "qb3": 6, "kb1": 7, "kb3": 8, "vb1": 9, "vb3": 10}

        xin = [at(32, D), at(36, D)]
        mhT = at(32, 8, 512)
        xT = [at(40, 8, CAP), at(42, 8, CAP)]
        sg, hb = at(44, 512), at(46, 512)
        hT = [at(48, 4, CAP), at(49, 4, CAP)]
        ysb = [at(50, 512), at(52, 512)]
        yg = at(54, 8, D)
        wr = at(86, 8, NR)
        brow = at(87.75, NR)
        prow = at(87.25, P)[0:80]
        lgT = at(32, 512)
        lg = at(34, NT, NR)
        gp, gm8, gi8 = at(35, NT, 8), at(35.125, NT, 8), at(35.25, NT, 8).bitcast(U32)
        em8, ei8 = at(35.375, NT, 8), at(35.5, NT, 8).bitcast(U32)
        gf, rt_dv, rt_gs = at(35.625, NT), at(35.65625, NT), at(35.6875, NT, NG)
        ef, gw, rden = at(35.75, 2, NT), at(35.78125, NT), at(35.8125, NT)
        rk, ok, rsl = at(35.84375, 2, NT), at(35.875, 2, NT), at(35.90625, 2, NT)
        geq, em, onehot = at(36, NT, E), at(36.5, NT, E), at(37, 2, NT, E)
        nover, oend, oexcl = at(39.125, E), at(39.25, E), at(39.375, E)
        ovf = at(39.5, OVR)
        cntb = at(40, NT * E // 2).bitcast(BF16).rearrange("p (t e) -> p t e", t=NT)
        cmp = at(41, E, CR - 1)
        cmp2 = at(43, OVR, E)
        picked, picked2 = at(46, 2 * NT, E), at(47, 2 * NT, E)

        XS, Y = at(16, NT, D), at(32, NT, D)
        BT, CT = at(48, 2, 512), at(52, 2, 512)
        Btok, CBT = at(56, NT, 2, P), at(60, 2, NT, P)
        MT = [at(64, 16, P), at(72, 16, P)]
        acc = [at(32, 512), at(34, 512)]
        cso = [at(36, 512), at(38, 512)]
        zg = at(0, NT, D)
        xdec, prev = at(84, D), at(88, D)
        tmp = at(92, 512)
        dtx, dt2, acsT, m128 = at(96, 512), at(98, 512), at(100, 512), at(102, 512)
        CONV = [8, 9, 10, 11, 0, 1, 2, 3, 4, 5, 6, 7]
        TURNED = [0, 1, 4, 5, 6, 7, 8, 9, 10, 11]
        yT = at(16, 8, 512)
        V = at(32, NT, D)
        O = V
        QD, ATT, KTOK, ST = at(48, 4, 512), at(56, 4, 512), at(64, NT, 512), at(72, 4, 256)
        g1, g2, g3, gen, gke = ([at(76 + 2 * i, 512), at(2 * i, 512)] for i in range(5))
        gki, gkd = at(86, 512), at(88, 512)
        glrT, gkw, m64 = at(94, 512), at(90, 512), at(92, 512)
        oT = at(48, 8, 512)
        rt = [at(76, 512), at(78, 512)]
        fin_g = at(0, D)
        fin_o = at(16, NT, D)
        odec = sb("odec", [P, 4, 8])

        def norm_act(act, k, src, junk, ready=None):
            for t in range(NT):
                if ready:
                    act.wait_ge(*ready(t))
                nc.scalar.activation(junk(t), src[:, t, :], ACT.Square,
                                     accum_out=ssq[:, t:t + 1]).then_inc(sem("norm_squares"), 1)
            act.wait_ge(sem("norm_recip"), k + 1)
            nc.scalar.activation(rstd[:, 0:NT], rstd[:, 0:NT], ACT.Sqrt).then_inc(sem("norm_rstd"), 1)

        def norm_dve(dve, step, k, src, dst, dstT, gain, first=False):
            dve.wait_ge(sem("norm_squares"), NT * (k + 1))
            step(nc.vector.tensor_scalar(ssq[:, 0:NT], ssq[:, 0:NT], 1.0 / D, EPS, ALU.mult, ALU.add))
            nc.vector.reciprocal(rstd[:, 0:NT], ssq[:, 0:NT]).then_inc(sem("norm_recip"), 1)
            dve.wait_ge(sem("norm_rstd"), k + 1)
            for t in range(NT):
                nc.vector.tensor_scalar(dst[:, t, :], src[:, t, :], rstd[:, t:t + 1], None,
                                        ALU.mult).then_inc(sem("norm_rows"), 1)
            if first:
                dve.wait_ge(sem("gains_loaded"), 64)
            for i in range(2 * NT):
                t, g = i // 2, i % 2
                dve.wait_ge(sem("norm_turned"), 8 * k + i + 1)
                nc.vector.tensor_tensor(dstT[:, 4 * g:4 * g + 4, t * P:t * P + P],
                                        B[i % 2][:, :].rearrange("p (c n) -> p c n", c=4),
                                        bc_in(gain[:, 4 * g:4 * g + 4], P),
                                        ALU.mult).then_inc(sem("norm_kept"), 1)
            dve.wait_ge(sem("norm_kept"), 8 * k + 8)

        def norm_pe(pe, k, rows, strided):
            for i in range(2 * NT):
                t, g = i // 2, i % 2
                pe.wait_ge(sem("norm_rows"), NT * k + t + 1)
                if i >= 2:
                    pe.wait_ge(sem("norm_kept"), 8 * k + i - 1)
                for j in range(4):
                    c = 4 * g + j
                    if strided:
                        src = rows[:, t, :].rearrange("p (q c) -> p c q", c=KC)[:, c, :]
                    else:
                        src = rows[:, t, c * P:c * P + P]
                    last = nc.tensor.transpose(B[i % 2][:, j * P:j * P + P], src, ident[:, :])
                last.then_inc(sem("norm_turned"), 1)
            pe.wait_ge(sem("norm_kept"), 8 * k + 8)

        def project_T(dst, k, col):
            w = slice(col, col + P)
            for c in range(KC):
                for i, (a, b) in enumerate(((whi, xhi), (whi, xlo), (wlo, xhi))):
                    last = nc.tensor.matmul(dst, a[:, k % 2, c, w], b[:, c, :], start=c == 0 and i == 0,
                                            stop=c == KC - 1 and i == 2)
            return last

        def project(bank, k, pair):
            for j in range(2):
                t = 2 * pair + j
                for c in range(KC):
                    for i, (a, b) in enumerate(((xhi, whi), (xhi, wlo), (xlo, whi))):
                        last = nc.tensor.matmul(bank[:, j * 256:j * 256 + 256], a[:, c, t * P:t * P + P],
                                                b[:, k % 2, c, :], start=c == 0 and i == 0,
                                                stop=c == KC - 1 and i == 2)
            return last

        @block.sync
        def _(sp):
            w_ev = even_w_in[0].rearrange("(p c) n -> p c n", c=8)
            w_od = odd_w_in[0].rearrange("(p c) n -> p c n", c=8)
            wo_ev = even_w_out[0].rearrange("(c p) n -> p c n", p=P)
            wo_od = odd_w_out[0].rearrange("(k c p) n -> k p c n", k=2, p=P)
            ev_cols = [(0, 512), (512, 256), (768, 512), (1280, 512), (1792, 512)]
            od_cols = [2048, 1024, 1536, 0, 512, 2576, 3088, 3600, 4112]

            def load(n, src, cols=512):
                before = n - 2
                if n >= OD and before < OD:
                    sp.wait_ge(sem("gate_up_used"), E - 1)
                elif before >= 0:
                    sp.wait_ge(sem("w_low"), max(k for k, (m, _) in enumerate(PIECES) if m == before) + 1)
                    if before == EV_IN + 1:
                        sp.wait_ge(sem("job_done"), JI["va"] + 1)
                sp.dma_start(unit(n)[:, :, 0:cols], src).then_inc(unit_loaded[slot[n]], 16)

            for t in range(NT):
                sp.dma_start(h[:, t, :], x[0, t * P:t * P + P, :]).then_inc(x_loaded[t], 16)
            for dst, src in ((gmix, norm_mix), (gmoe, norm_moe)):
                for layer in range(2):
                    sp.dma_start(dst[:, layer, :], src[layer].rearrange("(p c) -> p c", c=8)).then_inc(
                        sem("gains_loaded"), 16)
            for i, (c0, n) in enumerate(ev_cols):
                load(EV_IN + i, w_ev[:, :, c0:c0 + n], n)
                if i == 2:
                    sp.wait_ge(sem("params"), 16 * NPARAMS)
                    sp.wait_ge(sem("zero_row"), 1)
                    sp.dma_start(xrows.rearrange("(n p) d -> p n d", p=P),
                                 zrow.unsqueeze(1).to_broadcast([P, XROWS // P, D])).then_inc(sem("rows_zeroed"), 16)
                    sp.dma_start(yrows[E * CAP:, :].rearrange("(n p) d -> p n d", p=P),
                                 zrow.unsqueeze(1).to_broadcast([P, OVR * CAP // P, D])).then_inc(sem("rows_zeroed"), 16)
            load(EV_OUT, wo_ev[:, :, 0:512])
            load(EV_OUT + 1, wo_ev[:, :, 512:1024])

            def expert_unit(L, e, k):
                j = k % 3
                src = (moe_w_gate, moe_w_up, moe_w_down)[j][L, bass.ds(e, 1)].rearrange(
                    "a (p c) n -> p (a c n)", c=4 if j == 2 else 8)
                sp.dma_start(place(k), src).then_inc(unit_loaded[k], 16)

            def expert(L, e, r, first=False):
                for j in range(3):
                    k = 3 * r + j
                    if first and k < 2:
                        before = max(m for m in slot if m < MOE[L] and slot[m] == k and not 0 <= m - MOE0 < 3 * E)
                        sp.wait_ge(sem("w_low"), max(q for q, (m, _) in enumerate(PIECES) if m == before) + 1)
                    elif first:
                        sp.wait_ge(sem("out_products"), (8, 24)[L])
                    else:
                        sp.wait_ge(sem("down_used") if j == 2 else sem("gate_up_used"), E * L + e - 2)
                    expert_unit(L, e, k)

            def block_rows(L, e, u, first=False):
                if not first:
                    sp.wait_ge(sem("x_turned"), E * L + e - 1)
                sp.dma_start(xin[u][0:CAP, :], xrows[bass.ds(e * CAP, CAP), :]).then_inc(sem(f"block{u}_loaded"), 16)

            def moe(L):
                if L == 1:
                    sp.wait_ge(sem("o_scaled"), 16)
                    for c0, c1, w, bias in ((0, NG, moe_w_group, moe_b_group), (NG, NR, moe_w_router, moe_b_router)):
                        sp.dma_start(wr[:, :, c0:c1], w[1].rearrange("(p c) n -> p c n", c=8),
                                     allow_slow_non_contiguous=True).then_inc(sem("router_loaded"), 16)
                        sp.dma_start(brow[:, c0:c1], bias[1:2, :].to_broadcast([P, c1 - c0])).then_inc(
                            sem("router_loaded"), 16)
                    expert_unit(L, 2, 6)
                    expert_unit(L, 2, 8)
                    sp.wait_ge(sem("x_low"), X_O + 4)
                    expert_unit(L, 2, 7)
                else:
                    sp.wait_ge(sem("b_values"), HQ)
                    sp.wait_ge(sem("x_low"), X_HEADS + 5)
                    for k in (6, 7, 8):
                        expert_unit(L, 2, k)
                for e in range(2):
                    expert(L, e, e, True)
                sp.wait_ge(sem("routed"), L + 1)
                sp.wait_ge(sem("scattered"), 16 * 2 * NT * (L + 1))
                block_rows(L, 0, 0, True)
                block_rows(L, 1, 1, True)
                with sp.Fori(0, (E - 3) // 6) as i:
                    for v in range(6):
                        block_rows(L, 6 * i + 2 + v, v % 2)
                        expert(L, 6 * i + 3 + v, v % 3)
                for e in range(3 + (E - 3) // 6 * 6, E):
                    block_rows(L, e - 1, (e - 1) % 2)
                    expert(L, e, e % 3)
                block_rows(L, E - 1, (E - 1) % 2)
                n_over = sp.value_load(ovtab[0:1, OVR:OVR + 1], min_val=0, max_val=MAXOV)
                with sp.If(n_over > 0):
                    sp.wait_ge(sem("down_used"), E * (L + 1))
                    with sp.Fori(0, n_over) as b:
                        e = sp.value_load(ovtab[0:1, bass.ds(b, 1)], min_val=0, max_val=E - 1)
                        sp.dma_start(xin[0][0:CAP, :], xrows[bass.ds(E * CAP + b * CAP, CAP), :]).then_inc(
                            sem(f"over{L}_rows"), 16)
                        for j, w in enumerate((moe_w_gate, moe_w_up, moe_w_down)):
                            src = w[L, bass.ds(e, 1)].rearrange("a (p c) n -> p (a c n)", c=4 if j == 2 else 8)
                            sp.dma_start(ring[:, j, :], src).then_inc(sem(f"over{L}_weights"), 16)
                        sp.wait_ge(sem(f"over{L}_stored"), 32 * b + 32)
                        sp.sem_inc(sem("wait_passed"), 1)

            moe(0)
            for i, c0 in enumerate(od_cols):
                load(OD + i, w_od[:, :, c0:c0 + 512])
                if i == 0:
                    for t in range(NT):
                        sp.wait_ge(sem("combined"), t + 1)
                        sp.dma_start(hsave[t * P:t * P + P, :], h[:, t, :]).then_inc(sem("h_saved"), 16)
            for kg in range(2):
                if kg == 0:
                    for half in range(2):
                        load(OD_R + half, w_od[:, :, 4640 + half * 512:5152 + half * 512])
                for half in range(2):
                    load(OD_OUT[kg] + half, wo_od[kg, :, :, half * 512:half * 512 + 512])
            moe(1)
            for t in range(NT):
                sp.wait_ge(sem("final_rows"), t + 1)
                sp.dma_start(out[0, t * P:t * P + P, :], fin_o[:, t, :]).then_inc(sem("out_stored"), 16)
            sp.wait_ge(sem("out_stored"), 16 * NT)

        @block.gpsimd
        def _(pool):
            g = nc.gpsimd
            step = Steps(pool, sem("pool_steps"))
            step(g.memset(ident[:, :], 0.0))
            g.affine_select(out=ident[:, :], in_=ident[:, :], compare_op=ALU.not_equal, fill=1.0, base=0,
                            pattern=[[-1, P]], channel_multiplier=1).then_inc(sem("constants"), 1)
            g.memset(zrow, 0.0).then_inc(sem("zero_row"), 1)
            step(g.memset(wdg[:, :, 16:32], 0.0))
            step(g.memset(qpad, 0.0))
            step(g.memset(qb[64:128], 0.0))
            step(g.memset(qb[64:66], 1.0))
            for m in (tri, upper, ones_b, gmask, ones_f):
                step(g.memset(m[:, :], 1.0))
            step(g.memset(cmask[:, :], 0.0))
            step(g.affine_select(out=tri[:, :], in_=tri[:, :], compare_op=ALU.is_ge, fill=0.0, base=0,
                                 pattern=[[1, P]], channel_multiplier=-1))
            step(g.affine_select(out=gmask[:, :], in_=gmask[:, :], compare_op=ALU.is_ge, fill=0.0, base=0,
                                 pattern=[[1, P]], channel_multiplier=-1))
            step(g.memset(gmask[0:64, 64:128], 0.0))
            step(g.affine_select(out=upper[:, :], in_=upper[:, :], compare_op=ALU.is_gt, fill=0.0, base=0,
                                 pattern=[[1, P]], channel_multiplier=-1))
            step(g.affine_select(out=cmask[:, :], in_=cmask[:, :], compare_op=ALU.is_ge, fill=-BIG, base=0,
                                 pattern=[[-1, P]], channel_multiplier=1))
            step(g.iota(dist[:, :], [[-1, 256]], base=P, channel_multiplier=1, allow_small_or_imprecise_dtypes=True))
            step(g.affine_select(out=dist[:, :], in_=dist[:, :], compare_op=ALU.is_ge, fill=BIG, base=P,
                                 pattern=[[-1, 256]], channel_multiplier=1))
            step(g.affine_select(out=dist[:, :], in_=dist[:, :], compare_op=ALU.is_ge, fill=BIG, base=-1,
                                 pattern=[[1, 256]], channel_multiplier=-1))
            step(g.iota(it32[:, :], [[1, E]], base=0, channel_multiplier=0, allow_small_or_imprecise_dtypes=True))
            step(g.iota(gid32[:, :].rearrange("p (g e) -> p g e", g=NG), [[1, NG], [0, EPG]], base=0,
                        channel_multiplier=0, allow_small_or_imprecise_dtypes=True))
            g.iota(thr[:, :], [[CAP, CR]], base=CAP, channel_multiplier=0,
                   allow_small_or_imprecise_dtypes=True).then_inc(sem("constants"), 1)
            pool.wait_ge(sem("constants"), 2)
            pool.wait_ge(sem("norm_turned"), 8)
            step(g.memset(kb[64:128], 0.0))
            g.memset(kb[64:66], 1.0).then_inc(sem("k_padded"), 1)
            pool.wait_ge(sem("k_padded"), 1)
            pool.wait_ge(sem("gate_sums"), 1)
            for hh in range(HQ):
                pool.dma_start(qb[65:66, hh, :], c8[hh:hh + 1, :]).then_inc(sem("gate_rows"), 16)
                pool.dma_start(kb[64:65, hh, :], cn8[hh:hh + 1, :]).then_inc(sem("gate_rows"), 16)

            for j in range(4 * HQ):
                n = j % 4
                pool.wait_ge(sem("b_recip"), j + 1)
                g.tensor_tensor(PB[:, j % 4, 0:(n + 1) * P], PB[:, j % 4, 0:(n + 1) * P],
                                stat[:, 2, j % 4:j % 4 + 1].to_broadcast([P, (n + 1) * P]),
                                ALU.mult).then_inc(sem("b_probs"), 1)

            pool.wait_ge(sem("b_turned"), 4 * HQ)
            pool.dma_start(h[:, :, :], x[0].rearrange("(t p) d -> p t d", p=P)).then_inc(
                sem("residual_loaded"), 16)

            def moe(L):
                pool.wait_ge(sem("slots_ready"), L + 1)
                if L == 0:
                    pool.wait_ge(sem("rows_zeroed"), 32)
                for i in range(2 * NT):
                    g.indirect_dma_start(out=xrows, out_offset=bass.IndirectOffsetOnAxis(ap=slots[:, i:i + 1], axis=0),
                                         in_=xs[:, i // 2, :], in_offset=None).then_inc(sem("scattered"), 16)
                pool.wait_ge(sem("routed"), L + 1)
                n_over = pool.value_load(ovtab[0:1, OVR:OVR + 1], min_val=0, max_val=MAXOV)
                with pool.If(n_over > 0):
                    pool.wait_ge(sem(f"over{L}_stored"), 32 * n_over)
                    pool.sem_inc(sem("wait_passed"), 1)
                for u in range(2):
                    pool.wait_ge(sem(f"y{u}_stored"), 32 * (E // 2) * (L + 1))
                for i in range(2 * NT):
                    g.indirect_dma_start(out=yg[:, i, :], out_offset=None, in_=yrows,
                                         in_offset=bass.IndirectOffsetOnAxis(ap=slots[:, i:i + 1], axis=0)).then_inc(
                        sem(f"gathered{i // 2}"), 16)

            moe(0)
            pool.wait_ge(sem("w_low"), 13)
            weight_low(pool, 13)
            weight_low(pool, 14)
            pool.wait_ge(sem("h_saved"), 16 * NT)
            pool.wait_ge(sem("norm_rows"), 8)
            step(g.memset(m128, 1.0))
            g.memset(m128.rearrange("p (c n) -> p c n", c=NT)[:, :, 0:1], 0.0).then_inc(sem("scan_mask"), 1)
            pool.wait_ge(sem("scan_mask"), 1)
            for k in range(15, 21):
                weight_low(pool, k)
            for q in range(4 * NT):
                c, qq = divmod(q, 4)
                pool.wait_ge(sem("seg_exp"), q + 1)
                if q == 0:
                    pool.wait_ge(sem("cb_kept"), 2)
                g.tensor_tensor(MT[c % 2][:, 4 * qq:4 * qq + 4, :], MT[c % 2][:, 4 * qq:4 * qq + 4, :],
                                bc_out(CBT[:, qq // 2, c, :], 4), ALU.mult).then_inc(sem("mt_ready"), 1)
                if qq == 3:
                    weight_low(pool, 21 + c)
            pool.wait_ge(sem("ydiag"), NT)
            pool.dma_start(gkw[0:16, :], odd_gk_w[0]).then_inc(sem("late_params"), 16)
            pool.wait_ge(sem("norm_turned"), 24)
            step(g.memset(m64, 1.0))
            step(g.memset(ATT, 0.0))
            g.memset(m64.rearrange("p (c n) -> p c n", c=8)[:, :, 0:1], 0.0).then_inc(sem("scan_mask"), 1)
            pool.wait_ge(sem("scan_mask"), 2)
            for k in (25, 26, 27, 28):
                weight_low(pool, k)
            pool.wait_ge(sem("scores_kept"), 4)
            pool.wait_ge(sem("k_turned_kept"), 4)
            pool.dma_start(h[:, :, :], hsave.rearrange("(t p) d -> p t d", p=P)).then_inc(
                sem("residual_loaded"), 16)
            for k in range(29, len(PIECES)):
                weight_low(pool, k)
            moe(1)
            pool.dma_start(fin_g, norm_final.rearrange("(a n) -> a n", a=1).to_broadcast([P, D])).then_inc(
                sem("late_params"), 16)

        def even_keep(name, bank, copy, done):
            if name[:2] == "qa":
                m = int(name[2])
                kv = 64 * (m // 2)
                copy(qpad[kv:kv + 64, 2 * m, :], bank[0:64, :])
                copy(qpad[kv:kv + 64, 2 * m + 1, :], bank[64:128, :]).then_inc(done, 1)
            elif name == "ka":
                copy(kaT, bank[:, :]).then_inc(done, 1)
            elif name == "va":
                copy(va, bank[:, :].rearrange("p (t n) -> p t n", t=NT)).then_inc(done, 1)
            elif name[:2] in ("qb", "kb"):
                m, dst = int(name[2]), qb if name[0] == "q" else kb
                copy(dst[0:64, 2 * m, :], bank[0:64, :])
                copy(dst[0:64, 2 * m + 1, :], bank[64:128, :]).then_inc(done, 1)
            elif name[:2] == "vb":
                q, pair = divmod(int(name[2]), 2)
                copy(vb[:, 2 * pair:2 * pair + 2, q * 256:q * 256 + 256],
                     bank[:, :].rearrange("p (t n) -> p t n", t=2)).then_inc(done, 1)
            elif name[:2] == "pt":
                n, m = int(name[2]), int(name[4])
                a = 1 if n == 0 else 0
                copy(PTA[:, 2 * m:2 * m + 2, a:2, :],
                     bank[:, :].rearrange("p (h a q) -> p h a q", h=2, a=2)[:, :, a:2, :]).then_inc(done, 1)
            elif name[:2] == "pv":
                n = int(name[2])
                copy(headsA[:, :, n * P:n * P + P], bank[:, :].rearrange("p (m q) -> p m q", m=4)).then_inc(done, 1)

        @block.scalar
        def _(act):
            s = nc.scalar
            step = Steps(act, sem("act_steps"))
            copy = lambda o, i: s.activation(o, i, ACT.Copy)
            loads = [
                (wf[:, :, :], even_w_in[0].rearrange("(p c) n -> p c n", c=8)[:, :, 2304:2312]),
                (fbias[:, :], even_forget_bias[0].rearrange("(p c) -> p c", c=1)),
                (sink8[:, :], even_sinks[0:1, :].to_broadcast([P, HQ])),
                (prow[CONVW:CONVW + 48, :], odd_conv_w[0].rearrange("j (c p) -> (j c) p", p=P)),
                (prow[CONVB:CONVB + 12, :], odd_conv_b[0].rearrange("(c p) -> c p", p=P)),
                (prow[GKB:GKB + 4, :], odd_gk_b[0].rearrange("(c p) -> c p", p=P)),
                (prow[SSDN:SSDN + 8, :], odd_ssd_norm[0].rearrange("(c p) -> c p", p=P)),
                (prow[GLAN:GLAN + 2, :], odd_gla_norm[0].rearrange("(c p) -> c p", p=P)),
                (wdg[:, :, 0:16], odd_w_in[0].rearrange("(p c) n -> p c n", c=8)[:, :, 2560:2576]),
                (wdg[:, :, 32:48], odd_w_in[0].rearrange("(p c) n -> p c n", c=8)[:, :, 4624:4640]),
                (brow[:, 0:NG], moe_b_group[0:1, :].to_broadcast([P, NG])),
                (brow[:, NG:NR], moe_b_router[0:1, :].to_broadcast([P, E])),
                (dskip[:, :], odd_d_skip[0:1, :].to_broadcast([P, 16])),
                (dtb[:, :], odd_dt_bias[0].rearrange("(p c) -> p c", c=1)),
                (acol[:, :], odd_a_log[0].rearrange("(p c) -> p c", c=1)),
                (wr[:, :, 0:NG], moe_w_group[0].rearrange("(p c) n -> p c n", c=8)),
                (wr[:, :, NG:NR], moe_w_router[0].rearrange("(p c) n -> p c n", c=8)),
            ]
            assert len(loads) == NPARAMS
            norm_act(act, 0, h, lambda t: e_xs[:, t, :], lambda t: (x_loaded[t], 16))
            weight_high(act, 0)
            for t in range(NT):
                act.wait_ge(sem("norm_kept"), 2 * t + 2)
                x_high(tile_of(t)(hnT), tile_of(t))
            weight_high(act, 1)
            for dst, src in loads:
                act.dma_start(dst, src, allow_slow_non_contiguous=True).then_inc(sem("params"), 16)


            def keep(j):
                act.wait_ge(sem("job_done"), j + 1)
                if JOBS[j] == "f":
                    act.wait_ge(sem("params"), 16 * NPARAMS)
                    s.activation(fx[0:8], B[j % 4][0:8, :], ACT.Identity,
                                 bias=fbias[:, 0:1]).then_inc(sem("job_kept_act"), 1)
                    act.wait_ge(sem("job_kept_act"), j // 2 + 1)
                    step(s.activation(fe[0:8], fx[0:8], ACT.Abs))
                    step(s.activation(fe[0:8], fe[0:8], ACT.Exp, scale=-1.0))
                    s.activation(fe[0:8], fe[0:8], ACT.Ln, bias=1.0).then_inc(sem("gate_log"), 1)
                    return
                if JOBS[j] == "pv0":
                    act.wait_ge(sem("gate_rows"), 16 * 2 * HQ)
                if JOBS[j][:2] == "vb":
                    act.wait_ge(sem("rows_zeroed"), 32)
                even_keep(JOBS[j], B[j % 4], copy, sem("job_kept_act"))

            def window_exp(n):
                k0 = P if n == 0 else 0
                act.wait_ge(sem("a_max"), n + 1)
                for hh in range(HQ):
                    s.activation(SA[:, hh, k0:256], SA[:, hh, k0:256], ACT.Exp,
                                 bias=stat[:, hh // 4, hh % 4:hh % 4 + 1], scale=0.125,
                                 accum_out=ssq[:, hh:hh + 1]).then_inc(sem("a_exp"), 1)
                s.activation(stat[:, 2:4, :], stat[:, 2:4, :], ACT.Exp).then_inc(sem("a_exp"), 1)

            for j, name in enumerate(JOBS):
                if j % 2 == 0:
                    keep(j)
                if name in PIECE_AFTER:
                    weight_high(act, PIECE_AFTER[name])
                if name in EXP_AFTER:
                    window_exp(EXP_AFTER[name])
            act.wait_ge(sem("job_done"), len(JOBS))
            act.wait_ge(sem("job_kept_act"), kept_before(len(JOBS), 0))
            act.wait_ge(sem("job_kept_dve"), kept_before(len(JOBS), 1))
            x_high(headsA, chunks_of(0, 4))
            for i in range(4 * HQ + 4):
                if i < 4 * HQ:
                    n = i % 4
                    act.wait_ge(sem("b_negmax"), i + 1)
                    if i >= 4:
                        act.wait_ge(sem("b_turned"), i - 3)
                    s.activation(PB[:, i % 4, 0:(n + 1) * P], B[2 + i % 4][:, 0:(n + 1) * P], ACT.Exp,
                                 bias=stat[:, 0, i % 4:i % 4 + 1], scale=0.125,
                                 accum_out=ssq[:, i % 4:i % 4 + 1]).then_inc(sem("b_exp"), 1)
                if i >= 4:
                    j = i - 4
                    hh, n = divmod(j, 4)
                    act.wait_ge(sem("b_turned"), j + 1)
                    if n == 0 and hh >= 2:
                        act.wait_ge(sem("b_values"), hh - 1)
                    s.activation(PTB[:, hh % 2, 0:n + 1, n * P:n * P + P],
                                 B[6 + j % 2][:, 0:(n + 1) * P].rearrange("p (c n) -> p c n", c=n + 1),
                                 ACT.Copy).then_inc(sem("b_tkept"), 1)
                    if n == 3 and hh % 2 == 0 and hh:
                        act.wait_ge(sem("b_heads"), hh // 2)
                        x_high(headsB[:, hh // 2 - 1:hh // 2, :], chunks_of(3 + hh // 2, 4 + hh // 2))
            act.wait_ge(sem("b_heads"), HQ // 2)
            x_high(headsB[:, 3:4, :], chunks_of(7, 8))
            weight_high(act, 11)
            weight_high(act, 12)

            def moe(L):
                for t in range(NT):
                    act.wait_ge(sem("mixer_added"), (0, 16)[L] + 7 + t // 2)
                    s.activation(xs[:, t, :], h[:, t, :], ACT.Square,
                                 accum_out=ssq[:, t:t + 1]).then_inc(sem("moe_squares"), 1)
                act.wait_ge(sem("moe_recip"), L + 1)
                s.activation(rstd[:, 0:NT], rstd[:, 0:NT], ACT.Sqrt).then_inc(sem("moe_rstd"), 1)
                act.wait_ge(sem("logits"), L + 1)
                s.activation(lgT[0:NR, :], B[2][0:NR, :], ACT.Copy).then_inc(sem("logits_kept"), 1)
                act.wait_ge(sem("route_args"), L + 1)
                step(s.activation(rt_gs, rt_gs, ACT.Exp))
                s.activation(rt_dv, rt_dv, ACT.Exp).then_inc(sem("route_exps"), 1)

                def silu(i, u):
                    act.wait_ge(sem("gate_up_used"), E * L + 2 * i + u + 1)
                    s.activation(sg[64:128, :], B[0][0:64, :], ACT.Silu).then_inc(sem("gated"), 1)

                def y_store(i, u):
                    act.wait_ge(sem("down_used"), E * L + 2 * i + u + 1)
                    s.activation(ysb[u], B[4 + u][:, :], ACT.Copy).then_inc(sem("y_kept"), 1)
                    act.wait_ge(sem("y_kept"), E * L + 2 * i + u + 1)
                    for a in range(2):
                        act.dma_start(yrows[bass.ds((2 * i + u) * CAP, CAP), a * 512:a * 512 + 512],
                                      ysb[u][64 * a:64 * a + 64, :]).then_inc(sem(f"y{u}_stored"), 16)

                silu(0, 0)
                silu(0, 1)
                y_store(0, 0)
                with act.Fori(1, E // 2) as i:
                    silu(i, 0)
                    y_store(i - 1, 1)
                    silu(i, 1)
                    act.wait_ge(sem("y0_stored"), 32 * ((E // 2) * L + i))
                    y_store(i, 0)
                    act.wait_ge(sem("y1_stored"), 32 * ((E // 2) * L + i))
                y_store(E // 2 - 1, 1)

                act.wait_ge(sem("routed"), L + 1)
                n_over = act.value_load(ovtab[0:1, OVR:OVR + 1], min_val=0, max_val=MAXOV)
                with act.If(n_over > 0):
                    with act.Fori(0, n_over) as b:
                        act.wait_ge(sem(f"over{L}_steps"), OVS * b + 3)
                        s.activation(sg[64:128, :], B[0][0:64, :], ACT.Silu).then_inc(sem(f"over{L}_steps"), 1)
                        act.wait_ge(sem(f"over{L}_steps"), OVS * b + 8)
                        act.wait_ge(sem("y0_stored"), 32 * (E // 2) * (L + 1))
                        s.activation(ysb[0], B[4][:, :], ACT.Copy).then_inc(sem(f"over{L}_steps"), 1)
                        act.wait_ge(sem(f"over{L}_steps"), OVS * b + 9)
                        for a in range(2):
                            act.dma_start(yrows[bass.ds(E * CAP + b * CAP, CAP), a * 512:a * 512 + 512],
                                          ysb[0][64 * a:64 * a + 64, :]).then_inc(sem(f"over{L}_stored"), 16)

            moe(0)

            act.wait_ge(sem("combined"), 1)
            weight_high(act, 13)
            norm_act(act, 1, h, lambda t: xs[:, t, :], lambda t: (sem("combined"), t + 1))
            weight_high(act, 14)
            for t in range(NT):
                act.wait_ge(sem("norm_kept"), 8 + 2 * t + 2)
                x_high(tile_of(t)(hnT), tile_of(t))
            act.wait_ge(sem("pcol_turned"), 1)
            s.activation(pcol[:, 0:74], B[7][:, 0:74], ACT.Copy).then_inc(sem("pcol_kept"), 1)
            act.wait_ge(sem("pcol_kept"), 1)
            act.wait_ge(sem("dt_products"), 1)
            act.wait_ge(sem("h_saved"), 16 * NT)
            step(s.activation(dtx[0:16], B[4][0:16, :], ACT.Identity, bias=dtb[:, 0:1]))
            step(s.activation(dt2[0:16], dtx[0:16], ACT.Abs))
            step(s.activation(dt2[0:16], dt2[0:16], ACT.Exp, scale=-1.0))
            step(s.activation(dt2[0:16], dt2[0:16], ACT.Ln, bias=1.0))
            s.activation(acol[:, :], acol[:, :], ACT.Exp).then_inc(sem("dt_log"), 1)
            s.activation(glrT[0:16], B[4][32:48, :], ACT.Copy).then_inc(sem("rank_kept"), 1)

            def spread(c):
                act.dma_start(MT[c % 2], sums_d[:, c * P:c * P + P].unsqueeze(0).to_broadcast([P, 16, P])).then_inc(
                    sem("spread"), 16)

            for j in range(CH):
                if j == 1:
                    act.wait_ge(sem("decays"), 1)
                    act.dma_start(sums_d, acsT[0:16]).then_inc(sem("sums_saved"), 16)
                if j == 4:
                    act.wait_ge(sem("sums_saved"), 16)
                    spread(0)
                    spread(1)
                ch = CONV[j]
                act.wait_ge(sem("conv_products"), j + 1)
                s.activation(acc[j % 2], B[j % 2][:, :], ACT.Identity, bias=pcol[:, CONVB + ch:CONVB + ch + 1],
                             scale=pcol[:, CONVW + 36 + ch:CONVW + 37 + ch]).then_inc(sem("conv_first"), 1)
                act.wait_ge(sem("conv_summed"), j + 1)
                if j < 2:
                    dst = BT[:, j, :]
                elif j < 4:
                    dst = CT[:, j - 2, :]
                else:
                    dst = cso[j % 2]
                    if j >= 6:
                        act.wait_ge(sem("conv_turned"), j - 3)
                s.activation(dst, acc[j % 2], ACT.Silu).then_inc(sem("conv_out"), 1)
                if j % 2 == 1:
                    weight_high(act, 15 + j // 2)
            for c in range(NT):
                for qq in range(4):
                    q = 4 * c + qq
                    act.wait_ge(sem("seg_args"), q + 1)
                    part = MT[c % 2][:, 4 * qq:4 * qq + 4, :]
                    s.activation(part, part, ACT.Exp).then_inc(sem("seg_exp"), 1)
                act.wait_ge(sem("chunk_args"), c + 1)
                step(s.activation(endb[:, 2, :], endb[:, 2, :], ACT.Exp))
                step(s.activation(endb[:, 0, :], endb[:, 0, :], ACT.Exp))
                s.activation(endb[:, 1, :], datok[:, c, 1, :], ACT.Exp).then_inc(sem("chunk_exps"), 1)
                for half in range(2):
                    i = 2 * c + half
                    act.wait_ge(sem("z_products"), i + 1)
                    s.activation(zg[:, 2 * half:2 * half + 2, c * 256:c * 256 + 256],
                                 B[4 + half][:, :].rearrange("p (t n) -> p t n", t=2),
                                 ACT.Silu).then_inc(sem("z_gate"), 1)
                weight_high(act, 21 + c)
                if 1 <= c < NT - 1:
                    act.wait_ge(sem("ydiag"), c)
                    spread(c + 1)
            act.wait_ge(sem("ydiag"), NT)
            act.wait_ge(sem("z_used"), 4)
            norm_act(act, 2, Y, lambda t: at(16, NT, D)[:, t, :])
            def gate_logs(d):
                act.wait_ge(sem("gate_products"), d + 1)
                if d >= 2:
                    act.wait_ge(sem("gate_keys"), d - 1)
                a, b = g1[d % 2], g2[d % 2]
                step(s.activation(a, B[4 + d % 2][:, :], ACT.Identity, bias=pcol[:, GKB + d:GKB + d + 1]))
                step(s.activation(b, a, ACT.Abs))
                step(s.activation(b, b, ACT.Exp, scale=-1.0))
                s.activation(b, b, ACT.Ln, bias=1.0).then_inc(sem("gla_log"), 1)

            weight_high(act, 25)
            gate_logs(0)
            for d in range(4):
                if d < 3:
                    gate_logs(d + 1)
                act.wait_ge(sem("gla_sums"), d + 1)
                s.activation(g2[d % 2], g3[d % 2], ACT.Exp, scale=1.0 / 16)
                s.activation(gen[d % 2], g3[d % 2], ACT.Exp, scale=-1.0 / 16)
                s.activation(gke[d % 2], g1[d % 2], ACT.Exp, scale=1.0 / 16).then_inc(sem("gla_exps"), 1)
                if d == 0:
                    weight_high(act, 26)
                elif d >= 2:
                    weight_high(act, 25 + d)
            for q in range(4):
                act.wait_ge(sem("v_products"), 2 * q + 1)
                copy(V[:, 0:2, q * 256:q * 256 + 256],
                     B[4 + 2 * q % 4][:, :].rearrange("p (t n) -> p t n", t=2)).then_inc(sem("v_kept_act"), 1)
                weight_high(act, 29 + q)

            def r_gate(i):
                q, pair = divmod(i, 2)
                act.wait_ge(sem("r_products"), i + 1)
                s.activation(zg[:, 2 * pair:2 * pair + 2, q * 256:q * 256 + 256],
                             B[6 + i % 2][:, :].rearrange("p (t n) -> p t n", t=2),
                             ACT.Silu).then_inc(sem("r_gate"), 1)
                if i % 2 == 1 and i < 7:
                    weight_high(act, 33 + i // 2)

            for t in range(NT):
                if t:
                    r_gate(2 * t - 2)
                    r_gate(2 * t - 1)
                act.wait_ge(sem("o_products"), t + 1)
                act.wait_ge(sem("gla_states"), min(2 * t + 2, 7))
                for d in range(4):
                    src = B[2 * (t % 2) + d // 2][:, (d % 2) * 256:(d % 2) * 256 + 256]
                    if t or d:
                        act.wait_ge(sem("o_squares"), 4 * t + d)
                    s.activation(rt[0][:, 0:256], src, ACT.Square,
                                 accum_out=ssq[:, 4 * t + d:4 * t + d + 1]).then_inc(sem("o_squares"), 1)
                for a in range(2):
                    copy(O[:, t, a * 512:a * 512 + 512], B[2 * (t % 2) + a][:, :]).then_inc(sem("o_kept"), 1)
            r_gate(6)
            r_gate(7)
            for t in range(NT):
                x_high(tile_of(t)(yT), tile_of(t))
                if t == 1:
                    act.wait_ge(sem("o_recip"), 1)
                    s.activation(rstd[:, :], rstd[:, :], ACT.Sqrt).then_inc(sem("o_rstd"), 1)
            for k in range(36, 41):
                weight_high(act, k)
            for t in range(NT):
                act.wait_ge(sem("out_products"), 16)
                act.wait_ge(sem("o_tkept"), 2 * t + 2)
                x_high(tile_of(t)(oT), tile_of(t))
            for k in range(41, 43):
                weight_high(act, k)

            moe(1)
            norm_act(act, 3, h, lambda t: fin_o[:, t, :], lambda t: (sem("combined"), NT + t + 1))

        @block.vector
        def _(dve):
            v = nc.vector
            step = Steps(dve, sem("dve_steps"))
            copy = v.tensor_copy

            norm_dve(dve, step, 0, h, e_xs, hnT, gmix[:, 0, :], first=True)

            def keep(j):
                dve.wait_ge(sem("job_done"), j + 1)
                if JOBS[j][:2] == "vb":
                    dve.wait_ge(sem("rows_zeroed"), 32)
                if JOBS[j] == "pv0":
                    dve.wait_ge(sem("gate_rows"), 16 * 2 * HQ)
                even_keep(JOBS[j], B[j % 4], copy, sem("job_kept_dve"))

            weight_low(dve, 0)
            for t in range(NT):
                x_low(dve, X_EVEN + t + 1, tile_of(t)(hnT), tile_of(t))
            weight_low(dve, 1)

            def gate_sums():
                dve.wait_ge(sem("gate_log"), 1)
                step(v.scalar_tensor_tensor(out=fx[0:8], in0=fx[0:8], scalar=0.0, in1=fe[0:8],
                                            op0=ALU.min, op1=ALU.subtract))
                step(v.tensor_tensor_scan(cT[0:8], ones_f[0:8, 0:1].to_broadcast([8, 512]), fx[0:8], 0.0,
                                          ALU.mult, ALU.add))
                step(v.tensor_scalar(c8[0:8], cT[0:8], 8.0, None, ALU.mult))
                v.tensor_scalar(cn8[0:8], cT[0:8], -8.0, None, ALU.mult).then_inc(sem("gate_sums"), 1)

            m8 = stat[:, 2:4, :].rearrange("p a b -> p (a b)")
            neg = stat[:, 0:2, :].rearrange("p a b -> p (a b)")
            den = stat[:, 4:6, :].rearrange("p a b -> p (a b)")

            def window_max(n):
                k0 = P if n == 0 else 0
                if n == 0:
                    dve.wait_ge(sem("params"), 16 * NPARAMS)
                    dve.wait_ge(sem("constants"), 2)
                    step(v.tensor_scalar(sink8[:, :], sink8[:, :], 8.0, None, ALU.mult))
                if n:
                    dve.wait_ge(sem("job_done"), JI[f"pt{n - 1}_3"] + 1)
                for g in range(2):
                    dve.wait_ge(sem("a_scores"), 2 * n + g + 1)
                    for hh in range(4 * g, 4 * g + 4):
                        v.scalar_tensor_tensor(out=SA[:, hh, k0:256], in0=dist[:, k0:256],
                                               scalar=-8.0 * 2.0 ** -(hh + 1),
                                               in1=B[4 + hh // 2][:, (hh % 2) * 256 + k0:(hh % 2) * 256 + 256],
                                               op0=ALU.mult, op1=ALU.add).then_inc(sem("a_biased"), 1)
                dve.wait_ge(sem("a_biased"), HQ * (n + 1))
                step(v.tensor_reduce(m8, SA[:, :, k0:256], AX.X, ALU.max))
                step(v.tensor_tensor(m8, m8, sink8[:, :], ALU.max))
                step(v.tensor_scalar(neg, m8, -0.125, None, ALU.mult))
                v.scalar_tensor_tensor(out=m8, in0=sink8[:, :], scalar=0.125, in1=neg, op0=ALU.mult,
                                       op1=ALU.add).then_inc(sem("a_max"), 1)

            def window_probs(n):
                k0 = P if n == 0 else 0
                dve.wait_ge(sem("a_exp"), (HQ + 1) * (n + 1))
                step(v.tensor_tensor(den, ssq[:, 0:HQ], m8, ALU.add))
                step(v.reciprocal(den, den))
                v.tensor_tensor(SA[:, :, k0:256], SA[:, :, k0:256], bc_in(den, 256 - k0),
                                ALU.mult).then_inc(sem("a_probs"), 1)

            for j, name in enumerate(JOBS):
                if j % 2 == 1:
                    keep(j)
                if name in PIECE_AFTER:
                    weight_low(dve, PIECE_AFTER[name])
                if name == "f":
                    gate_sums()
                if name in MAX_AFTER:
                    window_max(MAX_AFTER[name])
                if name in PROBS_AFTER:
                    window_probs(PROBS_AFTER[name])
            dve.wait_ge(sem("a_probs"), 4)
            x_low(dve, X_HEADS + 1, headsA, chunks_of(0, 4))
            for i in range(4 * HQ + 2):
                if i < 4 * HQ:
                    n, bank = i % 4, B[2 + i % 4]
                    dve.wait_ge(sem("b_scores"), i + 1)
                    step(v.tensor_tensor(bank[:, n * P:n * P + P], bank[:, n * P:n * P + P], cmask[:, :], ALU.add))
                    step(v.tensor_reduce(stat[:, 1, i % 4:i % 4 + 1], bank[:, 0:(n + 1) * P], AX.X, ALU.max))
                    v.tensor_scalar(stat[:, 0, i % 4:i % 4 + 1], stat[:, 1, i % 4:i % 4 + 1], -0.125, None,
                                    ALU.mult).then_inc(sem("b_negmax"), 1)
                if 1 <= i <= 4 * HQ:
                    j = i - 1
                    n = j % 4
                    dve.wait_ge(sem("b_exp"), j + 1)
                    v.reciprocal(stat[:, 2, j % 4:j % 4 + 1], ssq[:, j % 4:j % 4 + 1]).then_inc(sem("b_recip"), 1)
                if i >= 15 and (i - 15) % 8 == 0 or i == 4 * HQ + 1:
                    pair = (i - 15) // 8 if i <= 4 * HQ else HQ // 2 - 1
                    dve.wait_ge(sem("b_values"), 2 * pair + 2)
                    copy(headsB[:, pair, :], B[pair % 2][:, :]).then_inc(sem("b_heads"), 1)
                    if pair:
                        x_low(dve, X_HEADS + 1 + pair, headsB[:, pair - 1:pair, :], chunks_of(3 + pair, 4 + pair))
            x_low(dve, X_HEADS + 5, headsB[:, 3:4, :], chunks_of(7, 8))

            def add_out(count, j, bank):
                q, pair = divmod(j, 2)
                dve.wait_ge(sem("out_products"), count)
                dst = h[:, 2 * pair:2 * pair + 2, q * 256:q * 256 + 256]
                v.tensor_tensor(dst, dst, bank[:, :].rearrange("p (t n) -> p t n", t=2),
                                ALU.add).then_inc(sem("mixer_added"), 1)

            def keep_tile(L, t):
                for g in range(2):
                    dve.wait_ge(sem("moe_turned"), 8 * L + 2 * t + g + 1)
                    v.tensor_tensor(mhT[:, 4 * g:4 * g + 4, t * P:t * P + P],
                                    B[g][:, :].rearrange("p (c n) -> p c n", c=4),
                                    bc_in(gmoe[:, L, 4 * g:4 * g + 4], P), ALU.mult).then_inc(sem("moe_kept"), 1)

            dve.wait_ge(sem("residual_loaded"), 16)
            for j in range(8):
                add_out(j + 1, j, B[2 + j % 4])
                if j in (1, 3):
                    weight_low(dve, 11 + j // 2)

            def moe(L):
                for t in range(NT):
                    keep_tile(L, t)
                dve.wait_ge(sem("moe_squares"), NT * (L + 1))
                step(v.tensor_scalar(ssq[:, 0:NT], ssq[:, 0:NT], 1.0 / D, EPS, ALU.mult, ALU.add))
                v.reciprocal(rstd[:, 0:NT], ssq[:, 0:NT]).then_inc(sem("moe_recip"), 1)
                dve.wait_ge(sem("moe_rstd"), L + 1)
                dve.wait_ge(sem("mixer_added"), (8, 24)[L])
                for t in range(NT):
                    ins = v.tensor_scalar(xs[:, t, :], h[:, t, :], rstd[:, t:t + 1], None, ALU.mult)
                step(ins)
                if L == 1:
                    dve.wait_ge(sem("router_loaded"), 64)
                dve.wait_ge(sem("logits_turned"), L + 1)
                v.memset(gp, -BIG)
                for t in range(NT):
                    ins = v.scalar_tensor_tensor(out=lg[:, t, :], in0=B[3][:, t * NR:t * NR + NR],
                                                 scalar=rstd[:, t:t + 1], in1=brow, op0=ALU.mult, op1=ALU.add)
                step(ins)
                step(copy(gp[:, :, 0:NG], lg[:, :, 0:NG]))
                for t in range(NT):
                    ins = v.max(gm8[:, t, :], gp[:, t, :])
                step(ins)
                for t in range(NT):
                    ins = v.max_index(gi8[:, t, :], gm8[:, t, :], gp[:, t, :])
                step(ins)
                step(copy(gf, gi8[:, :, 0]))
                step(v.tensor_tensor(geq, bc_out(gid32[:, :], NT), bc_in(gf, E), ALU.is_equal))
                step(v.tensor_scalar(geq, geq, BIG, -BIG, ALU.mult, ALU.add))
                step(v.tensor_tensor(em, lg[:, :, NG:NR], geq, ALU.add))
                for t in range(NT):
                    ins = v.max(em8[:, t, :], em[:, t, :])
                step(ins)
                for t in range(NT):
                    ins = v.max_index(ei8[:, t, :], em8[:, t, :], em[:, t, :])
                step(ins)
                step(copy(ef, ei8[:, :, 0:2].rearrange("p t k -> p k t")))
                for k in range(2):
                    ins = v.tensor_tensor(onehot[:, k], bc_out(it32[:, :], NT), bc_in(ef[:, k, :], E), ALU.is_equal)
                step(ins)
                v.tensor_tensor(cntb, onehot[:, 0], onehot[:, 1], ALU.add).then_inc(sem("picks"), 1)
                v.tensor_tensor(rt_gs, lg[:, :, 0:NG], bc_in(gm8[:, :, 0], NG), ALU.subtract)
                v.tensor_tensor(rt_dv, em8[:, :, 1], em8[:, :, 0], ALU.subtract).then_inc(sem("route_args"), 1)
                dve.wait_ge(sem("ranks"), L + 1)
                step(v.tensor_tensor(cmp, bc_in(B[2][:, NT * E:NT * E + E], CR - 1), bc_out(thr[:, 0:CR - 1], E),
                                     ALU.is_gt))
                step(v.tensor_reduce(nover, cmp, AX.X, ALU.add))
                step(v.tensor_tensor_scan(oend, ones_f[:, 0:1].to_broadcast([P, E]), nover, 0.0, ALU.mult, ALU.add))
                for k in range(2):
                    v.tensor_tensor(picked[:, k * NT:k * NT + NT, :], onehot[:, k],
                                    B[2][:, 0:NT * E].rearrange("p (t e) -> p t e", t=NT), ALU.mult)
                step(v.tensor_tensor(oexcl, oend, nover, ALU.subtract))
                both = onehot.rearrange("p k t e -> p (k t) e")
                flat = lambda a: a.rearrange("p k t -> p (k t)")
                v.tensor_reduce(flat(rk), picked, AX.X, ALU.add)
                step(v.tensor_tensor(picked2, both, bc_out(oexcl, 2 * NT), ALU.mult))
                step(v.tensor_reduce(flat(ok), picked2, AX.X, ALU.add))
                v.scalar_tensor_tensor(out=ef, in0=ef, scalar=float(CAP), in1=rk, op0=ALU.mult, op1=ALU.add)
                step(v.scalar_tensor_tensor(out=ok, in0=ok, scalar=float(CAP), in1=rk, op0=ALU.mult, op1=ALU.add))
                step(v.scalar_tensor_tensor(out=ok, in0=ok, scalar=float(E * CAP - CAP), in1=ef,
                                            op0=ALU.add, op1=ALU.subtract))
                step(v.scalar_tensor_tensor(out=ok, in0=rk, scalar=float(CAP), in1=ok, op0=ALU.is_ge, op1=ALU.mult))
                step(v.tensor_tensor(rsl, ok, ef, ALU.add))
                copy(slots[:, :].rearrange("p (t k) -> p k t", k=2), rsl).then_inc(sem("slots_ready"), 1)
                step(v.tensor_tensor(cmp2[0:1], bc_out(oend[0:1, :], OVR), bc_in(it32[0:1, 0:OVR], E), ALU.is_le))
                step(v.tensor_reduce(ovf[0:1, :], cmp2[0:1], AX.X, ALU.add))
                copy(ovtab[:, 0:OVR], ovf[0:1, :])
                step(copy(ovtab[:, OVR:OVR + 1], oend[0:1, E - 1:E]))
                dve.wait_ge(sem("route_exps"), L + 1)
                v.tensor_scalar(rden, rt_dv, 1.0, None, ALU.add)
                step(v.tensor_reduce(gw, rt_gs, AX.X, ALU.add))
                v.reciprocal(gw, gw)
                step(v.reciprocal(rden, rden))
                step(v.tensor_tensor(gates[:, :, 0], gw, rden, ALU.mult))
                v.tensor_tensor(gates[:, :, 1], gates[:, :, 0], rt_dv, ALU.mult).then_inc(sem("routed"), 1)

                def x_kept(i, u):
                    dve.wait_ge(sem("x_turned"), E * L + 2 * i + u + 1)
                    v.tensor_tensor(xT[u], B[2][:, :].rearrange("p (c n) -> p c n", c=8),
                                    bc_in(gmoe[:, L, :], CAP), ALU.mult).then_inc(sem("x_kept"), 1)

                def hidden(i, u):
                    dve.wait_ge(sem("gated"), E * L + 2 * i + u + 1)
                    v.tensor_tensor(hb[64:128, :], sg[64:128, :], B[1][64:128, :],
                                    ALU.mult).then_inc(sem("hidden"), 1)

                def h_kept(i, u):
                    dve.wait_ge(sem("h_turned"), E * L + 2 * i + u + 1)
                    copy(hT[u], B[3][:, 0:4 * CAP].rearrange("p (c n) -> p c n", c=4)).then_inc(sem("h_kept"), 1)

                x_kept(0, 0)
                hidden(0, 0)
                x_kept(0, 1)
                h_kept(0, 0)
                hidden(0, 1)
                with dve.Fori(1, E // 2) as i:
                    x_kept(i, 0)
                    h_kept(i - 1, 1)
                    hidden(i, 0)
                    x_kept(i, 1)
                    h_kept(i, 0)
                    hidden(i, 1)
                h_kept(E // 2 - 1, 1)

                n_over = dve.value_load(ovtab[0:1, OVR:OVR + 1], min_val=0, max_val=MAXOV)
                with dve.If(n_over > 0):
                    with dve.Fori(0, n_over) as b:
                        dve.wait_ge(sem(f"over{L}_steps"), OVS * b + 1)
                        v.tensor_tensor(xT[0], B[2][:, :].rearrange("p (c n) -> p c n", c=8),
                                        bc_in(gmoe[:, L, :], CAP), ALU.mult).then_inc(sem(f"over{L}_steps"), 1)
                        dve.wait_ge(sem(f"over{L}_steps"), OVS * b + 4)
                        v.tensor_tensor(hb[64:128, :], sg[64:128, :], B[1][64:128, :],
                                        ALU.mult).then_inc(sem(f"over{L}_steps"), 1)
                        dve.wait_ge(sem(f"over{L}_steps"), OVS * b + 6)
                        copy(hT[0], B[3][:, 0:4 * CAP].rearrange("p (c n) -> p c n", c=4)).then_inc(
                            sem(f"over{L}_steps"), 1)

                for t in range(NT):
                    dve.wait_ge(sem(f"gathered{t}"), 32 * (L + 1))
                    step(v.scalar_tensor_tensor(out=h[:, t, :], in0=yg[:, 2 * t, :], scalar=gates[:, t, 0:1],
                                                in1=h[:, t, :], op0=ALU.mult, op1=ALU.add))
                    v.scalar_tensor_tensor(out=h[:, t, :], in0=yg[:, 2 * t + 1, :], scalar=gates[:, t, 1:2],
                                           in1=h[:, t, :], op0=ALU.mult, op1=ALU.add).then_inc(sem("combined"), 1)
                dve.wait_ge(sem("combined"), NT * (L + 1))

            moe(0)

            norm_dve(dve, step, 1, h, xs, hnT, gmix[:, 1, :])
            for t in range(NT):
                x_low(dve, X_ODD + t + 1, tile_of(t)(hnT), tile_of(t))
            dve.wait_ge(sem("pcol_kept"), 1)
            for j in range(4):
                step(copy(gla8[:, 2 * j:2 * j + 2], pcol[:, GLAN:GLAN + 2]))
            dve.wait_ge(sem("dt_log"), 1)
            dve.wait_ge(sem("scan_mask"), 1)
            step(v.tensor_scalar(acol[:, :], acol[:, :], -1.0, None, ALU.mult))
            step(v.scalar_tensor_tensor(out=dtx[0:16], in0=dtx[0:16], scalar=0.0, in1=dt2[0:16],
                                        op0=ALU.max, op1=ALU.add))
            step(v.tensor_scalar(dt2[0:16], dtx[0:16], acol[:, 0:1], None, ALU.mult))
            v.tensor_tensor_scan(acsT[0:16], m128[0:16], dt2[0:16], 0.0, ALU.mult, ALU.add).then_inc(sem("decays"), 1)
            for j in range(CH + 2):
                if j < CH:
                    ch, bank, a = CONV[j], B[j % 2], acc[j % 2]
                    dve.wait_ge(sem("conv_first"), j + 1)
                    for back in (1, 2, 3):
                        row = CONVW + 12 * (3 - back) + ch
                        ins = v.scalar_tensor_tensor(out=a[:, back:512], in0=bank[:, 0:512 - back],
                                                     scalar=pcol[:, row:row + 1], in1=a[:, back:512],
                                                     op0=ALU.mult, op1=ALU.add)
                        if back < 3:
                            step(ins)
                        else:
                            ins.then_inc(sem("conv_summed"), 1)
                if j >= 2:
                    i = TURNED.index(j - 2) if j - 2 in TURNED else None
                    if i is not None:
                        dve.wait_ge(sem("conv_turned"), i + 1)
                        src = B[2 + i % 2][:, :].rearrange("p (t n) -> p t n", t=NT)
                        dst = Btok[:, :, i, :] if i < 2 else XS[:, :, (i - 2) * P:(i - 2) * P + P]
                        copy(dst, src).then_inc(sem("conv_tkept"), 1)
            dve.wait_ge(sem("decays_turned"), 1)
            step(copy(datok[:, :, :, :], B[5][:, 0:NT * 32].rearrange("p (t w h) -> p t w h", t=NT, w=2)))
            for g in range(2):
                dve.wait_ge(sem("cb_products"), g + 1)
                v.tensor_tensor(CBT[:, g, :, :], B[6 + g][:, :].rearrange("p (c n) -> p c n", c=NT),
                                bc_out(tri[:, :], NT), ALU.mult).then_inc(sem("cb_kept"), 1)
            dve.wait_ge(sem("cb_kept"), 2)
            dve.wait_ge(sem("conv_tkept"), 10)

            def seg_args(c):
                if c:
                    dve.wait_ge(sem("chunk_exps"), c)
                    dve.wait_ge(sem("states_kept"), c)
                    dve.wait_ge(sem("y_summed"), 2 * c)
                dve.wait_ge(sem("spread"), 16 * max(c + 1, 2))
                step(copy(endb[:, 0, :], MT[c % 2][:, :, P - 1]))
                for hh in range(16):
                    ins = v.tensor_scalar(MT[c % 2][:, hh, :], MT[c % 2][:, hh, :],
                                          datok[:, c, 1, hh:hh + 1], 0.0, ALU.subtract, ALU.min)
                    if hh % 4 == 3:
                        ins.then_inc(sem("seg_args"), 1)
                v.tensor_tensor(endb[:, 2, :], endb[:, 0, :], datok[:, c, 1, :],
                                ALU.subtract).then_inc(sem("chunk_args"), 1)

            def heads_of(row):
                return row.rearrange("p (h n) -> p h n", n=64)

            for c in range(NT):
                seg_args(c)
                xc = heads_of(XS[:, c, :])
                step(v.tensor_tensor(heads_of(Y[:, c, :]), xc, bc_in(dskip[:, :], 64), ALU.mult))
                step(v.tensor_tensor(xc, xc, bc_in(datok[:, c, 0, :], 64), ALU.mult))
                dve.wait_ge(sem("chunk_exps"), c + 1)
                v.tensor_tensor(heads_of(xdec), xc, bc_in(endb[:, 2, :], 64), ALU.mult).then_inc(sem("x_decayed"), 1)
                if c < NT - 1:
                    dve.wait_ge(sem("state_products"), c + 1)
                    for g in range(2):
                        pg = prev[:, g * 512:g * 512 + 512]
                        if c == 0:
                            ins = copy(pg, B[2 + g][:, :])
                        else:
                            step(v.tensor_tensor(heads_of(pg), heads_of(pg), bc_in(endb[:, 0, 8 * g:8 * g + 8], 64),
                                                 ALU.mult))
                            ins = v.tensor_tensor(pg, pg, B[2 + g][:, :], ALU.add)
                    ins.then_inc(sem("states_kept"), 1)
                dve.wait_ge(sem("ydiag"), c + 1)
                for g in range(2):
                    yc = Y[:, c, g * 512:g * 512 + 512]
                    if c:
                        step(v.tensor_tensor(heads_of(tmp), heads_of(B[g][:, :]),
                                             bc_in(endb[:, 1, 8 * g:8 * g + 8], 64), ALU.mult))
                        step(v.tensor_tensor(yc, yc, tmp, ALU.add))
                    v.tensor_tensor(yc, yc, B[6 + g][:, :], ALU.add).then_inc(sem("y_summed"), 1)
            dve.wait_ge(sem("y_summed"), 2 * NT)
            dve.wait_ge(sem("z_gate"), 8)
            for t in range(NT):
                v.tensor_tensor(Y[:, t, :], Y[:, t, :], zg[:, t, :], ALU.mult).then_inc(sem("z_used"), 1)
            dve.wait_ge(sem("z_used"), 4)
            norm_dve(dve, step, 2, Y, Y, yT, pcol[:, SSDN:SSDN + 8])

            dve.wait_ge(sem("scan_mask"), 2)
            def gate_sums_of(d):
                a, c = g1[d % 2], g3[d % 2]
                dve.wait_ge(sem("gla_log"), d + 1)
                step(v.scalar_tensor_tensor(out=a, in0=a, scalar=0.0, in1=g2[d % 2], op0=ALU.min, op1=ALU.subtract))
                step(v.tensor_tensor_scan(c, m64, a, 0.0, ALU.mult, ALU.add))
                ends = c.rearrange("p (c n) -> p c n", n=64)[:, :, 63]
                v.tensor_tensor(a.rearrange("p (c n) -> p c n", n=64), bc_in(ends, 64),
                                c.rearrange("p (c n) -> p c n", n=64), ALU.subtract).then_inc(sem("gla_sums"), 1)

            gate_sums_of(0)
            for d in range(4):
                if d < 3:
                    gate_sums_of(d + 1)
                eg = g2[d % 2]
                dve.wait_ge(sem("gla_exps"), d + 1)
                copy(odec[:, d, :], eg.rearrange("p (c n) -> p c n", n=64)[:, :, 63])
                dve.wait_ge(sem("qk_products"), (4, 4, 7, 8)[d])
                step(v.scalar_tensor_tensor(out=QD[:, d, :], in0=B[6 if d % 2 == 0 else 2][:, :], scalar=P ** -0.5,
                                            in1=eg, op0=ALU.mult, op1=ALU.mult))
                if d:
                    dve.wait_ge(sem("head_scores"), d)
                step(v.tensor_tensor(gki, gen[d % 2], B[7 if d % 2 == 0 else 3][:, :], ALU.mult))
                v.tensor_tensor(gkd, gke[d % 2], B[7 if d % 2 == 0 else 3][:, :], ALU.mult).then_inc(sem("gate_keys"), 1)
                dve.wait_ge(sem("head_scores"), d + 1)
                v.copy_predicated(ATT[:, d, :].rearrange("p (t n) -> p t n", t=NT),
                                  bc_out(gmask[:, :].bitcast(U32), NT),
                                  B[0][:, :].rearrange("p (t n) -> p t n", t=NT)).then_inc(sem("scores_kept"), 1)
                copy(KTOK[:, :, d * P:d * P + P],
                     B[1][:, :].rearrange("p (t n) -> p t n", t=NT)).then_inc(sem("k_turned_kept"), 1)
            for q in range(4):
                dve.wait_ge(sem("v_products"), 2 * q + 2)
                copy(V[:, 2:4, q * 256:q * 256 + 256],
                     B[5 + 2 * q % 4][:, :].rearrange("p (t n) -> p t n", t=2)).then_inc(sem("v_kept_dve"), 1)
            for c in range(7):
                dve.wait_ge(sem("gla_states"), c + 1)
                for d in range(4):
                    src = B[4 + d // 2][:, (d % 2) * 256:(d % 2) * 256 + 256]
                    if c == 0:
                        ins = copy(ST[:, d, :], src)
                    else:
                        ins = v.scalar_tensor_tensor(out=ST[:, d, :], in0=ST[:, d, :], scalar=odec[:, d, c:c + 1],
                                                     in1=src, op0=ALU.mult, op1=ALU.add)
                ins.then_inc(sem("gla_states_kept"), 1)
                dve.wait_ge(sem("gla_states_kept"), c + 1)
            for t in range(2):
                x_low(dve, X_Y + t + 1, tile_of(t)(yT), tile_of(t))
            dve.wait_ge(sem("o_squares"), 16)
            step(v.tensor_scalar(ssq[:, :], ssq[:, :], 1.0 / 256, EPS, ALU.mult, ALU.add))
            v.reciprocal(rstd[:, :], ssq[:, :]).then_inc(sem("o_recip"), 1)
            dve.wait_ge(sem("o_rstd"), 1)
            dve.wait_ge(sem("o_kept"), 8)
            for t in range(2, NT):
                x_low(dve, X_Y + t + 1, tile_of(t)(yT), tile_of(t))
            dve.wait_ge(sem("r_gate"), 8)
            dve.wait_ge(sem("residual_loaded"), 32)
            for t in range(NT):
                for d in range(4):
                    oc = O[:, t, d * 256:d * 256 + 256]
                    v.scalar_tensor_tensor(out=oc, in0=oc, scalar=rstd[:, 4 * t + d:4 * t + d + 1],
                                           in1=zg[:, t, d * 256:d * 256 + 256],
                                           op0=ALU.mult, op1=ALU.mult).then_inc(sem("o_scaled"), 1)
            for j in range(4):
                add_out(8 + j + 1, j, B[4 + j])
            for i in range(2 * NT):
                t, g = i // 2, i % 2
                dve.wait_ge(sem("o_turned"), i + 1)
                v.tensor_tensor(oT[:, 4 * g:4 * g + 4, t * P:t * P + P],
                                B[i % 2][:, :].rearrange("p (c n) -> p c n", c=4),
                                bc_in(gla8[:, 4 * g:4 * g + 4], P), ALU.mult).then_inc(sem("o_tkept"), 1)
            for j in range(4, 8):
                add_out(8 + j + 1, j, B[4 + j % 4])
            for t in range(NT):
                x_low(dve, X_O + t + 1, tile_of(t)(oT), tile_of(t))
            dve.wait_ge(sem("mixer_added"), 16)
            for j in range(8):
                add_out(16 + j + 1, j, B[4 + j % 4])

            moe(1)
            dve.wait_ge(sem("norm_squares"), 4 * NT)
            step(v.tensor_scalar(ssq[:, 0:NT], ssq[:, 0:NT], 1.0 / D, EPS, ALU.mult, ALU.add))
            v.reciprocal(rstd[:, 0:NT], ssq[:, 0:NT]).then_inc(sem("norm_recip"), 1)
            dve.wait_ge(sem("norm_rstd"), 4)
            dve.wait_ge(sem("late_params"), 32)
            for t in range(NT):
                v.scalar_tensor_tensor(out=fin_o[:, t, :], in0=h[:, t, :], scalar=rstd[:, t:t + 1], in1=fin_g,
                                       op0=ALU.mult, op1=ALU.mult).then_inc(sem("final_rows"), 1)

        @block.tensor
        def _(pe):
            mm, turn = nc.tensor.matmul, nc.tensor.transpose
            pe.wait_ge(sem("constants"), 1)
            norm_pe(pe, 0, e_xs, True)
            pe.wait_ge(sem("constants"), 2)

            def job_bank(j):
                if j >= 4:
                    pe.wait_ge(sem("job_kept_act") if j % 2 == 0 else sem("job_kept_dve"), (j - 4) // 2 + 1)
                return B[j % 4]

            def window_scores(n):
                k0 = P if n == 0 else 0
                if n == 0:
                    pe.wait_ge(sem("job_kept_act"), JI["ka"] // 2 + 1)
                    pe.wait_ge(sem("job_kept_dve"), 2)
                for g in range(2):
                    if n:
                        pe.wait_ge(sem("a_biased"), HQ * (n - 1) + 4 * g + 4)
                    for hh in range(4 * g, 4 * g + 4):
                        last = mm(B[4 + hh // 2][:, (hh % 2) * 256 + k0:(hh % 2) * 256 + 256],
                                  qpad[:, hh, n * P:n * P + P], kaT[:, (n - 1) * P + k0:(n + 1) * P],
                                  start=True, stop=True)
                    last.then_inc(sem("a_scores"), 1)

            for j, name in enumerate(JOBS):
                bank = job_bank(j)
                if name == "qa0":
                    pe.wait_ge(sem("x_low"), X_EVEN + 4)
                if name[:2] == "qa":
                    k = piece[EV_IN, 256 * (int(name[2]) // 2)]
                    pe.wait_ge(sem("w_low"), k + 1)
                    last = project_T(bank[:, :], k, int(name[2]) % 2 * P)
                elif name == "ka":
                    pe.wait_ge(sem("w_low"), piece[EV_IN + 1, 0] + 1)
                    last = project_T(bank[:, :], piece[EV_IN + 1, 0], 0)
                elif name == "va":
                    for t in range(NT):
                        for c in range(KC):
                            last = mm(bank[:, t * P:t * P + P], hnT[:, c, t * P:t * P + P],
                                      unit(EV_IN + 1)[:, c, P:2 * P], start=c == 0, stop=c == KC - 1)
                elif name == "f":
                    pe.wait_ge(sem("params"), 16 * NPARAMS)
                    for c in range(KC):
                        last = mm(bank[0:8, :], wf[:, c, :], hnT[:, c, :], start=c == 0, stop=c == KC - 1)
                elif name[:2] in ("qb", "kb"):
                    k = piece[EV_IN + (2 if name[0] == "q" else 3), 256 * (int(name[2]) // 2)]
                    pe.wait_ge(sem("w_low"), k + 1)
                    last = project_T(bank[:, :], k, int(name[2]) % 2 * P)
                elif name[:2] == "vb":
                    q, pair = divmod(int(name[2]), 2)
                    k = piece[EV_IN + 4, 256 * q]
                    pe.wait_ge(sem("w_low"), k + 1)
                    last = project(bank, k, pair)
                elif name[:2] == "pt":
                    n, m = int(name[2]), int(name[4])
                    if m == 0:
                        pe.wait_ge(sem("a_probs"), n + 1)
                    for b in range(2):
                        for a in range(1 if n == 0 else 0, 2):
                            last = turn(bank[:, b * 256 + a * P:b * 256 + a * P + P],
                                        SA[:, 2 * m + b, a * P:a * P + P], ident[:, :])
                elif name[:2] == "pv":
                    n = int(name[2])
                    pe.wait_ge(sem("job_kept_act"), kept_before(j, 0))
                    pe.wait_ge(sem("job_kept_dve"), kept_before(j, 1))
                    for hh in range(HQ):
                        lo = 64 * (hh % 2)
                        o = bank[lo:lo + 64, (hh // 2) * P:(hh // 2) * P + P]
                        kv = 64 * (hh // 4)
                        if n:
                            mm(o, va[:, n - 1, kv:kv + 64], PTA[:, hh, 0, :], start=True, stop=False)
                        last = mm(o, va[:, n, kv:kv + 64], PTA[:, hh, 1, :], start=n == 0, stop=True)
                last.then_inc(sem("job_done"), 1)
                if name in SCORES_AFTER:
                    window_scores(SCORES_AFTER[name])

            pe.wait_ge(sem("gate_rows"), 16 * 2 * HQ)
            pe.wait_ge(sem("k_padded"), 1)
            pe.wait_ge(sem("job_kept_act"), kept_before(len(JOBS), 0))
            pe.wait_ge(sem("job_kept_dve"), kept_before(len(JOBS), 1))
            pe.wait_ge(sem("a_biased"), 4 * HQ)

            def values(hh):
                pe.wait_ge(sem("b_tkept"), 4 * hh + 4)
                pair, lo = hh // 2, 64 * (hh % 2)
                if pair >= 2:
                    pe.wait_ge(sem("b_heads"), pair - 1)
                for j in range(NT):
                    last = mm(B[pair % 2][lo:lo + 64, j * P:512], vb[:, j, hh * 64:hh * 64 + 64],
                              PTB[:, hh % 2, j, j * P:512], start=j == 0, stop=j == NT - 1)
                last.then_inc(sem("b_values"), 1)

            for i in range(4 * HQ + 4):
                if i < 4 * HQ:
                    hh, n = divmod(i, 4)
                    if i >= 4:
                        pe.wait_ge(sem("b_exp"), i - 3)
                    mm(B[2 + i % 4][:, 0:(n + 1) * P], qb[:, hh, n * P:n * P + P], kb[:, hh, 0:(n + 1) * P],
                       start=True, stop=True).then_inc(sem("b_scores"), 1)
                if i >= 4:
                    j = i - 4
                    n = j % 4
                    pe.wait_ge(sem("b_probs"), j + 1)
                    if j >= 2:
                        pe.wait_ge(sem("b_tkept"), j - 1)
                    for a in range(n + 1):
                        last = turn(B[6 + j % 2][:, a * P:a * P + P], PB[:, j % 4, a * P:a * P + P], ident[:, :])
                    last.then_inc(sem("b_turned"), 1)
                    if n == 2 and j >= 4:
                        values(j // 4 - 1)
            values(HQ - 1)

            def turn_tile(L, t):
                pe.wait_ge(sem("mixer_added"), (0, 16)[L] + 7 + t // 2)
                for g in range(2):
                    if t:
                        pe.wait_ge(sem("moe_kept"), 8 * L + 2 * t + g - 1)
                    for j in range(4):
                        src = h[:, t, :].rearrange("p (q c) -> p c q", c=KC)[:, 4 * g + j, :]
                        last = turn(B[g][:, j * P:j * P + P], src, ident[:, :])
                    last.then_inc(sem("moe_turned"), 1)

            pe.wait_ge(sem("x_low"), X_HEADS + 5)
            for j in range(8):
                q, pair = divmod(j, 2)
                k = piece[EV_OUT + q // 2, 256 * (q % 2)]
                pe.wait_ge(sem("w_low"), k + 1)
                if j >= 4:
                    pe.wait_ge(sem("mixer_added"), j - 3)
                project(B[2 + j % 4], k, pair).then_inc(sem("out_products"), 1)

            def turn_rows(u):
                pe.sem_inc(sem("wait_passed"), 1)
                for c in range(KC):
                    last = turn(B[2][:, c * CAP:c * CAP + CAP],
                                xin[u][0:CAP, :].rearrange("p (q c) -> p c q", c=KC)[:, c, :], ident[0:CAP, 0:CAP])
                return last

            def turn_hidden():
                pe.sem_inc(sem("wait_passed"), 1)
                for c in range(4):
                    last = turn(B[3][:, c * CAP:c * CAP + CAP],
                                hb[64:128, :].rearrange("p (q c) -> p c q", c=4)[:, c, :], ident[64:128, 64:128])
                return last

            def gate_up_products(u, k):
                gate, up = (place(k + j).rearrange("p (c n) -> p c n", c=8) for j in range(2))
                for c in range(KC):
                    mm(B[0][0:64, :], xT[u][:, c, :], gate[:, c, :], start=c == 0, stop=c == KC - 1)
                    last = mm(B[1][64:128, :], xT[u][:, c, :], up[:, c, :], start=c == 0, stop=c == KC - 1)
                return last

            def down_products(u, k, bank):
                w = place(k).rearrange("p (c n) -> p c n", c=4)
                for c in range(4):
                    for a in range(2):
                        last = mm(bank[64 * a:64 * a + 64, :], hT[u][:, c, :], w[:, c, a * 512:a * 512 + 512],
                                  start=c == 0, stop=c == 3)
                return last

            def moe(L):
                if L == 1:
                    pe.wait_ge(sem("router_loaded"), 64)
                for t in range(NT + 1):
                    if t < NT:
                        turn_tile(L, t)
                    if t:
                        pe.wait_ge(sem("moe_kept"), 8 * L + 2 * t)
                        q = slice((t - 1) * P, t * P)
                        for c in range(KC):
                            last = mm(B[2][0:NR, q], wr[:, c, :], mhT[:, c, q], start=c == 0, stop=c == KC - 1)
                last.then_inc(sem("logits"), 1)
                pe.wait_ge(sem("logits_kept"), L + 1)
                for t in range(NT):
                    last = turn(B[3][:, t * NR:t * NR + NR], lgT[0:NR, t * P:t * P + P], ident[0:NR, 0:NR])
                last.then_inc(sem("logits_turned"), 1)
                pe.wait_ge(sem("picks"), L + 1)
                for t in range(NT):
                    for j in range(t):
                        mm(B[2][:, t * E:t * E + E], ones_b[:, :], cntb[:, j, :], start=j == 0, stop=False)
                    mm(B[2][:, t * E:t * E + E], upper[:, :], cntb[:, t, :], start=t == 0, stop=True)
                for j in range(NT):
                    last = mm(B[2][:, NT * E:NT * E + E], ones_b[:, :], cntb[:, j, :], start=j == 0, stop=j == NT - 1)
                last.then_inc(sem("ranks"), 1)

                def unit_ready(k, turn):
                    pe.wait_ge(unit_loaded[k], 16 * (turn_of[MOE[L] + k] + turn))

                def rows(e, u, half_e):
                    pe.wait_ge(sem(f"block{u}_loaded"), 16 * ((E // 2) * L + half_e + 1))
                    pe.wait_ge(sem("x_kept"), E * L + e)
                    turn_rows(u).then_inc(sem("x_turned"), 1)

                def gate_up(e, u, r, turn):
                    pe.wait_ge(sem("x_kept"), E * L + e + 1)
                    unit_ready(3 * r, turn)
                    unit_ready(3 * r + 1, turn)
                    gate_up_products(u, 3 * r).then_inc(sem("gate_up_used"), 1)

                def down(e, u, r, turn):
                    pe.wait_ge(sem("h_kept"), E * L + e + 1)
                    unit_ready(3 * r + 2, turn)
                    down_products(u, 3 * r + 2, B[4 + u]).then_inc(sem("down_used"), 1)

                def hidden_rows(e):
                    pe.wait_ge(sem("hidden"), E * L + e + 1)
                    turn_hidden().then_inc(sem("h_turned"), 1)

                rows(0, 0, 0)
                gate_up(0, 0, 0, 0)
                rows(1, 1, 0)
                hidden_rows(0)
                gate_up(1, 1, 1, 0)
                down(0, 0, 0, 0)
                with pe.Fori(0, (E - 2) // 6) as i:
                    for d in range(2, 8):
                        e = 6 * i + d
                        rows(e, d % 2, 3 * i + d // 2)
                        hidden_rows(e - 1)
                        gate_up(e, d % 2, d % 3, 2 * i + d // 3)
                        pe.wait_ge(sem("y_kept"), E * L + e - 1)
                        down(e - 1, (d - 1) % 2, (d - 1) % 3, 2 * i + (d - 1) // 3)
                hidden_rows(E - 1)
                pe.wait_ge(sem("y_kept"), E * L + E - 2)
                down(E - 1, (E - 1) % 2, (E - 1) % 3, (E - 1) // 3)

                pe.wait_ge(sem("routed"), L + 1)
                n_over = pe.value_load(ovtab[0:1, OVR:OVR + 1], min_val=0, max_val=MAXOV)
                with pe.If(n_over > 0):
                    pe.wait_ge(sem("y_kept"), E * (L + 1))
                    with pe.Fori(0, n_over) as b:
                        pe.wait_ge(sem(f"over{L}_rows"), 16 * b + 16)
                        turn_rows(0).then_inc(sem(f"over{L}_steps"), 1)
                        pe.wait_ge(sem(f"over{L}_steps"), OVS * b + 2)
                        pe.wait_ge(sem(f"over{L}_weights"), 48 * b + 48)
                        gate_up_products(0, 0).then_inc(sem(f"over{L}_steps"), 1)
                        pe.wait_ge(sem(f"over{L}_steps"), OVS * b + 5)
                        turn_hidden().then_inc(sem(f"over{L}_steps"), 1)
                        pe.wait_ge(sem(f"over{L}_steps"), OVS * b + 7)
                        down_products(0, 2, B[4]).then_inc(sem(f"over{L}_steps"), 1)

            moe(0)

            norm_pe(pe, 1, xs, True)
            turn(B[7][:, 0:74], prow[0:74, :], ident[0:74, 0:74]).then_inc(sem("pcol_turned"), 1)
            for c in range(KC):
                last = mm(B[4][0:48, :], wdg[:, c, :], hnT[:, c, :], start=c == 0, stop=c == KC - 1)
            last.then_inc(sem("dt_products"), 1)
            for j in range(CH + 1):
                if j < CH:
                    if j == 0:
                        pe.wait_ge(sem("x_low"), X_ODD + 4)
                    k = piece[OD_BC + j // 4, 256 * (j // 2 % 2)]
                    pe.wait_ge(sem("w_low"), k + 1)
                    if j >= 2:
                        pe.wait_ge(sem("conv_summed"), j - 1)
                    project_T(B[j % 2][:, :], k, j % 2 * P).then_inc(sem("conv_products"), 1)
                if j >= 1 and j - 1 in TURNED:
                    i = TURNED.index(j - 1)
                    pe.wait_ge(sem("conv_out"), j)
                    if i >= 2:
                        pe.wait_ge(sem("conv_tkept"), i - 1)
                    src = BT[:, i, :] if i < 2 else cso[(j - 1) % 2]
                    for t in range(NT):
                        last = turn(B[2 + i % 2][:, t * P:t * P + P], src[:, t * P:t * P + P], ident[:, :])
                    last.then_inc(sem("conv_turned"), 1)
            pe.wait_ge(sem("decays"), 1)
            for t in range(NT):
                turn(B[5][:, t * 32:t * 32 + 16], dtx[0:16, t * P:t * P + P], ident[0:16, 0:16])
                last = turn(B[5][:, t * 32 + 16:t * 32 + 32], acsT[0:16, t * P:t * P + P], ident[0:16, 0:16])
            last.then_inc(sem("decays_turned"), 1)
            for g in range(2):
                for c in range(NT):
                    last = mm(B[6 + g][:, c * P:c * P + P], BT[:, g, c * P:c * P + P], CT[:, g, c * P:c * P + P],
                              start=True, stop=True)
                last.then_inc(sem("cb_products"), 1)
            pe.wait_ge(sem("cb_kept"), 2)

            pe.wait_ge(sem("rank_kept"), 1)
            for c in range(NT):
                for half in range(2):
                    if half == 0:
                        k = piece[OD_Z + c // 2, 256 * (c % 2)]
                        pe.wait_ge(sem("w_low"), k + 1)
                    if c:
                        pe.wait_ge(sem("z_gate"), 2 * c + half - 1)
                    project(B[4 + half], k, half).then_inc(sem("z_products"), 1)
                pe.wait_ge(sem("x_decayed"), c + 1)
                if c:
                    pe.wait_ge(sem("states_kept"), c)
                    pe.wait_ge(sem("y_summed"), 2 * c)
                    for g in range(2):
                        mm(B[g][:, :], CT[:, g, c * P:c * P + P], prev[:, g * 512:g * 512 + 512], start=True, stop=True)
                if c < NT - 1:
                    for g in range(2):
                        last = mm(B[2 + g][:, :], Btok[:, c, g, :], xdec[:, g * 512:g * 512 + 512],
                                  start=True, stop=True)
                    last.then_inc(sem("state_products"), 1)
                pe.wait_ge(sem("mt_ready"), 4 * c + 4)
                for hh in range(16):
                    last = mm(B[6 + hh // 8][:, (hh % 8) * 64:(hh % 8) * 64 + 64], MT[c % 2][:, hh, :],
                              XS[:, c, hh * 64:hh * 64 + 64], start=True, stop=True)
                last.then_inc(sem("ydiag"), 1)

            def qk_product(d, a):
                k = piece[(OD_Q, OD_K)[a], 256 * (d // 2)]
                pe.wait_ge(sem("w_low"), k + 1)
                project_T(B[(6, 2)[d % 2] + a][:, :], k, d % 2 * P).then_inc(sem("qk_products"), 1)

            def gate_product(d):
                mm(B[4 + d % 2][:, :], gkw[0:16, d * P:d * P + P], glrT[0:16, :],
                   start=True, stop=True).then_inc(sem("gate_products"), 1)

            pe.wait_ge(sem("states_kept"), NT - 1)
            qk_product(1, 0)
            pe.wait_ge(sem("y_summed"), 2 * NT)
            qk_product(0, 0)
            pe.wait_ge(sem("z_gate"), 8)
            pe.wait_ge(sem("late_params"), 16)
            gate_product(0)
            gate_product(1)
            qk_product(1, 1)
            norm_pe(pe, 2, Y, False)
            qk_product(0, 1)

            for d in range(1, 5):
                if d == 4:
                    pe.wait_ge(sem("gla_log"), 4)
                    pe.wait_ge(sem("w_low"), piece[OD_V, 0] + 1)
                    project(B[4], piece[OD_V, 0], 0).then_inc(sem("v_products"), 1)
                if d == 2 or d == 3:
                    pe.wait_ge(sem("gla_log"), d - 1)
                    gate_product(d)
                    pe.wait_ge(sem("gate_keys"), d - 1)
                    qk_product(d, 0)
                    if d == 3:
                        qk_product(2, 1)
                        qk_product(3, 1)
                if d:
                    e = d - 1
                    pe.wait_ge(sem("gate_keys"), e + 1)
                    pe.wait_ge(sem("scores_kept"), e)
                    pe.wait_ge(sem("k_turned_kept"), e)
                    for t in range(NT):
                        mm(B[0][:, t * P:t * P + P], gki[:, t * P:t * P + P], QD[:, e, t * P:t * P + P],
                           start=True, stop=True)
                    for t in range(NT):
                        last = turn(B[1][:, t * P:t * P + P], gkd[:, t * P:t * P + P], ident[:, :])
                    last.then_inc(sem("head_scores"), 1)
            pe.wait_ge(sem("gla_log"), 4)
            for i in range(1, 8):
                q, pair = divmod(i, 2)
                k = piece[OD_V + q // 2, 256 * (q % 2)]
                pe.wait_ge(sem("w_low"), k + 1)
                if i >= 4:
                    pe.wait_ge(sem("v_kept_act") if i % 2 == 0 else sem("v_kept_dve"), (i - 4) // 2 + 1)
                project(B[4 + i % 4], k, pair).then_inc(sem("v_products"), 1)
            pe.wait_ge(sem("scores_kept"), 4)
            pe.wait_ge(sem("k_turned_kept"), 4)
            pe.wait_ge(sem("v_kept_act"), 4)
            pe.wait_ge(sem("v_kept_dve"), 4)
            for t in range(NT):
                if t >= 2:
                    pe.wait_ge(sem("o_kept"), 2 * (t - 1))

                def o_bank(d):
                    return B[2 * (t % 2) + d // 2]

                for d in range(4):
                    mm(o_bank(d)[:, (d % 2) * 256:(d % 2) * 256 + 256], ATT[:, d, t * P:t * P + P],
                       V[:, t, d * 256:d * 256 + 256], start=d % 2 == 0, stop=True, skip_group_check=True)
                for j in range(2):
                    c, lo = 2 * t + j, 64 * j
                    if c:
                        pe.wait_ge(sem("gla_states_kept"), c)
                        for d in range(4):
                            last = mm(o_bank(d)[lo:lo + 64, (d % 2) * 256:(d % 2) * 256 + 256],
                                      QD[:, d, c * 64:c * 64 + 64], ST[:, d, :], start=False, stop=True,
                                      skip_group_check=True)
                        if j:
                            last.then_inc(sem("o_products"), 1)
                    if c < 7:
                        for d in range(4):
                            last = mm(B[4 + d // 2][:, (d % 2) * 256:(d % 2) * 256 + 256],
                                      KTOK[lo:lo + 64, t, d * P:d * P + P], V[lo:lo + 64, t, d * 256:d * 256 + 256],
                                      start=True, stop=True)
                        last.then_inc(sem("gla_states"), 1)
                    q, pair = divmod(c, 2)
                    k = piece[OD_R + q // 2, 256 * (q % 2)]
                    pe.wait_ge(sem("w_low"), k + 1)
                    if c >= 2:
                        pe.wait_ge(sem("r_gate"), c - 1)
                    project(B[6 + c % 2], k, pair).then_inc(sem("r_products"), 1)
            pe.wait_ge(sem("gla_states_kept"), 7)

            def out_product(j):
                kg, (q, pair) = j // 8, divmod(j % 8, 2)
                k = piece[OD_OUT[kg] + q // 2, 256 * (q % 2)]
                pe.wait_ge(sem("w_low"), k + 1)
                if q == 0:
                    pe.wait_ge(sem("x_low"), (X_Y, X_O)[kg] + 2 * pair + 2)
                if j >= 4:
                    pe.wait_ge(sem("mixer_added"), 8 + j - 3)
                project(B[4 + j % 4], k, pair).then_inc(sem("out_products"), 1)

            pe.wait_ge(sem("r_gate"), 8)
            for j in range(4):
                out_product(j)
            pe.wait_ge(sem("o_scaled"), 16)
            for i in range(2 * NT):
                t, g = i // 2, i % 2
                if i >= 2:
                    pe.wait_ge(sem("o_tkept"), i - 1)
                for j in range(4):
                    c = 4 * g + j
                    last = turn(B[i % 2][:, j * P:j * P + P], O[:, t, c * P:c * P + P], ident[:, :])
                last.then_inc(sem("o_turned"), 1)
            pe.wait_ge(sem("o_tkept"), 8)
            for j in range(4, 16):
                out_product(j)
            moe(1)


_INS = ['x', 'norm_mix', 'norm_moe', 'norm_final', 'even_w_in', 'even_sinks', 'even_forget_bias', 'even_w_out',
        'odd_w_in', 'odd_conv_w', 'odd_conv_b', 'odd_dt_bias', 'odd_a_log', 'odd_d_skip', 'odd_ssd_norm',
        'odd_gk_w', 'odd_gk_b', 'odd_gla_norm', 'odd_w_out', 'moe_w_group', 'moe_b_group', 'moe_w_router',
        'moe_b_router', 'moe_w_gate', 'moe_w_up', 'moe_w_down']


def kernel(**inputs):
    import numpy as _np
    import concourse.bacc as _bacc
    from concourse import mybir as _mybir
    from concourse.bass_utils import run_bass_kernel_spmd as _run

    nc = _bacc.Bacc("TRN2", target_bir_lowering=False, num_devices=1)
    arrays, args = {}, []
    for name in _INS:
        a = _np.ascontiguousarray(inputs[name])
        arrays[f"in_{name}"] = a
        args.append(nc.dram_tensor(f"in_{name}", a.shape, _mybir.dt.from_np(a.dtype), kind="ExternalInput").ap())
    x = arrays["in_x"]
    out = nc.dram_tensor("out", x.shape, _mybir.dt.from_np(x.dtype), kind="ExternalOutput").ap()
    build(nc, *args, out)
    r = _run(nc, [arrays], core_ids=[0])
    return r.results[0]["out"]
```
